# Optimizing a Trainium2 kernel written in Bass

```python
import jax, jax.numpy as jnp
from jax import lax
import numpy as np

D_MODEL = 1024
BATCH = 1
SEQ = 256
DEPTH = 1

GLA_HEADS = 4
GLA_QK_WIDTH = D_MODEL // 2
GLA_V_WIDTH = D_MODEL
GLA_DK = GLA_QK_WIDTH // GLA_HEADS
GLA_DV = GLA_V_WIDTH // GLA_HEADS
GLA_GATE_RANK = 16
GLA_TAU = 16.0
GLA_CHUNK = 64
GLA_NORM_EPS = 1e-5
RWKV_HEAD_DIM = 64
RWKV_WIDTH = D_MODEL
RWKV_HEADS = RWKV_WIDTH // RWKV_HEAD_DIM
RWKV_DECAY_LORA = 64
RWKV_ICLR_LORA = 64
RWKV_GATE_LORA = 128
RWKV_GN_EPS = 64e-5
N_EXPERTS = 32
TOP_K = 4
EXPERT_FF = D_MODEL
SWIGLU_ALPHA = 1.702
SWIGLU_LIMIT = 7.0
MOE_BLOCK = 256
RMS_EPS = 1e-6

GLA_COLS = 2 * GLA_QK_WIDTH + GLA_V_WIDTH + GLA_GATE_RANK + GLA_V_WIDTH
RWKV_COLS = 3 * RWKV_WIDTH + RWKV_DECAY_LORA + RWKV_ICLR_LORA + RWKV_GATE_LORA
GATE_COLS = 2 * D_MODEL
IN_WIDTH = GLA_COLS + RWKV_COLS + GATE_COLS

kernel_name = 'hybrid_gla_rwkv7_moe_block'

def _split(z, sizes):
    out, start = [], 0
    for s in sizes:
        out.append(z[..., start:start + s])
        start += s
    return out

def rms_norm(x, gain, eps=RMS_EPS):
    xf = x.astype(jnp.float32)
    y = xf * lax.rsqrt(jnp.mean(xf * xf, axis=-1, keepdims=True) + eps)
    return y.astype(x.dtype) * gain

def gla_chunked(q, k, v, log_a):
    f32 = jnp.float32
    Bn, S, H, DK = q.shape
    DV = v.shape[-1]
    C = GLA_CHUNK
    N = S // C
    q = q.astype(f32).reshape(Bn, N, C, H, DK) * (DK ** -0.5)
    k = k.astype(f32).reshape(Bn, N, C, H, DK)
    v = v.astype(f32).reshape(Bn, N, C, H, DV)
    b = jnp.cumsum(log_a.astype(f32).reshape(Bn, N, C, H, DK), axis=2)
    b_ref = b[:, :, C // 2:C // 2 + 1]
    b_end = b[:, :, C - 1:]
    causal = jnp.tril(jnp.ones((C, C), dtype=bool))
    scores = jnp.einsum('bnihd,bnjhd->bnhij', q * jnp.exp(b - b_ref), k * jnp.exp(b_ref - b))
    scores = jnp.where(causal, scores, 0.0)
    o_intra = jnp.einsum('bnhij,bnjhv->bnihv', scores, v)
    q_in = q * jnp.exp(b)
    k_st = k * jnp.exp(b_end - b)
    decay = jnp.exp(b_end[:, :, 0])

    def step(state, inp):
        q_n, k_n, v_n, d_n = inp
        o_n = jnp.einsum('bihd,bhdv->bihv', q_n, state)
        state = state * d_n[..., None] + jnp.einsum('bjhd,bjhv->bhdv', k_n, v_n)
        return state, o_n

    state0 = jnp.zeros((Bn, H, DK, DV), f32)
    xs = (jnp.moveaxis(q_in, 1, 0), jnp.moveaxis(k_st, 1, 0), jnp.moveaxis(v, 1, 0), jnp.moveaxis(decay, 1, 0))
    _, o_inter = lax.scan(step, state0, xs)
    o = o_intra + jnp.moveaxis(o_inter, 0, 1)
    return o.reshape(Bn, S, H, DV)

def gla_branch(z_gla, gate_up, gate_bias, norm_g):
    Bn, S, _ = z_gla.shape
    q, k, v, gate_lr, o_gate = _split(z_gla, (GLA_QK_WIDTH, GLA_QK_WIDTH, GLA_V_WIDTH, GLA_GATE_RANK, GLA_V_WIDTH))
    log_a = jax.nn.log_sigmoid((gate_lr @ gate_up + gate_bias).astype(jnp.float32)) / GLA_TAU
    o = gla_chunked(q.reshape(Bn, S, GLA_HEADS, GLA_DK), k.reshape(Bn, S, GLA_HEADS, GLA_DK),
                    v.reshape(Bn, S, GLA_HEADS, GLA_DV), log_a.reshape(Bn, S, GLA_HEADS, GLA_DK))
    o = o * lax.rsqrt(jnp.mean(o * o, axis=-1, keepdims=True) + GLA_NORM_EPS) * norm_g
    o = o.reshape(Bn, S, GLA_V_WIDTH) * jax.nn.silu(o_gate.astype(jnp.float32))
    return o.astype(z_gla.dtype)

def rwkv7_scan(r, w, k, v, a_vec, b_vec):
    f32 = jnp.float32
    Bn, S, H, N = r.shape

    def step(state, inp):
        r_t, w_t, k_t, v_t, a_t, b_t = inp
        sa = jnp.einsum('bhij,bhj->bhi', state, a_t)
        state = state * w_t[:, :, None, :] + sa[..., None] * b_t[:, :, None, :] + v_t[..., None] * k_t[:, :, None, :]
        y_t = jnp.einsum('bhij,bhj->bhi', state, r_t)
        return state, y_t

    state0 = jnp.zeros((Bn, H, N, N), f32)
    xs = tuple(jnp.moveaxis(t.astype(f32), 1, 0) for t in (r, w, k, v, a_vec, b_vec))
    _, ys = lax.scan(step, state0, xs)
    return jnp.moveaxis(ys, 0, 1)

def rwkv7_branch(z_rwkv, mu, w0, w2, a0, a2, g2, k_k, k_a, r_k, ln_w, ln_b):
    f32 = jnp.float32
    Bn, S, _ = z_rwkv.shape
    prev = jnp.pad(z_rwkv, ((0, 0), (1, 0), (0, 0)))[:, :-1]
    u = z_rwkv + mu * (prev - z_rwkv)
    r, k, v, xw, xa, xg = _split(u, (RWKV_WIDTH, RWKV_WIDTH, RWKV_WIDTH, RWKV_DECAY_LORA, RWKV_ICLR_LORA, RWKV_GATE_LORA))
    w_log = -jax.nn.softplus(-(w0 + jnp.tanh(xw) @ w2).astype(f32)) - 0.5
    decay = jnp.exp(-jnp.exp(w_log))
    a = jax.nn.sigmoid((a0 + xa @ a2).astype(f32))
    g = jax.nn.sigmoid(xg) @ g2
    hs = (Bn, S, RWKV_HEADS, RWKV_HEAD_DIM)
    kf = k.astype(f32)
    kk = (kf * k_k).reshape(hs)
    kk = kk / jnp.maximum(jnp.sqrt(jnp.sum(kk * kk, axis=-1, keepdims=True)), 1e-12)
    kmod = (kf * (1.0 + (a - 1.0) * k_a)).reshape(hs)
    rf = r.astype(f32).reshape(hs)
    vf = v.astype(f32).reshape(hs)
    y = rwkv7_scan(rf, decay.reshape(hs), kmod, vf, -kk, kk * a.reshape(hs))
    mean = jnp.mean(y, axis=-1, keepdims=True)
    var = jnp.mean(jnp.square(y - mean), axis=-1, keepdims=True)
    y = ((y - mean) * lax.rsqrt(var + RWKV_GN_EPS)).reshape(Bn, S, RWKV_WIDTH) * ln_w + ln_b
    y = y + (jnp.sum(rf * kmod * r_k, axis=-1, keepdims=True) * vf).reshape(Bn, S, RWKV_WIDTH)
    return (y * g).astype(z_rwkv.dtype)

def hybrid_mixer(h, w_in, gla_gate_up, gla_gate_bias, gla_norm_g, rwkv_mu, rwkv_w0, rwkv_w2, rwkv_a0, rwkv_a2,
                 rwkv_g2, rwkv_k_k, rwkv_k_a, rwkv_r_k, rwkv_ln_w, rwkv_ln_b, w_branch_a, w_branch_b, w_out):
    z = h @ w_in
    z_gla, z_rwkv, z_gate = _split(z, (GLA_COLS, RWKV_COLS, GATE_COLS))
    y_a = gla_branch(z_gla, gla_gate_up, gla_gate_bias, gla_norm_g)
    y_b = rwkv7_branch(z_rwkv, rwkv_mu, rwkv_w0, rwkv_w2, rwkv_a0, rwkv_a2, rwkv_g2, rwkv_k_k, rwkv_k_a,
                       rwkv_r_k, rwkv_ln_w, rwkv_ln_b)
    gates = jax.nn.sigmoid(z_gate.astype(jnp.float32)).astype(h.dtype)
    g_a, g_b = _split(gates, (D_MODEL, D_MODEL))
    merged = g_a * (y_a @ w_branch_a) + g_b * (y_b @ w_branch_b)
    return merged @ w_out

def clamped_swiglu(hid):
    hid = hid.reshape(hid.shape[:-1] + (EXPERT_FF, 2))
    glu = jnp.minimum(hid[..., 0], SWIGLU_LIMIT)
    lin = jnp.clip(hid[..., 1], -SWIGLU_LIMIT, SWIGLU_LIMIT)
    return glu * jax.nn.sigmoid(SWIGLU_ALPHA * glu) * (lin + 1.0)

def moe_ffn(h, router_w, router_b, w1, b1, w2, b2):
    Bn, S, D = h.shape
    T = Bn * S
    t = h.reshape(T, D)
    logits = (t @ router_w + router_b).astype(jnp.float32)
    top_vals, top_idx = lax.top_k(logits, TOP_K)
    gates = jax.nn.softmax(top_vals, axis=-1)
    TK = T * TOP_K
    e_flat = top_idx.reshape(TK)
    tok_flat = jnp.arange(TK, dtype=jnp.int32) // TOP_K
    gate_flat = gates.reshape(TK).astype(t.dtype)
    order = jnp.argsort(e_flat, stable=True)
    e_sorted = e_flat[order]
    tok_sorted = tok_flat[order]
    gate_sorted = gate_flat[order]
    counts = jnp.bincount(e_flat, length=N_EXPERTS)
    starts = jnp.cumsum(counts) - counts
    padded = (counts + MOE_BLOCK - 1) // MOE_BLOCK * MOE_BLOCK
    pad_ends = jnp.cumsum(padded)
    pad_starts = pad_ends - padded
    dest = pad_starts[e_sorted] + (jnp.arange(TK) - starts[e_sorted])
    NB = -(-TK // MOE_BLOCK) + N_EXPERTS
    rows_tok = jnp.zeros((NB * MOE_BLOCK,), jnp.int32).at[dest].set(tok_sorted)
    rows_gate = jnp.zeros((NB * MOE_BLOCK,), t.dtype).at[dest].set(gate_sorted)
    block_expert = jnp.minimum(jnp.searchsorted(pad_ends, jnp.arange(NB) * MOE_BLOCK, side='right'), N_EXPERTS - 1)

    def block_fn(args):
        tok_b, gate_b, e = args
        hid = t[tok_b] @ w1[e] + b1[e]
        out = clamped_swiglu(hid) @ w2[e] + b2[e]
        return out * gate_b[:, None]

    outs = lax.map(block_fn, (rows_tok.reshape(NB, MOE_BLOCK), rows_gate.reshape(NB, MOE_BLOCK), block_expert))
    y = jax.ops.segment_sum(outs.reshape(NB * MOE_BLOCK, D), rows_tok, num_segments=T)
    return y.reshape(Bn, S, D).astype(h.dtype)

def setup_inputs(seed: int = 0) -> dict:
    key = jax.random.key(seed)
    ks = jax.random.split(key, 32)
    f32 = jnp.float32
    L = DEPTH

    def nrm(k, shape, scale):
        return jax.random.normal(k, shape, f32) * scale

    ramp = (jnp.arange(RWKV_WIDTH, dtype=f32) / (RWKV_WIDTH - 1)) ** 0.85
    return {
        'x': nrm(ks[0], (BATCH, SEQ, D_MODEL), 1.0),
        'norm_mix_g': 1.0 + nrm(ks[1], (L, D_MODEL), 0.02),
        'w_in': nrm(ks[2], (L, D_MODEL, IN_WIDTH), D_MODEL ** -0.5),
        'gla_gate_up': nrm(ks[3], (L, GLA_GATE_RANK, GLA_QK_WIDTH), GLA_GATE_RANK ** -0.5),
        'gla_gate_bias': nrm(ks[4], (L, GLA_QK_WIDTH), 0.5),
        'gla_norm_g': 1.0 + nrm(ks[5], (L, GLA_DV), 0.02),
        'rwkv_mu': jax.random.uniform(ks[6], (L, RWKV_COLS), f32),
        'rwkv_w0': -6.5 + 5.0 * ramp + nrm(ks[7], (L, RWKV_WIDTH), 0.1),
        'rwkv_w2': nrm(ks[8], (L, RWKV_DECAY_LORA, RWKV_WIDTH), 0.1 * RWKV_DECAY_LORA ** -0.5),
        'rwkv_a0': nrm(ks[9], (L, RWKV_WIDTH), 0.1),
        'rwkv_a2': nrm(ks[10], (L, RWKV_ICLR_LORA, RWKV_WIDTH), RWKV_ICLR_LORA ** -0.5),
        'rwkv_g2': nrm(ks[11], (L, RWKV_GATE_LORA, RWKV_WIDTH), RWKV_GATE_LORA ** -0.5),
        'rwkv_k_k': 0.85 + nrm(ks[12], (L, RWKV_WIDTH), 0.02),
        'rwkv_k_a': 1.0 + nrm(ks[13], (L, RWKV_WIDTH), 0.02),
        'rwkv_r_k': -0.04 + nrm(ks[14], (L, RWKV_HEADS, RWKV_HEAD_DIM), 0.02),
        'rwkv_ln_w': 1.0 + nrm(ks[15], (L, RWKV_WIDTH), 0.02),
        'rwkv_ln_b': nrm(ks[16], (L, RWKV_WIDTH), 0.02),
        'w_branch_a': nrm(ks[17], (L, GLA_V_WIDTH, D_MODEL), GLA_V_WIDTH ** -0.5),
        'w_branch_b': nrm(ks[18], (L, RWKV_WIDTH, D_MODEL), RWKV_WIDTH ** -0.5),
        'w_out': nrm(ks[19], (L, D_MODEL, D_MODEL), D_MODEL ** -0.5),
        'norm_ffn_g': 1.0 + nrm(ks[20], (L, D_MODEL), 0.02),
        'router_w': nrm(ks[21], (L, D_MODEL, N_EXPERTS), D_MODEL ** -0.5),
        'router_b': nrm(ks[22], (L, N_EXPERTS), 0.01),
        'expert_w1': nrm(ks[23], (L, N_EXPERTS, D_MODEL, 2 * EXPERT_FF), D_MODEL ** -0.5),
        'expert_b1': nrm(ks[24], (L, N_EXPERTS, 2 * EXPERT_FF), 0.01),
        'expert_w2': nrm(ks[25], (L, N_EXPERTS, EXPERT_FF, D_MODEL), EXPERT_FF ** -0.5),
        'expert_b2': nrm(ks[26], (L, N_EXPERTS, D_MODEL), 0.01),
        'norm_final_g': 1.0 + nrm(ks[27], (D_MODEL,), 0.02),
    }

def reference(x, norm_mix_g, w_in, gla_gate_up, gla_gate_bias, gla_norm_g, rwkv_mu, rwkv_w0, rwkv_w2, rwkv_a0,
              rwkv_a2, rwkv_g2, rwkv_k_k, rwkv_k_a, rwkv_r_k, rwkv_ln_w, rwkv_ln_b, w_branch_a, w_branch_b, w_out,
              norm_ffn_g, router_w, router_b, expert_w1, expert_b1, expert_w2, expert_b2, norm_final_g):
    for l in range(DEPTH):
        h = rms_norm(x, norm_mix_g[l])
        x = x + hybrid_mixer(h, w_in[l], gla_gate_up[l], gla_gate_bias[l], gla_norm_g[l], rwkv_mu[l], rwkv_w0[l],
                             rwkv_w2[l], rwkv_a0[l], rwkv_a2[l], rwkv_g2[l], rwkv_k_k[l], rwkv_k_a[l], rwkv_r_k[l],
                             rwkv_ln_w[l], rwkv_ln_b[l], w_branch_a[l], w_branch_b[l], w_out[l])
        h = rms_norm(x, norm_ffn_g[l])
        x = x + moe_ffn(h, router_w[l], router_b[l], expert_w1[l], expert_b1[l], expert_w2[l], expert_b2[l])
    return rms_norm(x, norm_final_g)


_drawn_inputs = setup_inputs


def setup_inputs(seed=0):
    import zlib

    import numpy as np

    out = dict(_drawn_inputs(seed))
    spreads = {}
    factors = {'rwkv_w2': 3.485,
     'rwkv_k_k': 16.529,
     'expert_b1': 8.0,
     'expert_b2': 8.0,
     'norm_final_g': 9.724,
     'rwkv_k_a': 3.287}
    for name, (base, spread) in spreads.items():
        noise = np.random.default_rng([zlib.crc32(name.encode()), seed]).standard_normal(out[name].shape)
        drawn = base * np.exp(spread * noise) if base else spread * noise
        out[name] = __import__('jax').numpy.asarray(drawn.astype(out[name].dtype))
    for name, factor in factors.items():
        out[name] = (out[name] * factor).astype(out[name].dtype)
    return out
```

```python
from contextlib import ExitStack

import numpy as np

import concourse.bass as bass
from concourse import mybir

ALU = mybir.AluOpType
ACT = mybir.ActivationFunctionType
F32 = mybir.dt.float32
I32 = mybir.dt.int32
U8 = mybir.dt.uint8
AX_X = mybir.AxisListType.X

P = 128
T = 256
NT = T // P
D = 1024
KD = D // P
ITERS = 4
CH = 64
NCH = T // CH
HN = 64
E = 32
FF = 1024
TOPK = 4
SLOTS = 64
PASSES = T // SLOTS
KAPPA = float(np.exp(-0.5))
RMS_EPS, GLA_EPS, GN_EPS = 1e-6, 1e-5, 64e-5
TAU = 16.0
LEVELS = (1, 2, 4, 8, 16, 32)

C_Q, C_K, C_V, C_LR, C_OG = 0, 512, 1024, 2048, 2064
C_RW = 3088
C_R, C_RK, C_RV, C_LORA = C_RW, C_RW + 1024, C_RW + 2048, C_RW + 3072
C_GA, C_GB = C_RW + 3328, C_RW + 3328 + 1024
RANK = 16

R_MIXG, R_W0, R_A0, R_KK, R_KA, R_RK, R_LNW, R_LNB, R_MU, R_GB, R_NG = 0, 8, 16, 24, 32, 40, 48, 56, 64, 90, 94
NROWS = 96
MU_R, MU_K, MU_V, MU_L = R_MU, R_MU + 8, R_MU + 16, R_MU + 24

WRING = 3
ROUND = ("rk", "rr", "rv", "qk", "gv", "og", "ga", "gb")


def weight_blocks():
    blocks = [("lora", 0), ("lr", 0)]
    blocks += [(kind, it) for it in range(ITERS) for kind in ROUND]
    for m in range(4):
        blocks += [("wa", m), ("wb", m)]
    return blocks + [("wo", m) for m in range(4)]


def fill_order():
    low, order = set(), []

    def z(name):
        low.add(name)
        order.append(name)

    order.append(("par",))
    order.extend(("hT", c) for c in range(KD // 2))

    def project(it):
        if it == 0:
            for j in range(2):
                z(("z", "lora", 0, j))
            z(("z", "lr", 0, 0))
        for kind in ROUND:
            for j in range(2):
                z(("z", kind, it, j))
        order.extend([("lw", it), ("la", it), ("lg", it), ("gl", it)])

    def norms(it):
        order.extend([("kn", it), ("bo", it)])

    def core(it):
        order.extend((("tr", it, kind) for kind in "ABKV"))
        for kind in "BK":
            for hh in range(2):
                for u in range(2):
                    order.append(("L" + kind, it, hh, u))
        order.extend(("LL", it, hh) for hh in range(2))
        order.append(("X", it))
        for lev in LEVELS[1:]:
            order.extend(("Z", it, lev, g) for g in range(4))
            order.extend(("TG", it, lev, g) for g in range(4))
        order.extend([("Q", it), ("PT", it)])
        for c in range(NCH):
            if c:
                order.append(("U", it, c))
            if c < NCH - 1:
                order.append(("S", it, c))
        order.extend([("y", it), ("mean", it), ("var", it)])

    def gla(it):
        order.extend([("gs", it), ("gk", it)])
        order.extend(("gS", it, c) for c in range(NCH - 1))
        order.extend([("go", it), ("gn", it)])

    project(0)
    norms(0)
    for it in range(ITERS):
        if it + 1 < ITERS:
            project(it + 1)
        core(it)
        gla(it)
        if it + 1 < ITERS:
            norms(it + 1)
    for m in range(KD):
        z(("ba", m))
        z(("bb", m))
    for m in range(4):
        for tt in range(NT):
            z(("out", m, tt))
    order.extend(("h2T", c) for c in range(4))
    order.extend([("log",), ("pos",), ("cnt",), ("gT",)])
    order.extend(("b2", i) for i in range(4))
    bank, nth, used = {}, {}, [0] * 8
    turn = [0, 0]
    for name in order:
        lo = name in low
        b = turn[0] % 4 if lo else 4 + turn[1] % 4
        turn[0 if lo else 1] += 1
        bank[name], nth[name] = b, used[b]
        used[b] += 1
    return order, bank, nth, used


def bass_hybrid_gla_rwkv7_moe_block(
    nc, x, norm_mix_g, w_in, gla_gate_up, gla_gate_bias, gla_norm_g, rwkv_mu, rwkv_w0, rwkv_w2, rwkv_a0,
    rwkv_a2, rwkv_g2, rwkv_k_k, rwkv_k_a, rwkv_r_k, rwkv_ln_w, rwkv_ln_b, w_branch_a, w_branch_b, w_out,
    norm_ffn_g, router_w, router_b, expert_w1, expert_b1, expert_w2, expert_b2, norm_final_g, out, debug=None,
):
    order, bank_of, nth_of, fills = fill_order()
    blocks = weight_blocks()
    block_index = {b: n for n, b in enumerate(blocks)}

    with ExitStack() as ctx:
        def sem(name):
            return ctx.enter_context(nc.semaphore(name))

        def keep(name, shape, dt=F32):
            return ctx.enter_context(nc.sbuf_tensor(name, shape, dt))

        banks = [ctx.enter_context(nc.psum_tensor(f"bank{b}", [P, 512], F32)) for b in range(8)]

        xs = keep("xs", [P, NT, D])
        ident = keep("ident", [P, P])
        ones = keep("ones", [P, P])
        headones = keep("headones", [P, P])
        before = keep("before", [P, P])
        stat = keep("stat", [P, 16])
        epsc = keep("epsc", [P, 4])

        mix = ExitStack()

        def sb(name, shape, dt=F32):
            return mix.enter_context(nc.sbuf_tensor(name, shape, dt))

        wring = sb("wring", [P, WRING, KD, 256])
        hT = sb("hT", [P, KD, T])
        gates = sb("gates", [P, 16, T])
        yA = sb("yA", [P, KD, T])
        yB = sb("yB", [P, KD, T])
        prow = sb("prow", [P, P])
        pcol = sb("pcol", [P, NROWS])
        w2a2 = sb("w2a2", [P, D])
        g2 = sb("g2", [P, D])
        gup = sb("gup", [RANK, 512])
        below = sb("below", [P, P])
        upto = sb("upto", [P, P])
        upto8 = sb("upto8", [P, P], U8)
        low8 = sb("low8", [P, len(LEVELS), P], U8)
        up8 = sb("up8", [P, len(LEVELS), P], U8)
        chunkmask = sb("chunkmask", [P, 2 * T])
        zl = sb("zl", [P, 2, T + 1])
        ul = sb("ul", [P, 2, T])
        zlr = sb("zlr", [RANK, T])
        zs = sb("zs", [P, 6, T + 1])
        dsh = sb("dsh", [P, 6, T])
        u = sb("u", [P, 4, T])
        uv = sb("uv", [P, 2, 2, T])
        gg = sb("gg", [P, 2, 2, T])
        sgw = sb("sgw", [P, 2, T])
        aa = sb("aa", [P, 2, T])
        cc = sb("cc", [P, 2, T])
        cm = sb("cm", [P, 2, T])
        Wc = cc
        Wi = sb("Wi", [P, 2, T])
        Wp = cm
        kk0 = sb("kk0", [P, 2, T])
        sq = sb("sq", [P, 2, T])
        km = sb("km", [P, 2, T])
        bp = sb("bp", [P, 2, T])
        bon = sb("bon", [P, 2, T])
        ch4 = {k: sb("ch" + k, [P, 4, P]) for k in "bkBK"}
        AR = sb("AR", [P, 4, 2, P])
        tm = {k: sb("tm" + k, [P, 4, P]) for k in "ABKV"}
        mats = {k: sb("m" + k, [P, 8, P]) for k in ("N", "T", "G", "Z", "Mrb", "Mrk")}
        mats["Lak"] = mats["Z"]
        Xs = sb("Xs", [P, 4, P])
        Qs = sb("Qs", [P, 4, P])
        PTs = sb("PTs", [P, 4, P])
        Us = Xs
        Ss = sb("Ss", [P, NCH - 1, 2, P])
        ys = sb("ys", [P, 2, T])
        gq = sb("gq", [P, 2, T])
        gk = sb("gk", [P, 2, T])
        gv = sb("gv", [P, 2, NT, T])
        og = sb("og", [P, 2, 2, T])
        gx = sb("gx", [P, 2, T])
        halves = {k: ch4[k][:, :, :].rearrange("p a t -> p (a t)").rearrange("p (a t) -> p a t", t=T) for k in "bkBK"}
        gprod = [halves["b"][:, 0, :], halves["b"][:, 1, :], halves["k"][:, 0, :], halves["k"][:, 1, :]]
        gtmp = [halves["B"][:, 0, :], halves["B"][:, 1, :], halves["K"][:, 0, :], halves["K"][:, 1, :]]
        gsT = mats["N"][:, 0:2, :]
        gkt = mats["N"][:, 2:4, :]
        gSt = mats["Mrb"][:, :, :].rearrange("p (c a) t -> p c (a t)", a=2)

        ints = og[:, :, :, :].rearrange("p a b t -> p (a b t)").bitcast(I32).rearrange("p (a t) -> p a t", t=P)
        mix.close()

        moe = ctx.enter_context(ExitStack())

        def mb(name, shape, dt=F32):
            return moe.enter_context(nc.sbuf_tensor(name, shape, dt))

        h2 = mb("h2", [P, NT, D])
        w1s = mb("w1s", [P, KD, 2 * FF])
        w2s = mb("w2s", [P, FF // P, D])
        ffn_g = mb("ffn_g", [P, D])
        final_g = mb("final_g", [P, D])
        rw = mb("rw", [P, KD, E])
        rb = mb("rb", [P, E])
        acc = xs
        h2T = mb("h2T", [P, KD, T])
        b1s = mb("b1s", [E, 2 * FF])
        b2s = mb("b2s", [E, D])
        lg = mb("lg", [P, NT, E])
        top = mb("top", [P, NT, 8])
        rt = mb("rt", [P, 6, NT, E])
        selM = mb("selM", [P, NT, E])
        posm = mb("posm", [P, E, NT])
        gatev = mb("gatev", [P, E, NT])
        gT = mb("gT", [E, T])
        rs = mb("rs", [P, 16])
        over = mb("over", [P, 1], I32)
        iota = mb("iota", [P, (PASSES + 1) * SLOTS])
        onesE = mb("onesE", [E, SLOTS])
        ehot = mb("ehot", [E, SLOTS])
        sel = mb("sel", [P, NT, SLOTS])
        selg = mb("selg", [P, NT, 2, SLOTS])
        selgT = mb("selgT", [P, NT, P])
        xg = mb("xg", [P, KD, SLOTS])
        glu = mb("glu", [P, 2, 256])
        sgm = mb("sgm", [P, 2, 256])
        lin = mb("lin", [P, 2, 256])
        act_s = mb("act_s", [P, 2, 256])
        actT = mb("actT", [P, 4, P])
        eo = mb("eo", [P, 512])

        filled = [sem(f"bank{b}_filled") for b in range(8)]
        drained = [sem(f"bank{b}_drained") for b in range(8)]
        x_in, rows_in, lora_in, late_in = sem("x_in"), sem("rows_in"), sem("lora_in"), sem("late_in")
        w_in_ready = [sem(f"weights_in{s}") for s in range(WRING)]
        w_used = sem("weights_used")
        dve_step, act_step, pool_step = sem("dve_step"), sem("act_step"), sem("pool_step")
        raw_consts, mask_ready, consts_ready = sem("raw_consts"), sem("mask_ready"), sem("consts_ready")
        sumsq_ready, rstd_ready, xn_ready = sem("sumsq_ready"), sem("rstd_ready"), sem("xn_ready")
        lora_mixed, lora_act = sem("lora_mixed"), sem("lora_act")
        shifted = sem("shifted")
        cum_ready, exps_ready = sem("cum_ready"), sem("exps_ready")
        ksq_ready, bprod_ready, knorm_ready = sem("ksq_ready"), sem("bprod_ready"), sem("knorm_ready")
        prepared = sem("prepared")
        eye_ready, u0_ready = sem("eye_ready"), sem("u0_ready")
        ysq_ready, ystd_ready, yB_ready = sem("ysq_ready"), sem("ystd_ready"), sem("yB_ready")
        softplus_ready = sem("softplus_ready")
        b_ready, gexp_ready, gprep_ready = sem("b_ready"), sem("gexp_ready"), sem("gprep_ready")
        gsq_ready, gstd_ready, yA_ready = sem("gsq_ready"), sem("gstd_ready"), sem("yA_ready")
        merged_ready, x1_ready, h2_ready = sem("merged_ready"), sem("x1_ready"), sem("h2_ready")
        mask_sel, route_ready, gexpo = sem("mask_sel"), sem("route_ready"), sem("gexpo")
        lmax_ready, gatev_ready = sem("lmax_ready"), sem("gatev_ready")
        moe_pool = sem("moe_pool")
        w1_in = [sem(f"w1_in{k}") for k in range(KD)]
        w2_in = [sem(f"w2_in{k}") for k in range(4)]
        w1_used, w2_used = sem("w1_used"), sem("w2_used")
        sel_ready, selg_ready = sem("sel_ready"), sem("selg_ready")
        gather_done, selT_done = sem("gather_done"), sem("selT_done")
        xg_ready, selgT_ready = sem("xg_ready"), sem("selgT_ready")
        hid_done, glu_ready, sgm_ready, act_ready = (
            sem("hid_done"), sem("glu_ready"), sem("sgm_ready"), sem("act_ready"))
        actT_done, actT_ready = sem("actT_done"), sem("actT_ready")
        eo_done, eo_ready = sem("eo_done"), sem("eo_ready")
        y_done, y_added = sem("y_done"), sem("y_added")
        final_ready, out_done = sem("final_ready"), sem("out_done")

        def view(name, *shape):
            b = banks[bank_of[name]][:, :]
            if len(shape) == 2:
                return b[:, 0:shape[0] * shape[1]].rearrange("p (a b) -> p a b", a=shape[0])
            if len(shape) == 3:
                return b[:, 0:shape[0] * shape[1] * shape[2]].rearrange("p (a b c) -> p a b c", a=shape[0], b=shape[1])
            return b[:, 0:shape[0]]

        def await_filled(eng, name):
            eng.wait_ge(filled[bank_of[name]], nth_of[name] + 1)

        def await_drained(eng, name):
            eng.wait_ge(drained[bank_of[name]], nth_of[name] + 1)

        def wait_after(eng, semaphore, value):
            if not (isinstance(value, int) and value == 0):
                eng.wait_ge(semaphore, value)

        ring_count, slot_total = [], [0] * WRING
        for n, (kind, _) in enumerate(blocks):
            slot_total[n % WRING] += 32 if kind == "qk" else 16
            ring_count.append(slot_total[n % WRING])

        def wslot(kind, it):
            return wring[:, block_index[(kind, it)] % WRING]

        def col(row):
            return pcol[:, row:row + 1]

        win = w_in[0].rearrange("(k p) n -> p k n", p=P)
        branch = {
            "wa": w_branch_a[0].rearrange("(k p) n -> p k n", p=P),
            "wb": w_branch_b[0].rearrange("(k p) n -> p k n", p=P),
            "wo": w_out[0].rearrange("(k p) n -> p k n", p=P),
        }

        ehot_ready = sem("ehot_ready")
        glu_half, lin_ready, gated_ready = sem("glu_half"), sem("lin_ready"), sem("gated_ready")

        block = ctx.enter_context(nc.Block())

        @block.sync
        def _(sp):
            sp.dma_start(xs[:, :, :], x[0].rearrange("(a p) d -> p a d", p=P)).then_inc(x_in, 16)
            rows = [
                (R_MIXG, 8, norm_mix_g[0]), (R_W0, 8, rwkv_w0[0]), (R_A0, 8, rwkv_a0[0]), (R_KK, 8, rwkv_k_k[0]),
                (R_KA, 8, rwkv_k_a[0]), (R_RK, 8, rwkv_r_k[0].rearrange("h n -> (h n)")), (R_LNW, 8, rwkv_ln_w[0]),
                (R_LNB, 8, rwkv_ln_b[0]), (R_MU, 26, rwkv_mu[0]), (R_GB, 4, gla_gate_bias[0]), (R_NG, 2, gla_norm_g[0]),
            ]
            for r0, n, src in rows:
                sp.dma_start(prow[r0:r0 + n, :], src.rearrange("(r c) -> r c", c=P)).then_inc(rows_in, 16)
            for n, (kind, it) in enumerate(blocks):
                if n >= WRING:
                    sp.wait_ge(w_used, n - WRING + 1)
                dst = wring[:, n % WRING]
                ready = w_in_ready[n % WRING]
                if kind in branch:
                    sp.dma_start(dst, branch[kind][:, :, 256 * it:256 * it + 256]).then_inc(ready, 16)
                elif kind == "qk":
                    sp.dma_start(dst[:, :, 0:P], win[:, :, C_Q + P * it:C_Q + P * it + P]).then_inc(ready, 16)
                    sp.dma_start(dst[:, :, P:2 * P], win[:, :, C_K + P * it:C_K + P * it + P]).then_inc(ready, 16)
                else:
                    first = {"lora": C_LORA, "lr": C_LR, "rk": C_RK, "rr": C_R, "rv": C_RV, "gv": C_V, "og": C_OG,
                             "ga": C_GA, "gb": C_GB}[kind] + 256 * it
                    width = RANK if kind == "lr" else 256
                    sp.dma_start(dst[:, :, 0:width], win[:, :, first:first + width]).then_inc(ready, 16)
                if n == 1:
                    sp.dma_start(w2a2[0:64, :], rwkv_w2[0]).then_inc(lora_in, 16)
                    sp.dma_start(w2a2[64:128, :], rwkv_a2[0]).then_inc(lora_in, 16)
                    sp.dma_start(g2[:, :], rwkv_g2[0]).then_inc(lora_in, 16)
                    sp.dma_start(gup[:, :], gla_gate_up[0]).then_inc(lora_in, 16)
            await_filled(sp, ("out", 3, 1))
            sp.wait_ge(x1_ready, 1)
            sp.wait_ge(merged_ready, KD)
            sp.dma_start(b1s[:, :], expert_b1[0]).then_inc(late_in, 16)
            sp.dma_start(b2s[:, :], expert_b2[0]).then_inc(late_in, 16)
            sp.dma_start(rw[:, :, :], router_w[0].rearrange("(k p) e -> p k e", p=P)).then_inc(late_in, 16)
            sp.dma_start(rb[:, :], router_b.broadcast_to([P, E])).then_inc(late_in, 16)
            sp.dma_start(ffn_g[:, :], norm_ffn_g.broadcast_to([P, D])).then_inc(late_in, 16)
            sp.dma_start(final_g[:, :], norm_final_g.rearrange("(a d) -> a d", a=1).broadcast_to([P, D])).then_inc(late_in, 16)

            w1v = expert_w1[0].rearrange("e (k p) n -> e p k n", p=P)
            w2v = expert_w2[0].rearrange("e (k p) n -> e p k n", p=P)

            def load_expert(i):
                e = i if isinstance(i, int) else i % E
                for k in range(KD):
                    if not isinstance(i, int):
                        sp.wait_ge(w1_used, (i - 1) * KD + (k + 1))
                    sp.dma_start(w1s[:, k, :], w1v[bass.ds(e, 1), :, k, :].rearrange("a p n -> (a p) n")).then_inc(w1_in[k], 16)
                for k in range(4):
                    if not isinstance(i, int):
                        sp.wait_ge(w2_used, (i - 1) * 4 + (k + 1))
                    sp.dma_start(w2s[:, 2 * k:2 * k + 2, :],
                                 w2v[bass.ds(e, 1), :, 2 * k:2 * k + 2, :].rearrange("a p k n -> (a p) k n")).then_inc(w2_in[k], 16)

            load_expert(0)
            with sp.Fori(1, E) as i:
                load_expert(i)
            sp.wait_ge(route_ready, 1)
            most = sp.value_load(over[0:1, 0:1], min_val=0, max_val=T)
            with sp.If(most > SLOTS):
                with sp.Fori(E, PASSES * E) as i:
                    load_expert(i)
            sp.wait_ge(final_ready, 1)
            sp.dma_start(out[0].rearrange("(a p) d -> p a d", p=P), h2T[:, :, :].rearrange("p a b -> p (a b)").rearrange(
                "p (a d) -> p a d", a=NT)).then_inc(out_done, 16)
            sp.wait_ge(out_done, 16)

        @block.gpsimd
        def _(pool):
            pool.memset(ones[:, :], 1.0).then_inc(raw_consts, 1)
            pool.iota(ints[:, 0, :], [[0, P]], 0, 1).then_inc(raw_consts, 1)
            pool.iota(ints[:, 1, :], [[1, P]], 0, 0).then_inc(raw_consts, 1)
            pool.memset(zs[:, :, 0:1], 0.0).then_inc(raw_consts, 1)
            pool.memset(zl[:, :, 0:1], 0.0).then_inc(raw_consts, 1)
            pool.memset(Ss[:, :, :, :], 0.0).then_inc(raw_consts, 1)
            pool.memset(chunkmask[:, :], 1.0).then_inc(raw_consts, 1)
            pool.wait_ge(raw_consts, 7)
            pool.memset(chunkmask[:, :].rearrange("p (c t) -> p c t", t=CH)[:, :, 0:1], 0.0).then_inc(raw_consts, 1)
            pool.memset(epsc[:, 0:1], RMS_EPS).then_inc(raw_consts, 1)
            pool.memset(epsc[:, 1:2], GLA_EPS).then_inc(raw_consts, 1)
            pool.memset(epsc[:, 2:3], GN_EPS).then_inc(raw_consts, 1)
            for it in range(ITERS):
                if it == 0:
                    pool.wait_ge(consts_ready, 1)
                else:
                    await_filled(pool, ("PT", it - 1))
                for k in "TG":
                    pool.tensor_copy(mats[k][:, :, :], ident[:, :].unsqueeze(1).broadcast_to([P, 8, P])).then_inc(eye_ready, 1)
            pool.wait_ge(x1_ready, 1)
            pool.iota(iota[:, :], [[1, (PASSES + 1) * SLOTS]], 0, 0,
                      allow_small_or_imprecise_dtypes=True).then_inc(moe_pool, 1)
            pool.memset(onesE[:, :], 1.0).then_inc(moe_pool, 1)

        @block.scalar
        def _(act):
            steps = [0]

            def link(ins):
                steps[0] += 1
                ins.then_inc(act_step, 1)
                act.wait_ge(act_step, steps[0])

            def drains(ins, name):
                ins.then_inc(drained[bank_of[name]], 1)

            act.wait_ge(x_in, 16)
            act.wait_ge(raw_consts, 11)
            for tt in range(NT):
                act.activation(hT[:, 4 * tt:4 * tt + 4, :].rearrange("p a b -> p (a b)"), xs[:, tt, :], ACT.Square,
                               accum_out=stat[:, tt:tt + 1]).then_inc(sumsq_ready, 1)
            act.wait_ge(sumsq_ready, 2)
            act.activation(stat[:, 2:4], stat[:, 0:2], ACT.Sqrt, bias=epsc[:, 0:1], scale=1.0 / D).then_inc(sumsq_ready, 1)
            act.wait_ge(rstd_ready, 1)
            xn = yA[:, :, :].rearrange("p a b -> p (a b)").rearrange("p (a d) -> p a d", a=NT)
            for tt in range(NT):
                act.activation(xn[:, tt, :], xs[:, tt, :], ACT.Copy, scale=stat[:, 4 + tt:5 + tt]).then_inc(xn_ready, 1)

            def project(it):
                par = it % 2
                if it == 0:
                    for j in range(2):
                        name = ("z", "lora", 0, j)
                        await_filled(act, name)
                        drains(act.activation(zl[:, j, 1:T + 1], view(name, T), ACT.Copy), name)
                    name = ("z", "lr", 0, 0)
                    await_filled(act, name)
                    drains(act.activation(zlr[:, :], view(name, T)[0:RANK, :], ACT.Copy), name)
                else:
                    act.wait_ge(shifted, it)
                for kind in ROUND:
                    if kind == "qk" and it >= 2:
                        act.wait_ge(yA_ready, it - 1)
                    for j in range(2):
                        name = ("z", kind, it, j)
                        await_filled(act, name)
                        z = view(name, T)
                        if kind in ("rk", "rr", "rv"):
                            at = 2 * ("rk", "rr", "rv").index(kind) + j
                            drains(act.activation(zs[:, at, 1:T + 1], z, ACT.Copy), name)
                        elif kind == "qk":
                            drains(act.activation((gq, gk)[j][:, par, :], z, ACT.Copy,
                                                  scale=float(P) ** -0.5 if j == 0 else 1.0), name)
                        elif kind == "gv":
                            drains(act.activation(gv[:, par, j, :], z, ACT.Copy), name)
                        elif kind == "og":
                            drains(act.activation(og[:, par, j, :], z, ACT.Copy), name)
                        else:
                            at = (0 if kind == "ga" else KD) + 2 * it + j
                            drains(act.activation(gates[:, at, :], z, ACT.Sigmoid), name)
                if it == 0:
                    act.wait_ge(lora_mixed, 1)
                    act.activation(ul[0:64, 0, :], ul[0:64, 0, :], ACT.Tanh).then_inc(lora_act, 1)
                    act.activation(ul[:, 1, :], ul[:, 1, :], ACT.Sigmoid).then_inc(lora_act, 1)
                if it >= 1:
                    act.wait_ge(prepared, it)
                for key, dst, r0 in (("lw", sgw, R_W0), ("la", aa, R_A0)):
                    await_filled(act, (key, it))
                    link(act.activation(dst[:, 0, :], view((key, it), 2, T)[:, 0, :], ACT.Sigmoid, bias=col(r0 + 2 * it)))
                    drains(act.activation(dst[:, 1, :], view((key, it), 2, T)[:, 1, :], ACT.Sigmoid,
                                          bias=col(r0 + 2 * it + 1)), (key, it))
                await_filled(act, ("lg", it))
                if it >= 2:
                    act.wait_ge(yB_ready, it - 1)
                drains(act.activation(gg[:, par, :, :], view(("lg", it), 2, T), ACT.Copy), ("lg", it))
                await_filled(act, ("gl", it))
                drains(act.activation(gx[:, par, :], view(("gl", it), T), ACT.Identity, bias=col(R_GB + it)), ("gl", it))

            def exps(it):
                await_filled(act, ("kn", it))
                act.activation(kk_n, view(("kn", it), 512), ACT.Sqrt).then_inc(drained[bank_of[("kn", it)]], 1)
                act.wait_ge(cum_ready, it + 1)
                if it >= 1:
                    act.wait_ge(yB_ready, it)
                act.activation(Wi[:, :, :], cc[:, :, :], ACT.Exp, scale=KAPPA).then_inc(exps_ready, 1)
                act.activation(Wc[:, :, :], cc[:, :, :], ACT.Exp, scale=-KAPPA).then_inc(exps_ready, 1)
                act.activation(Wp[:, :, :], cm[:, :, :], ACT.Exp, scale=-KAPPA).then_inc(exps_ready, 1)

            kk_n = sq[:, :, :].rearrange("p a b -> p (a b)")

            def core(it):
                for kind in "ABKV":
                    await_filled(act, ("tr", it, kind))
                    drains(act.activation(tm[kind][:, :, :], view(("tr", it, kind), 4, P), ACT.Copy), ("tr", it, kind))
                await_filled(act, ("X", it))
                drains(act.activation(Xs[:, :, :], view(("X", it), 4, P), ACT.Copy), ("X", it))
                for lev in LEVELS[1:]:
                    for g in range(4):
                        name = ("Z", it, lev, g)
                        await_filled(act, name)
                        drains(act.activation(mats["Z"][:, 2 * g:2 * g + 2, :], view(name, 2, P), ACT.Copy), name)
                for key, dst in (("Q", Qs), ("PT", PTs)):
                    await_filled(act, (key, it))
                    drains(act.activation(dst[:, :, :], view((key, it), 4, P), ACT.Copy), (key, it))
                await_filled(act, ("y", it))
                drains(act.activation(ys[:, :, :], view(("y", it), 2, T), ACT.Copy), ("y", it))
                await_filled(act, ("var", it))
                drains(act.activation(kk_n2, view(("var", it), 512), ACT.Sqrt, bias=epsc[:, 2:3], scale=1.0 / HN), ("var", it))

            kk_n2 = dsh[:, 0:2, :].rearrange("p a b -> p (a b)")

            def gla(it):
                act.wait_ge(yB_ready, it + 1)
                link(act.activation(gtmp[0], gx[:, it % 2, :], ACT.Abs))
                link(act.activation(gtmp[0], gtmp[0], ACT.Exp, scale=-1.0))
                act.activation(gtmp[1], gtmp[0], ACT.Ln, bias=1.0).then_inc(softplus_ready, 1)
                act.wait_ge(b_ready, it + 1)
                for k in range(4):
                    src = (dsh[:, 2, :], dsh[:, 2, :], dsh[:, 3, :], dsh[:, 4, :])[k]
                    act.activation(gtmp[k], src, ACT.Exp, scale=(-1.0 if k == 1 else 1.0) / TAU).then_inc(gexp_ready, 1)
                act.activation(dsh[:, 0:2, :], og[:, it % 2, :, :], ACT.Sigmoid).then_inc(gexp_ready, 1)
                await_filled(act, ("gk", it))
                drains(act.activation(gkt[:, :, :], view(("gk", it), 2, P), ACT.Copy), ("gk", it))
                await_filled(act, ("go", it))
                act.activation(dsh[:, 2:4, :], view(("go", it), 2, T), ACT.Square).then_inc(gsq_ready, 1)
                await_filled(act, ("gn", it))
                drains(act.activation(dsh[:, 4, :], view(("gn", it), T), ACT.Sqrt, bias=epsc[:, 1:2], scale=1.0 / 256), ("gn", it))

            act.wait_ge(consts_ready, 1)
            project(0)
            exps(0)
            for it in range(ITERS):
                if it + 1 < ITERS:
                    project(it + 1)
                core(it)
                gla(it)
                if it + 1 < ITERS:
                    exps(it + 1)
            act.wait_ge(x1_ready, 1)
            for tt in range(NT):
                act.activation(h2[:, tt, :], xs[:, tt, :], ACT.Square, accum_out=stat[:, 6 + tt:7 + tt]).then_inc(sumsq_ready, 1)
            act.wait_ge(sumsq_ready, 5)
            act.activation(stat[:, 8:10], stat[:, 6:8], ACT.Sqrt, bias=epsc[:, 0:1], scale=1.0 / D).then_inc(sumsq_ready, 1)
            act.wait_ge(lmax_ready, 1)
            for tt in range(NT):
                act.activation(rt[:, 4, tt, :], lg[:, tt, :], ACT.Exp, bias=rs[:, tt:tt + 1]).then_inc(gexpo, 1)

            def gathered(i):
                act.wait_ge(gather_done, i + 1)
                act.activation(xg[:, :, :], banks[0][:, :].rearrange("p (k s) -> p k s", k=KD), ACT.Copy).then_inc(xg_ready, 1)

            def expert(i):
                act.wait_ge(glu_ready, i + 1)
                act.activation(sgm[:, :, :], glu[:, :, :], ACT.Sigmoid, scale=1.702).then_inc(sgm_ready, 1)
                gathered(i + 1)
                act.wait_ge(actT_done, i + 1)
                act.activation(actT[:, :, :], banks[4][:, :].rearrange("p (k s) -> p k s", k=4), ACT.Copy).then_inc(actT_ready, 1)
                act.wait_ge(eo_done, i + 1)
                act.activation(eo[:, :], banks[5][:, :], ACT.Copy).then_inc(eo_ready, 1)

            gathered(0)
            expert(0)
            with act.Fori(1, E) as i:
                expert(i)
            act.wait_ge(route_ready, 1)
            most = act.value_load(over[0:1, 0:1], min_val=0, max_val=T)
            with act.If(most > SLOTS):
                with act.Fori(E, PASSES * E) as i:
                    expert(i)
            act.wait_ge(mask_sel, 3)
            for tt in range(NT):
                act.activation(h2[:, tt, :], xs[:, tt, :], ACT.Square, accum_out=stat[:, 10 + tt:11 + tt]).then_inc(sumsq_ready, 1)
            act.wait_ge(sumsq_ready, 8)
            act.activation(stat[:, 12:14], stat[:, 10:12], ACT.Sqrt, bias=epsc[:, 0:1], scale=1.0 / D).then_inc(sumsq_ready, 1)

        @block.vector
        def _(dve):
            steps = [0]

            def link(ins):
                steps[0] += 1
                ins.then_inc(dve_step, 1)
                dve.wait_ge(dve_step, steps[0])

            def drains(ins, name):
                ins.then_inc(drained[bank_of[name]], 1)
                dve.wait_ge(drained[bank_of[name]], nth_of[name] + 1)

            dve.wait_ge(raw_consts, 11)
            diff = gates[:, :, :].rearrange("p a b -> p (a b)").rearrange("p (a t) -> p a t", t=P)
            for k in range(7):
                link(dve.tensor_scalar(ints[:, 2, :], ints[:, 0, :], k, None, ALU.arith_shift_right))
                link(dve.tensor_scalar(ints[:, 3, :], ints[:, 1, :], k, None, ALU.arith_shift_right))
                link(dve.tensor_tensor(diff[:, k, :], ints[:, 2, :], ints[:, 3, :], ALU.subtract))
            link(dve.tensor_scalar(ident[:, :], diff[:, 0, :], 0.0, None, ALU.is_equal))
            link(dve.tensor_scalar(before[:, :], diff[:, 0, :], 0.0, None, ALU.is_lt))
            link(dve.tensor_scalar(headones[:, :], diff[:, 6, :], 0.0, None, ALU.is_equal))
            link(dve.tensor_tensor(below[:, :], before[:, :], headones[:, :], ALU.mult))
            link(dve.tensor_tensor(upto[:, :], below[:, :], ident[:, :], ALU.add))
            link(dve.tensor_copy(upto8[:, :], upto[:, :]))
            for k in range(len(LEVELS)):
                link(dve.tensor_scalar(diff[:, 8, :], diff[:, k + 1, :], 0.0, None, ALU.is_equal))
                link(dve.scalar_tensor_tensor(out=low8[:, k, :], in0=diff[:, k, :], scalar=1.0, in1=diff[:, 8, :],
                                              op0=ALU.is_equal, op1=ALU.mult))
                link(dve.scalar_tensor_tensor(out=up8[:, k, :], in0=diff[:, k, :], scalar=-1.0, in1=diff[:, 8, :],
                                              op0=ALU.is_equal, op1=ALU.mult))
            dve.sem_inc(consts_ready, 1)

            dve.wait_ge(sumsq_ready, 3)
            dve.reciprocal(stat[:, 4:6], stat[:, 2:4]).then_inc(rstd_ready, 1)
            await_filled(dve, ("par",))
            drains(dve.tensor_copy(pcol[:, :], view(("par",), NROWS)), ("par",))
            for c in range(KD // 2):
                name = ("hT", c)
                await_filled(dve, name)
                link(dve.tensor_scalar(hT[:, 2 * c, :], view(name, 2, T)[:, 0, :], col(R_MIXG + 2 * c), None, ALU.mult))
                drains(dve.tensor_scalar(hT[:, 2 * c + 1, :], view(name, 2, T)[:, 1, :], col(R_MIXG + 2 * c + 1), None,
                                         ALU.mult), name)

            def first_half(it):
                par = it % 2
                if it == 0:
                    await_drained(dve, ("z", "lora", 0, 1))
                    link(dve.tensor_tensor(dsh[:, 0:2, :], zl[:, :, 0:T], zl[:, :, 1:T + 1], ALU.subtract))
                    link(dve.scalar_tensor_tensor(out=ul[:, 0, :], in0=dsh[:, 0, :], scalar=col(MU_L), in1=zl[:, 0, 1:T + 1],
                                                  op0=ALU.mult, op1=ALU.add))
                    link(dve.scalar_tensor_tensor(out=ul[:, 1, :], in0=dsh[:, 1, :], scalar=col(MU_L + 1),
                                                  in1=zl[:, 1, 1:T + 1], op0=ALU.mult, op1=ALU.add))
                    dve.sem_inc(lora_mixed, 1)
                await_drained(dve, ("z", "rv", it, 1))
                link(dve.tensor_tensor(dsh[:, :, :], zs[:, :, 0:T], zs[:, :, 1:T + 1], ALU.subtract))
                for n in range(6):
                    kind, j = n // 2, n % 2
                    dst = u[:, n, :] if n < 4 else uv[:, par, j, :]
                    mu = (MU_K, MU_R, MU_V)[kind] + 2 * it + j
                    ins = dve.scalar_tensor_tensor(out=dst, in0=dsh[:, n, :], scalar=col(mu), in1=zs[:, n, 1:T + 1],
                                                   op0=ALU.mult, op1=ALU.add)
                    if n < 5:
                        link(ins)
                    else:
                        ins.then_inc(shifted, 1)
                        dve.wait_ge(shifted, it + 1)
                for j in range(2):
                    link(dve.tensor_scalar(kk0[:, j, :], u[:, j, :], col(R_KK + 2 * it + j), None, ALU.mult))
                dve.tensor_tensor(sq[:, :, :], kk0[:, :, :], kk0[:, :, :], ALU.mult).then_inc(ksq_ready, 1)
                dve.wait_ge(ksq_ready, it + 1)
                await_drained(dve, ("la", it))
                for j in range(2):
                    link(dve.tensor_scalar(km[:, j, :], aa[:, j, :], -1.0, col(R_KA + 2 * it + j), ALU.add, ALU.mult))
                link(dve.scalar_tensor_tensor(out=km[:, :, :], in0=km[:, :, :], scalar=1.0, in1=u[:, 0:2, :],
                                              op0=ALU.add, op1=ALU.mult))
                link(dve.scalar_tensor_tensor(out=bp[:, 0, :], in0=u[:, 2, :], scalar=col(R_RK + 2 * it), in1=km[:, 0, :],
                                              op0=ALU.mult, op1=ALU.mult))
                dve.scalar_tensor_tensor(out=bp[:, 1, :], in0=u[:, 3, :], scalar=col(R_RK + 2 * it + 1), in1=km[:, 1, :],
                                         op0=ALU.mult, op1=ALU.mult).then_inc(bprod_ready, 1)
                dve.wait_ge(bprod_ready, it + 1)

            def second_half(it):
                await_drained(dve, ("la", it))
                link(dve.tensor_tensor_scan(cc[:, :, :].rearrange("p a b -> p (a b)"), chunkmask[:, :],
                                            sgw[:, :, :].rearrange("p a b -> p (a b)"), 0.0, ALU.mult, ALU.add))
                dve.tensor_tensor(cm[:, :, :], cc[:, :, :], sgw[:, :, :], ALU.subtract).then_inc(cum_ready, 1)
                dve.wait_ge(cum_ready, it + 1)
                await_drained(dve, ("kn", it))
                link(dve.tensor_scalar(sq[:, :, :], sq[:, :, :], 1e-12, None, ALU.max))
                link(dve.reciprocal(sq[:, :, :], sq[:, :, :]))
                link(dve.tensor_tensor(kk0[:, :, :], kk0[:, :, :], sq[:, :, :], ALU.mult))
                await_filled(dve, ("bo", it))
                drains(dve.tensor_tensor(bon[:, :, :], view(("bo", it), 2, T), uv[:, it % 2, :, :], ALU.mult), ("bo", it))
                dve.wait_ge(exps_ready, 3 * (it + 1))
                w4 = [w[:, :, :].rearrange("p j (a t) -> p (j a) t", t=P) for w in (Wc, Wi, Wp)]
                kk4 = kk0[:, :, :].rearrange("p j (a t) -> p (j a) t", t=P)
                link(dve.scalar_tensor_tensor(out=AR[:, :, 0, :], in0=kk4, scalar=-1.0, in1=w4[2], op0=ALU.mult, op1=ALU.mult))
                link(dve.tensor_tensor(AR[:, :, 1, :], u[:, 2:4, :].rearrange("p j (a t) -> p (j a) t", t=P), w4[0], ALU.mult))
                link(dve.tensor_tensor(aa[:, :, :], kk0[:, :, :], aa[:, :, :], ALU.mult))
                link(dve.tensor_tensor(ch4["b"][:, :, :], aa[:, :, :].rearrange("p j (a t) -> p (j a) t", t=P), w4[1], ALU.mult))
                link(dve.tensor_tensor(ch4["k"][:, :, :], km[:, :, :].rearrange("p j (a t) -> p (j a) t", t=P), w4[1], ALU.mult))
                ends = Wc[:, :, :].rearrange("p j (c t) -> p (j c) t", t=CH)[:, :, CH - 1:CH].broadcast_to([P, 2 * NCH, CH])
                for n, k in enumerate("bk"):
                    ins = dve.tensor_tensor(ch4[k.upper()][:, :, :].rearrange("p a (c t) -> p (a c) t", t=CH),
                                            ch4[k][:, :, :].rearrange("p a (c t) -> p (a c) t", t=CH), ends, ALU.mult)
                    if n == 0:
                        link(ins)
                    else:
                        ins.then_inc(prepared, 1)
                        dve.wait_ge(prepared, it + 1)

            def core(it):
                par = it % 2
                below2 = below[:, :].unsqueeze(1).broadcast_to([P, 2, P])
                upto2 = upto[:, :].unsqueeze(1).broadcast_to([P, 2, P])
                for kind, strict, incl in (("B", "N", "Mrb"), ("K", "Lak", "Mrk")):
                    for hh in range(2):
                        for uu in range(2):
                            name = ("L" + kind, it, hh, uu)
                            await_filled(dve, name)
                            i0 = 4 * hh + 2 * uu
                            link(dve.tensor_tensor(mats[strict][:, i0:i0 + 2, :], view(name, 2, 2, P)[:, :, 0, :], below2, ALU.mult))
                            drains(dve.tensor_tensor(mats[incl][:, i0:i0 + 2, :], view(name, 2, 2, P)[:, :, 1, :], upto2,
                                                     ALU.mult), name)
                dve.wait_ge(eye_ready, 2 * (it + 1))
                for hh in range(2):
                    name = ("LL", it, hh)
                    await_filled(dve, name)
                    m4 = [m[:, 0, :].unsqueeze(1).broadcast_to([P, 4, P]) for m in (low8, up8)]
                    link(dve.copy_predicated(mats["G"][:, 4 * hh:4 * hh + 4, :], m4[1], mats["N"][:, 4 * hh:4 * hh + 4, :]))
                    drains(dve.copy_predicated(mats["T"][:, 4 * hh:4 * hh + 4, :], m4[0], view(name, 4, P)), name)
                for n, lev in enumerate(LEVELS[1:]):
                    for g in range(4):
                        name = ("TG", it, lev, g)
                        await_filled(dve, name)
                        m2 = [m[:, n + 1, :].unsqueeze(1).broadcast_to([P, 2, P]) for m in (low8, up8)]
                        if n + 1 < len(LEVELS) - 1:
                            link(dve.copy_predicated(mats["T"][:, 2 * g:2 * g + 2, :], m2[0], view(name, 4, P)[:, 0:2, :]))
                        drains(dve.copy_predicated(mats["G"][:, 2 * g:2 * g + 2, :], m2[1], view(name, 4, P)[:, 2:4, :]), name)
                await_drained(dve, ("Q", it))
                Q4 = Qs[:, :, :].rearrange("p (j a) i -> p j a i", a=NT)
                U4 = Us[:, :, :].rearrange("p (j a) i -> p j a i", a=NT)
                for c in range(NCH):
                    tt, h = c // 2, slice(CH * (c % 2), CH * (c % 2) + CH)
                    if c == 0:
                        dve.tensor_copy(U4[h, :, tt, :], Q4[h, :, tt, :]).then_inc(u0_ready, 1)
                        dve.wait_ge(u0_ready, it + 1)
                    else:
                        name = ("U", it, c)
                        await_filled(dve, name)
                        drains(dve.tensor_tensor(U4[h, :, tt, :], view(name, 2, P)[h], Q4[h, :, tt, :], ALU.add), name)
                    if c == NCH - 1:
                        break
                    name = ("S", it, c)
                    await_filled(dve, name)
                    for n in range(4):
                        j, hh = n // 2, n % 2
                        r = slice(HN * hh, HN * hh + HN)
                        src = view(name, 2, P)[r, j, HN * hh:HN * hh + HN]
                        dst = Ss[r, c, j, HN * hh:HN * hh + HN]
                        if c == 0:
                            ins = dve.tensor_copy(dst, src)
                        else:
                            ins = dve.scalar_tensor_tensor(
                                out=dst, in0=Ss[r, c - 1, j, HN * hh:HN * hh + HN],
                                scalar=Wc[r, j, CH * c + CH - 1:CH * c + CH], in1=src, op0=ALU.mult, op1=ALU.add)
                        if n < 3:
                            link(ins)
                        else:
                            drains(ins, name)
                await_drained(dve, ("y", it))
                name = ("mean", it)
                await_filled(dve, name)
                drains(dve.scalar_tensor_tensor(out=ys[:, :, :], in0=view(name, 2, T), scalar=-1.0 / HN, in1=ys[:, :, :],
                                                op0=ALU.mult, op1=ALU.add), name)
                dve.tensor_tensor(dsh[:, 2:4, :], ys[:, :, :], ys[:, :, :], ALU.mult).then_inc(ysq_ready, 1)
                dve.wait_ge(ysq_ready, it + 1)
                await_drained(dve, ("var", it))
                link(dve.reciprocal(dsh[:, 0:2, :], dsh[:, 0:2, :]))
                link(dve.tensor_tensor(ys[:, :, :], ys[:, :, :], dsh[:, 0:2, :], ALU.mult))
                for j in range(2):
                    link(dve.tensor_scalar(ys[:, j, :], ys[:, j, :], col(R_LNW + 2 * it + j), col(R_LNB + 2 * it + j),
                                           ALU.mult, ALU.add))
                link(dve.tensor_tensor(ys[:, :, :], ys[:, :, :], bon[:, :, :], ALU.add))
                dve.tensor_tensor(yB[:, 2 * it:2 * it + 2, :], ys[:, :, :], gg[:, par, :, :], ALU.mult).then_inc(yB_ready, 1)
                dve.wait_ge(yB_ready, it + 1)

            def gla(it):
                par = it % 2
                await_drained(dve, ("gl", it))
                dve.wait_ge(softplus_ready, it + 1)
                link(dve.scalar_tensor_tensor(out=gtmp[2], in0=gx[:, par, :], scalar=0.0, in1=gtmp[1],
                                              op0=ALU.min, op1=ALU.subtract))
                link(dve.tensor_tensor_scan(dsh[:, 3, :], chunkmask[:, 0:T], gtmp[2], 0.0, ALU.mult, ALU.add))
                b4 = dsh[:, 3, :].rearrange("p (c t) -> p c t", t=CH)
                link(dve.tensor_tensor(dsh[:, 2, :].rearrange("p (c t) -> p c t", t=CH), b4,
                                       b4[:, :, CH // 2:CH // 2 + 1].broadcast_to([P, NCH, CH]), ALU.subtract))
                dve.tensor_tensor(dsh[:, 4, :].rearrange("p (c t) -> p c t", t=CH),
                                  b4[:, :, CH - 1:CH].broadcast_to([P, NCH, CH]), b4, ALU.subtract).then_inc(b_ready, 1)
                dve.wait_ge(gexp_ready, 5 * (it + 1))
                link(dve.tensor_tensor(gprod[0], gq[:, par, :], gtmp[0], ALU.mult))
                link(dve.tensor_tensor(gprod[1], gk[:, par, :], gtmp[1], ALU.mult))
                link(dve.tensor_tensor(gprod[2], gq[:, par, :], gtmp[2], ALU.mult))
                dve.tensor_tensor(gprod[3], gk[:, par, :], gtmp[3], ALU.mult).then_inc(gprep_ready, 1)
                dve.wait_ge(gprep_ready, it + 1)
                link(dve.tensor_tensor(og[:, par, :, :], og[:, par, :, :], dsh[:, 0:2, :], ALU.mult))
                link(dve.memset(gsT[:, :, :], 0.0))
                name = ("gs", it)
                await_filled(dve, name)
                drains(dve.copy_predicated(gsT[:, :, :], upto8[:, :].unsqueeze(1).broadcast_to([P, NT, P]), view(name, 2, P)), name)
                for c in range(NCH - 1):
                    name = ("gS", it, c)
                    await_filled(dve, name)
                    if c == 0:
                        drains(dve.tensor_copy(gSt[:, 1, :], view(name, T)), name)
                    else:
                        drains(dve.scalar_tensor_tensor(out=gSt[:, c + 1, :], in0=gSt[:, c, :],
                                                        scalar=gtmp[2][:, CH * c + CH - 1:CH * c + CH], in1=view(name, T),
                                                        op0=ALU.mult, op1=ALU.add), name)
                await_drained(dve, ("gn", it))
                link(dve.reciprocal(dsh[:, 4, :], dsh[:, 4, :]))
                name = ("go", it)
                await_filled(dve, name)
                drains(dve.tensor_tensor(dsh[:, 2:4, :], view(name, 2, T), dsh[:, 4:5, :].broadcast_to([P, 2, T]), ALU.mult), name)
                for j in range(2):
                    ins = dve.scalar_tensor_tensor(out=yA[:, 2 * it + j, :], in0=dsh[:, 2 + j, :], scalar=col(R_NG + j),
                                                   in1=og[:, par, j, :], op0=ALU.mult, op1=ALU.mult)
                    if j == 0:
                        link(ins)
                    else:
                        ins.then_inc(yA_ready, 1)
                        dve.wait_ge(yA_ready, it + 1)

            first_half(0)
            second_half(0)
            for it in range(ITERS):
                if it + 1 < ITERS:
                    first_half(it + 1)
                core(it)
                gla(it)
                if it + 1 < ITERS:
                    second_half(it + 1)

            for m in range(KD):
                await_filled(dve, ("ba", m))
                drains(dve.tensor_tensor(gates[:, m, :], gates[:, m, :], view(("ba", m), T), ALU.mult), ("ba", m))
                await_filled(dve, ("bb", m))
                drains(dve.tensor_tensor(gates[:, KD + m, :], gates[:, KD + m, :], view(("bb", m), T), ALU.mult), ("bb", m))
                dve.tensor_tensor(gates[:, m, :], gates[:, m, :], gates[:, KD + m, :], ALU.add).then_inc(merged_ready, 1)
            for m in range(4):
                for tt in range(NT):
                    name = ("out", m, tt)
                    await_filled(dve, name)
                    drains(dve.tensor_tensor(xs[:, tt, 256 * m:256 * m + 256], xs[:, tt, 256 * m:256 * m + 256], view(name, T),
                                             ALU.add), name)
            dve.sem_inc(x1_ready, 1)

            dve.wait_ge(sumsq_ready, 6)
            link(dve.reciprocal(stat[:, 8:10], stat[:, 8:10]))
            dve.wait_ge(late_in, 6 * 16)
            for tt in range(NT):
                dve.scalar_tensor_tensor(out=h2[:, tt, :], in0=xs[:, tt, :], scalar=stat[:, 8 + tt:9 + tt], in1=ffn_g[:, :],
                                         op0=ALU.mult, op1=ALU.mult).then_inc(h2_ready, 1)
            for c in range(4):
                name = ("h2T", c)
                await_filled(dve, name)
                drains(dve.tensor_copy(h2T[:, 2 * c:2 * c + 2, :], view(name, 2, T)), name)
            name = ("log",)
            await_filled(dve, name)
            drains(dve.tensor_tensor(lg[:, :, :], view(name, NT, E), rb[:, :].unsqueeze(1).broadcast_to([P, NT, E]), ALU.add), name)
            for tt in range(NT):
                link(dve.max(top[:, tt, :], lg[:, tt, :]))
            dve.tensor_scalar(rs[:, 0:2].unsqueeze(2), top[:, :, 0:1], -1.0, None, ALU.mult).then_inc(lmax_ready, 1)
            for tt in range(NT):
                fourth = top[:, tt, TOPK - 1:TOPK]
                link(dve.tensor_scalar(rt[:, 0, tt, :], lg[:, tt, :], fourth, 0.0, ALU.is_gt, ALU.add))
                link(dve.tensor_scalar(rt[:, 1, tt, :], lg[:, tt, :], fourth, None, ALU.is_equal))
                link(dve.tensor_reduce(rs[:, 2 + tt:3 + tt], rt[:, 0, tt, :], AX_X, ALU.add))
                link(dve.tensor_tensor_scan(rt[:, 2, tt, :], rt[:, 1, tt, :], rt[:, 1, tt, :], 0.0, ALU.bypass, ALU.add)
                     if False else dve.tensor_tensor_scan(rt[:, 2, tt, :], ones[:, 0:E], rt[:, 1, tt, :], 0.0, ALU.mult, ALU.add))
                link(dve.tensor_scalar(rt[:, 2, tt, :], rt[:, 2, tt, :], rs[:, 2 + tt:3 + tt], float(TOPK), ALU.add, ALU.is_le))
                link(dve.tensor_tensor(rt[:, 2, tt, :], rt[:, 2, tt, :], rt[:, 1, tt, :], ALU.mult))
                link(dve.tensor_tensor(selM[:, tt, :], rt[:, 2, tt, :], rt[:, 0, tt, :], ALU.add))
            dve.sem_inc(mask_sel, 1)
            dve.wait_ge(gexpo, 2)
            link(dve.tensor_tensor(rt[:, 4, :, :], rt[:, 4, :, :], selM[:, :, :], ALU.mult))
            link(dve.tensor_reduce(rs[:, 4:6], rt[:, 4, :, :], AX_X, ALU.add))
            link(dve.reciprocal(rs[:, 6:8], rs[:, 4:6]))
            for tt in range(NT):
                link(dve.tensor_scalar(rt[:, 5, tt, :], rt[:, 4, tt, :], rs[:, 6 + tt:7 + tt], None, ALU.mult))
            dve.tensor_copy(gatev[:, :, :].rearrange("p e a -> p a e"), rt[:, 5, :, :]).then_inc(gatev_ready, 1)
            name = ("pos",)
            await_filled(dve, name)
            drains(dve.scalar_tensor_tensor(out=rt[:, 0, :, :], in0=selM[:, :, :], scalar=-4096.0, in1=view(name, NT, E),
                                            op0=ALU.mult, op1=ALU.add), name)
            link(dve.tensor_scalar(posm[:, :, :].rearrange("p e a -> p a e"), rt[:, 0, :, :], 4096.0, None, ALU.add))
            name = ("cnt",)
            await_filled(dve, name)
            drains(dve.tensor_reduce(rs[:, 8:9], view(name, E), AX_X, ALU.max), name)
            dve.tensor_copy(over[:, :], rs[:, 8:9]).then_inc(route_ready, 1)
            name = ("gT",)
            await_filled(dve, name)
            drains(dve.tensor_copy(gT[:, :], view(name, T)[0:E, :]), name)
            for n in range(4):
                name = ("b2", n)
                await_filled(dve, name)
                drains(dve.tensor_tensor(acc[:, n // 2, 512 * (n % 2):512 * (n % 2) + 512],
                                         acc[:, n // 2, 512 * (n % 2):512 * (n % 2) + 512], view(name, 512), ALU.add), name)

            def choose(i):
                if isinstance(i, int):
                    e, s0 = i, 0
                else:
                    e, s0 = i % E, (i // E) * SLOTS
                wait_after(dve, gather_done, i)
                dve.tensor_tensor(sel[:, :, :], iota[:, bass.ds(s0, SLOTS)].unsqueeze(1).broadcast_to([P, NT, SLOTS]),
                                  posm[:, bass.ds(e, 1), :].rearrange("p a b -> p (a b)").unsqueeze(2).broadcast_to([P, NT, SLOTS]),
                                  ALU.is_equal).then_inc(sel_ready, 1)
                dve.wait_ge(sel_ready, i + 1)
                gt = gatev[:, bass.ds(e, 1), :].rearrange("p a b -> p (a b)").unsqueeze(2).broadcast_to([P, NT, SLOTS])
                wait_after(dve, selT_done, i)
                dve.tensor_tensor(selg[:, :, 0, :], sel[:, :, :], gt, ALU.mult).then_inc(selg_ready, 1)
                dve.tensor_tensor(selg[:, :, 1, :], sel[:, :, :], gt, ALU.mult).then_inc(selg_ready, 1)

            def point(i):
                e = i if isinstance(i, int) else i % E
                wait_after(dve, hid_done, i)
                dve.tensor_scalar(ehot[:, :], onesE[:, :], ident[0:E, bass.ds(e, 1)], None, ALU.mult).then_inc(ehot_ready, 1)

            def turn(i):
                dve.wait_ge(selT_done, i + 1)
                wait_after(dve, y_done, 2 * i)
                dve.tensor_copy(selgT[:, :, :], banks[3][:, 0:T].rearrange("p (a t) -> p a t", a=NT)).then_inc(selgT_ready, 1)

            def expert(i):
                hid = [banks[1 + q][:, :].rearrange("p (m two) -> p m two", two=2) for q in range(2)]
                point(i + 1)
                wait_after(dve, act_ready, i)
                for q in range(2):
                    dve.tensor_scalar(glu[:, q, :], hid[q][:, :, 0], 7.0, None, ALU.min).then_inc(glu_half, 1) if q == 0 else \
                        dve.tensor_scalar(glu[:, q, :], hid[q][:, :, 0], 7.0, None, ALU.min).then_inc(glu_ready, 1)
                for q in range(2):
                    dve.tensor_scalar(lin[:, q, :], hid[q][:, :, 1], 7.0, -7.0, ALU.min, ALU.max).then_inc(lin_ready, 1)
                dve.wait_ge(glu_ready, i + 1)
                dve.wait_ge(lin_ready, i * 2 + 2)
                dve.scalar_tensor_tensor(out=lin[:, :, :], in0=lin[:, :, :], scalar=1.0, in1=glu[:, :, :], op0=ALU.add,
                                         op1=ALU.mult).then_inc(gated_ready, 1)
                dve.wait_ge(gated_ready, i + 1)
                dve.wait_ge(sgm_ready, i + 1)
                wait_after(dve, actT_done, i)
                dve.tensor_tensor(act_s[:, :, :], lin[:, :, :], sgm[:, :, :], ALU.mult).then_inc(act_ready, 1)
                choose(i + 2)
                for n in range(2):
                    dve.wait_ge(y_done, i * 2 + (n + 1))
                    for h in range(2):
                        wait_after(dve, y_added, i * 4 + (2 * n + h))
                        dve.tensor_tensor(acc[:, n, 512 * h:512 * h + 512], acc[:, n, 512 * h:512 * h + 512],
                                          banks[6 + h][:, :], ALU.add).then_inc(y_added, 1)
                turn(i + 1)

            dve.wait_ge(moe_pool, 2)
            choose(0)
            turn(0)
            point(0)
            choose(1)
            expert(0)
            with dve.Fori(1, E) as i:
                expert(i)
            dve.wait_ge(route_ready, 1)
            most = dve.value_load(over[0:1, 0:1], min_val=0, max_val=T)
            with dve.If(most > SLOTS):
                with dve.Fori(E, PASSES * E) as i:
                    expert(i)
            dve.wait_ge(y_added, 4 * E)
            dve.sem_inc(mask_sel, 2)
            dve.wait_ge(sumsq_ready, 9)
            link(dve.reciprocal(stat[:, 14:16], stat[:, 12:14]))
            fin = h2T[:, :, :].rearrange("p a b -> p (a b)").rearrange("p (a d) -> p a d", a=NT)
            for tt in range(NT):
                link(dve.scalar_tensor_tensor(out=fin[:, tt, :], in0=xs[:, tt, :], scalar=stat[:, 14 + tt:15 + tt],
                                              in1=final_g[:, :], op0=ALU.mult, op1=ALU.mult))
            dve.sem_inc(final_ready, 1)

        @block.tensor
        def _(pe):
            at = [0]

            def begin(name):
                assert order[at[0]] == name, (order[at[0]], name)
                at[0] += 1
                if nth_of[name]:
                    pe.wait_ge(drained[bank_of[name]], nth_of[name])

            def end(ins, name):
                ins.then_inc(filled[bank_of[name]], 1)

            pe.wait_ge(rows_in, 11 * 16)
            pe.wait_ge(consts_ready, 1)
            begin(("par",))
            end(pe.transpose(view(("par",), NROWS), prow[0:NROWS, :], ident[0:NROWS, 0:NROWS]), ("par",))
            xn = yA[:, :, :].rearrange("p a b -> p (a b)").rearrange("p (a d) -> p a d", a=NT)
            pe.wait_ge(xn_ready, 2)
            for c in range(KD // 2):
                name = ("hT", c)
                begin(name)
                for k in range(2):
                    for tt in range(NT):
                        d0 = P * (2 * c + k)
                        last = pe.transpose(view(name, 2, NT, P)[:, k, tt, :], xn[:, tt, d0:d0 + P], ident[:, :])
                end(last, name)
            await_drained(pe, ("hT", KD // 2 - 1))

            def weights(kind, it):
                n = block_index[(kind, it)]
                pe.wait_ge(w_in_ready[n % WRING], ring_count[n])
                return wslot(kind, it)

            def tile(name, w, j, token_major, more=None):
                begin(name)
                for k in range(KD):
                    if token_major:
                        last = pe.matmul(view(name, T), hT[:, k, P * j:P * j + P], w[:, k, :], start=(k == 0), stop=(k == KD - 1))
                    elif name[1] == "lr":
                        last = pe.matmul(view(name, T)[0:RANK, :], w[:, k, 0:RANK], hT[:, k, :], start=(k == 0), stop=(k == KD - 1))
                    else:
                        last = pe.matmul(view(name, T), w[:, k, P * j:P * j + P], hT[:, k, :], start=(k == 0), stop=(k == KD - 1))
                end(last, name)

            used = [0]

            def release(name):
                await_filled(pe, name)
                pe.sem_inc(w_used, 1)

            def project(it):
                if it == 0:
                    w = weights("lora", 0)
                    for j in range(2):
                        tile(("z", "lora", 0, j), w, j, False)
                    release(("z", "lora", 0, 1))
                    tile(("z", "lr", 0, 0), weights("lr", 0), 0, False)
                    release(("z", "lr", 0, 0))
                for kind in ROUND:
                    w = weights(kind, it)
                    for j in range(2):
                        tile(("z", kind, it, j), w, j, kind == "gv")
                    release(("z", kind, it, 1))
                if it == 0:
                    pe.wait_ge(lora_in, 4 * 16)
                    pe.wait_ge(lora_act, 2)
                for key in ("lw", "la", "lg"):
                    name = (key, it)
                    begin(name)
                    for j in range(2):
                        c0 = P * (2 * it + j)
                        if key == "lg":
                            last = pe.matmul(view(name, 2, T)[:, j, :], g2[:, c0:c0 + P], ul[:, 1, :], start=True, stop=True)
                        else:
                            r = slice(0, 64) if key == "lw" else slice(64, 128)
                            last = pe.matmul(view(name, 2, T)[:, j, :], w2a2[r, c0:c0 + P], ul[r, 0, :], start=True, stop=True)
                    end(last, name)
                name = ("gl", it)
                begin(name)
                await_drained(pe, ("z", "lr", 0, 0))
                end(pe.matmul(view(name, T), gup[:, P * it:P * it + P], zlr[:, :], start=True, stop=True), name)

            def norms(it):
                name = ("kn", it)
                begin(name)
                pe.wait_ge(ksq_ready, it + 1)
                end(pe.matmul(view(name, 512), headones[:, :], sq[:, :, :], start=True, stop=True), name)
                name = ("bo", it)
                begin(name)
                pe.wait_ge(bprod_ready, it + 1)
                end(pe.matmul(view(name, 512), headones[:, :], bp[:, :, :], start=True, stop=True), name)

            def core(it):
                par = it % 2
                pe.wait_ge(prepared, it + 1)
                for kind in "ABKV":
                    name = ("tr", it, kind)
                    begin(name)
                    for jt in range(4):
                        src = {"A": AR[:, jt, 0, :], "B": ch4["B"][:, jt, :], "K": ch4["K"][:, jt, :],
                               "V": uv[:, par, jt // 2, P * (jt % 2):P * (jt % 2) + P]}[kind]
                        last = pe.transpose(view(name, 4, P)[:, jt, :], src, ident[:, :])
                    end(last, name)
                for kind in "BK":
                    for hh in range(2):
                        r = slice(HN * hh, HN * hh + HN)
                        for uu in range(2):
                            name = ("L" + kind, it, hh, uu)
                            begin(name)
                            for n in range(2):
                                jt = 2 * uu + n
                                last = pe.matmul(view(name, 2, 2 * P)[:, n, :], ch4[kind.lower()][r, jt, :],
                                                 AR[r, jt, :, :], start=True, stop=True)
                            end(last, name)
                for hh in range(2):
                    r = slice(HN * hh, HN * hh + HN)
                    name = ("LL", it, hh)
                    begin(name)
                    for jt in range(4):
                        last = pe.matmul(view(name, 4, P)[:, jt, :], AR[r, jt, 0, :], ch4["b"][r, jt, :], start=True, stop=True)
                    end(last, name)

                def items(hh_first=False):
                    return [(hh, jt, 4 * hh + jt) for hh in range(2) for jt in range(4)]

                name = ("X", it)
                begin(name)
                await_drained(pe, ("LK", it, 1, 1))
                await_drained(pe, ("tr", it, "V"))
                for hh, jt, i in items():
                    c = slice(HN * hh, HN * hh + HN)
                    last = pe.matmul(view(name, 4, P)[:, jt, c], mats["Lak"][:, i, :], tm["V"][:, jt, c], start=True, stop=True)
                end(last, name)
                before_lev = None
                for lev in LEVELS[1:]:
                    for g in range(4):
                        name = ("Z", it, lev, g)
                        begin(name)
                        if before_lev is None:
                            await_drained(pe, ("LL", it, g // 2))
                        else:
                            await_drained(pe, ("TG", it, before_lev, g))
                        for n in range(2):
                            last = pe.matmul(view(name, 2, P)[:, n, :], mats["N"][:, 2 * g + n, :], mats["T"][:, 2 * g + n, :],
                                             start=True, stop=True)
                        end(last, name)
                    for g in range(4):
                        name = ("TG", it, lev, g)
                        begin(name)
                        await_drained(pe, ("Z", it, lev, g))
                        for n in range(2):
                            Gm, Zm = mats["G"][:, 2 * g + n, :], mats["Z"][:, 2 * g + n, :]
                            if lev != LEVELS[-1]:
                                pe.matmul(view(name, 4, P)[:, n, :], Gm, Zm, start=True, stop=True)
                            last = pe.matmul(view(name, 4, P)[:, 2 + n, :], Zm, Gm, start=True, stop=True)
                        end(last, name)
                    before_lev = lev
                name = ("Q", it)
                begin(name)
                for g in range(4):
                    await_drained(pe, ("TG", it, LEVELS[-1], g))
                await_drained(pe, ("X", it))
                for hh, jt, i in items():
                    c = slice(HN * hh, HN * hh + HN)
                    last = pe.matmul(view(name, 4, P)[:, jt, c], mats["G"][:, i, :], Xs[:, jt, c], start=True, stop=True)
                end(last, name)
                name = ("PT", it)
                begin(name)
                await_drained(pe, ("tr", it, "A"))
                for hh, jt, i in items():
                    c = slice(HN * hh, HN * hh + HN)
                    last = pe.matmul(view(name, 4, P)[c, jt, :], tm["A"][:, jt, c], mats["G"][:, i, :], start=True, stop=True)
                end(last, name)
                for c in range(NCH):
                    tt, h = c // 2, slice(CH * (c % 2), CH * (c % 2) + CH)
                    if c:
                        name = ("U", it, c)
                        begin(name)
                        await_drained(pe, ("PT", it))
                        await_drained(pe, ("S", it, c - 1))
                        for j in range(2):
                            last = pe.matmul(view(name, 2, P)[h, j, :], PTs[:, 2 * j + tt, h], Ss[:, c - 1, j, :], start=True, stop=True)
                        end(last, name)
                        await_drained_u = ("U", it, c)
                    if c == NCH - 1:
                        break
                    name = ("S", it, c)
                    begin(name)
                    if c == 0:
                        pe.wait_ge(u0_ready, it + 1)
                    else:
                        await_drained(pe, await_drained_u)
                    for j in range(2):
                        o = view(name, 2, P)[:, j, :]
                        pe.matmul(o, tm["K"][h, 2 * j + tt, :], tm["V"][h, 2 * j + tt, :], start=True, stop=False)
                        last = pe.matmul(o, tm["B"][h, 2 * j + tt, :], Us[h, 2 * j + tt, :], start=False, stop=True)
                    end(last, name)
                name = ("y", it)
                begin(name)
                await_drained(pe, ("U", it, NCH - 1))
                for jt in range(4):
                    j, tt = jt // 2, jt % 2
                    for hh in range(2):
                        c = slice(HN * hh, HN * hh + HN)
                        pe.matmul(view(name, 4, P)[c, jt, :], tm["V"][:, jt, c], mats["Mrk"][:, 4 * hh + jt, :],
                                  start=True, stop=False, skip_group_check=True)
                    for c in range(max(1, 2 * tt), 2 * tt + 2):
                        h = slice(CH * (c % 2), CH * (c % 2) + CH)
                        pe.matmul(view(name, 4, P)[:, jt, h], Ss[:, c - 1, j, :], AR[:, jt, 1, h], start=False, stop=False,
                                  skip_group_check=True)
                    for hh in range(2):
                        c = slice(HN * hh, HN * hh + HN)
                        last = pe.matmul(view(name, 4, P)[c, jt, :], Us[:, jt, c], mats["Mrb"][:, 4 * hh + jt, :],
                                         start=False, stop=True, skip_group_check=True)
                end(last, name)
                name = ("mean", it)
                begin(name)
                await_drained(pe, ("y", it))
                end(pe.matmul(view(name, 512), headones[:, :], ys[:, :, :], start=True, stop=True), name)
                name = ("var", it)
                begin(name)
                pe.wait_ge(ysq_ready, it + 1)
                end(pe.matmul(view(name, 512), headones[:, :], dsh[:, 2:4, :], start=True, stop=True), name)

            def gla(it):
                par = it % 2
                name = ("gs", it)
                begin(name)
                pe.wait_ge(gprep_ready, it + 1)
                for tt in range(NT):
                    c = slice(P * tt, P * tt + P)
                    last = pe.matmul(view(name, 2, P)[:, tt, :], gprod[1][:, c], gprod[0][:, c], start=True, stop=True)
                end(last, name)
                name = ("gk", it)
                begin(name)
                for tt in range(NT):
                    last = pe.transpose(view(name, 2, P)[:, tt, :], gprod[3][:, P * tt:P * tt + P], ident[:, :])
                end(last, name)
                for c in range(NCH - 1):
                    tt, h = c // 2, slice(CH * (c % 2), CH * (c % 2) + CH)
                    name = ("gS", it, c)
                    begin(name)
                    await_drained(pe, ("gk", it))
                    end(pe.matmul(view(name, T), gkt[h, tt, :], gv[h, par, tt, :], start=True, stop=True), name)
                name = ("go", it)
                begin(name)
                await_drained(pe, ("gs", it))
                await_drained(pe, ("gS", it, NCH - 2))
                for dv in range(2):
                    for tt in range(NT):
                        o = view(name, 2, T)[:, dv, P * tt:P * tt + P]
                        last = pe.matmul(o, gv[:, par, tt, P * dv:P * dv + P], gsT[:, tt, :], start=True, stop=False,
                                         skip_group_check=True)
                        for c in range(max(1, 2 * tt), 2 * tt + 2):
                            last = pe.matmul(view(name, 2, T)[:, dv, CH * c:CH * c + CH], gSt[:, c, P * dv:P * dv + P],
                                             gprod[2][:, CH * c:CH * c + CH], start=False, stop=True, skip_group_check=True)
                end(last, name)
                name = ("gn", it)
                begin(name)
                pe.wait_ge(gsq_ready, it + 1)
                for dv in range(2):
                    last = pe.matmul(view(name, T), ones[:, :], dsh[:, 2 + dv, :], start=(dv == 0), stop=(dv == 1))
                end(last, name)

            project(0)
            norms(0)
            for it in range(ITERS):
                if it + 1 < ITERS:
                    project(it + 1)
                core(it)
                gla(it)
                if it + 1 < ITERS:
                    norms(it + 1)
            pe.wait_ge(yA_ready, ITERS)
            pe.wait_ge(yB_ready, ITERS)
            for m in range(KD):
                for key, kind, src in (("ba", "wa", yA), ("bb", "wb", yB)):
                    w = weights(kind, m // 2)
                    name = (key, m)
                    begin(name)
                    for k in range(KD):
                        last = pe.matmul(view(name, T), w[:, k, P * (m % 2):P * (m % 2) + P], src[:, k, :],
                                         start=(k == 0), stop=(k == KD - 1))
                    end(last, name)
                if m % 2:
                    release(("ba", m))
                    release(("bb", m))
            pe.wait_ge(merged_ready, KD)
            for m in range(4):
                w = weights("wo", m)
                for tt in range(NT):
                    name = ("out", m, tt)
                    begin(name)
                    for k in range(KD):
                        last = pe.matmul(view(name, T), gates[:, k, P * tt:P * tt + P], w[:, k, :],
                                         start=(k == 0), stop=(k == KD - 1))
                    end(last, name)
                release(("out", m, 1))

            pe.wait_ge(h2_ready, 2)
            for c in range(4):
                name = ("h2T", c)
                begin(name)
                for k in range(2):
                    for tt in range(NT):
                        d0 = P * (2 * c + k)
                        last = pe.transpose(view(name, 2, NT, P)[:, k, tt, :], h2[:, tt, d0:d0 + P], ident[:, :])
                end(last, name)
            name = ("log",)
            begin(name)
            for c in range(4):
                await_drained(pe, ("h2T", c))
            for tt in range(NT):
                for k in range(KD):
                    last = pe.matmul(view(name, NT, E)[:, tt, :], h2T[:, k, P * tt:P * tt + P], rw[:, k, :],
                                     start=(k == 0), stop=(k == KD - 1))
            end(last, name)
            pe.wait_ge(mask_sel, 1)
            name = ("pos",)
            begin(name)
            pe.matmul(view(name, NT, E)[:, 0, :], before[:, :], selM[:, 0, :], start=True, stop=True)
            pe.matmul(view(name, NT, E)[:, 1, :], ones[:, :], selM[:, 0, :], start=True, stop=False)
            end(pe.matmul(view(name, NT, E)[:, 1, :], before[:, :], selM[:, 1, :], start=False, stop=True), name)
            name = ("cnt",)
            begin(name)
            pe.matmul(view(name, E), ones[:, :], selM[:, 0, :], start=True, stop=False)
            end(pe.matmul(view(name, E), ones[:, :], selM[:, 1, :], start=False, stop=True), name)
            name = ("gT",)
            begin(name)
            pe.wait_ge(gatev_ready, 1)
            for tt in range(NT):
                last = pe.transpose(view(name, T)[0:E, P * tt:P * tt + P], rt[:, 5, tt, :], ident[:, :])
            end(last, name)
            pe.wait_ge(late_in, 6 * 16)
            for n in range(4):
                name = ("b2", n)
                begin(name)
                await_drained(pe, ("gT",))
                end(pe.matmul(view(name, 512), gT[:, P * (n // 2):P * (n // 2) + P], b2s[:, 512 * (n % 2):512 * (n % 2) + 512],
                              start=True, stop=True), name)
            for b in range(8):
                pe.wait_ge(drained[b], fills[b])

            def gather(i):
                pe.wait_ge(sel_ready, i + 1)
                wait_after(pe, xg_ready, i)
                o = banks[0][:, :].rearrange("p (k s) -> p k s", k=KD)
                for k in range(KD):
                    for tt in range(NT):
                        last = pe.matmul(o[:, k, :], h2[:, tt, P * k:P * k + P], sel[:, tt, :], start=(tt == 0), stop=(tt == NT - 1))
                last.then_inc(gather_done, 1)
                pe.wait_ge(selg_ready, i * 2 + 2)
                wait_after(pe, selgT_ready, i)
                for tt in range(NT):
                    last = pe.transpose(banks[3][:, P * tt:P * tt + P], selg[:, tt, :, :].rearrange("p a b -> p (a b)"), ident[:, :])
                last.then_inc(selT_done, 1)

            def expert(i):
                wait_after(pe, lin_ready, i * 2)
                pe.wait_ge(xg_ready, i + 1)
                pe.wait_ge(ehot_ready, i + 1)
                for j in range(4):
                    pe.matmul(banks[1 + j // 2][64 * (j % 2):64 * (j % 2) + 64, :], ehot[:, :], b1s[:, 512 * j:512 * j + 512],
                              start=True, stop=False)
                for k in range(KD):
                    pe.wait_ge(w1_in[k], i * 16 + 16)
                    for j in range(4):
                        last = pe.matmul(banks[1 + j // 2][64 * (j % 2):64 * (j % 2) + 64, :], xg[:, k, :],
                                         w1s[:, k, 512 * j:512 * j + 512], start=False, stop=(k == KD - 1))
                    if k < KD - 1:
                        last.then_inc(w1_used, 1)
                    else:
                        last.then_inc(hid_done, 1)
                        pe.wait_ge(hid_done, i + 1)
                        pe.sem_inc(w1_used, 1)
                gather(i + 1)
                pe.wait_ge(act_ready, i + 1)
                wait_after(pe, actT_ready, i)
                for q in range(2):
                    for b in range(2):
                        n = 2 * q + b
                        last = pe.transpose(banks[4][:, P * n:P * n + P], act_s[:, q, P * b:P * b + P], ident[:, :])
                last.then_inc(actT_done, 1)
                pe.wait_ge(actT_ready, i + 1)
                wait_after(pe, eo_ready, i)
                for f in range(FF // P):
                    q, half, b = f // 4, f // 2 % 2, f % 2
                    if f % 2 == 0:
                        pe.wait_ge(w2_in[f // 2], i * 16 + 16)
                    for dh in range(2):
                        last = pe.matmul(banks[5][64 * dh:64 * dh + 64, :], actT[:, 2 * q + b, 64 * half:64 * half + 64],
                                         w2s[:, f, 512 * dh:512 * dh + 512], start=(f == 0), stop=(f == FF // P - 1))
                    if f % 2:
                        if f < FF // P - 1:
                            last.then_inc(w2_used, 1)
                        else:
                            last.then_inc(eo_done, 1)
                            pe.wait_ge(eo_done, i + 1)
                            pe.sem_inc(w2_used, 1)
                pe.wait_ge(eo_ready, i + 1)
                pe.wait_ge(selgT_ready, i + 1)
                for tt in range(NT):
                    wait_after(pe, y_added, i * 4 + 2 * tt)
                    for dh in range(2):
                        r = slice(64 * dh, 64 * dh + 64)
                        last = pe.matmul(banks[6 + dh][:, :], selgT[r, tt, :], eo[r, :], start=True, stop=True)
                    last.then_inc(y_done, 1)

            gather(0)
            expert(0)
            with pe.Fori(1, E) as i:
                expert(i)
            pe.wait_ge(route_ready, 1)
            most = pe.value_load(over[0:1, 0:1], min_val=0, max_val=T)
            with pe.If(most > SLOTS):
                with pe.Fori(E, PASSES * E) as i:
                    expert(i)


_INS = ['x', 'norm_mix_g', 'w_in', 'gla_gate_up', 'gla_gate_bias', 'gla_norm_g', 'rwkv_mu', 'rwkv_w0', 'rwkv_w2', 'rwkv_a0',
        'rwkv_a2', 'rwkv_g2', 'rwkv_k_k', 'rwkv_k_a', 'rwkv_r_k', 'rwkv_ln_w', 'rwkv_ln_b', 'w_branch_a', 'w_branch_b',
        'w_out', 'norm_ffn_g', 'router_w', 'router_b', 'expert_w1', 'expert_b1', 'expert_w2', 'expert_b2', 'norm_final_g']
_OUTS = [((1, 256, 1024), 'float32')]


def kernel(**inputs):
    import numpy as _np
    import concourse.bacc as _bacc
    from concourse import mybir as _mybir
    from concourse.bass_utils import run_bass_kernel_spmd as _run

    nc = _bacc.Bacc("TRN2", target_bir_lowering=False, num_devices=1)
    arrays, args = {}, []
    for name in _INS:
        a = _np.ascontiguousarray(inputs[name])
        arrays[f"in_{name}_dram"] = a
        args.append(nc.dram_tensor(f"in_{name}_dram", a.shape, _mybir.dt.from_np(a.dtype), kind="ExternalInput").ap())
    for i, (shape, dtype) in enumerate(_OUTS):
        dt = _mybir.dt.from_np(_np.dtype(dtype))
        args.append(nc.dram_tensor(f"out_{i}_dram", shape, dt, kind="ExternalOutput").ap())
    bass_hybrid_gla_rwkv7_moe_block(nc, *args)
    r = _run(nc, [arrays], core_ids=[0])
    got = tuple(r.results[0][f"out_{i}_dram"] for i in range(len(_OUTS)))
    return got[0]
```

```python
from contextlib import ExitStack

import numpy as np

import concourse.bass as bass
from concourse import mybir

ALU = mybir.AluOpType
ACT = mybir.ActivationFunctionType
F32 = mybir.dt.float32
I32 = mybir.dt.int32
U8 = mybir.dt.uint8
AX_X = mybir.AxisListType.X

P = 128
T = 256
NT = T // P
D = 1024
KD = D // P
ITERS = 4
CH = 64
NCH = T // CH
HN = 64
E = 32
FF = 1024
TOPK = 4
SLOTS = 64
PASSES = T // SLOTS
KAPPA = float(np.exp(-0.5))
RMS_EPS, GLA_EPS, GN_EPS = 1e-6, 1e-5, 64e-5
TAU = 16.0
LEVELS = (1, 2, 4, 8, 16, 32)

C_Q, C_K, C_V, C_LR, C_OG = 0, 512, 1024, 2048, 2064
C_RW = 3088
C_R, C_RK, C_RV, C_LORA = C_RW, C_RW + 1024, C_RW + 2048, C_RW + 3072
C_GA, C_GB = C_RW + 3328, C_RW + 3328 + 1024
RANK = 16

R_MIXG, R_W0, R_A0, R_KK, R_KA, R_RK, R_LNW, R_LNB, R_MU, R_GB, R_NG, R_FFN = 0, 8, 16, 24, 32, 40, 48, 56, 64, 90, 94, 96
NROWS = 104
MU_R, MU_K, MU_V, MU_L = R_MU, R_MU + 8, R_MU + 16, R_MU + 24

WRING = 3
ROUND = ("rk", "rr", "rv", "qk", "gv", "og")
GATES = ("ga", "gb")

POINTS = ("prep", "pt", "s0", "u1", "s1", "u2", "s2", "u3", "y", "mean", "var")
SHARE = {False: (4, 1, 1, 1, 1, 1, 1, 1, 1, 0, 0), True: (5, 1, 1, 1, 1, 1, 1, 1, 1, 1, 2)}


def weight_blocks():
    blocks = [("lora", 0), ("lr", 0)]
    blocks += [(kind, it) for it in range(ITERS) for kind in ROUND]
    blocks += [(kind, it) for it in range(ITERS) for kind in GATES]
    for m in range(4):
        blocks += [("wa", m), ("wb", m)]
    return blocks + [("wo", m) for m in range(4)]


def between(it):
    last = it == ITERS - 1
    if last:
        tiles = [(kind, n, j) for n in range(ITERS) for kind in GATES for j in range(2)]
    else:
        tiles = [(kind, it + 1, j) for kind in ROUND for j in range(2)]
    plan = {}
    for point, count in zip(POINTS, SHARE[last]):
        plan[point], tiles = tiles[:count], tiles[count:]
    assert not tiles
    return plan


def fill_order():
    low, order = set(), []

    def z(name):
        low.add(name)
        order.append(name)

    order.append(("par",))
    order.extend(("hT", c) for c in range(KD // 2))

    def ranks(it):
        order.extend([("lw", it), ("la", it), ("lg", it), ("gl", it)])

    def norms(it):
        order.extend([("kn", it), ("bo", it)])

    for j in range(2):
        z(("z", "lora", 0, j))
    z(("z", "lr", 0, 0))
    for kind in ROUND:
        for j in range(2):
            z(("z", kind, 0, j))
    ranks(0)
    norms(0)
    for it in range(ITERS):
        plan = between(it)

        def more(point):
            for kind, n, j in plan[point]:
                z(("z", kind, n, j))

        more("prep")
        order.extend((("tr", it, kind) for kind in "ABKV"))
        for kind in "BK":
            for hh in range(2):
                for u in range(2):
                    order.append(("L" + kind, it, hh, u))
        order.extend(("LL", it, hh) for hh in range(2))
        order.append(("X", it))
        for lev in LEVELS[1:]:
            order.extend(("Z", it, lev, g) for g in range(4))
            order.extend(("TG", it, lev, g) for g in range(4))
        order.extend([("Q", it), ("PT", it)])
        more("pt")
        order.extend([("gs", it), ("gk", it), ("S", it, 0), ("gS", it, 0)])
        more("s0")
        order.extend([("U", it, 1), ("gS", it, 1)])
        more("u1")
        order.extend([("S", it, 1), ("gS", it, 2)])
        more("s1")
        order.extend([("U", it, 2), ("go", it)])
        more("u2")
        order.append(("S", it, 2))
        more("s2")
        order.extend([("U", it, 3), ("gn", it)])
        more("u3")
        order.append(("y", it))
        if it + 1 < ITERS:
            ranks(it + 1)
        more("y")
        order.append(("mean", it))
        more("mean")
        order.append(("var", it))
        more("var")
        if it + 1 < ITERS:
            norms(it + 1)
    for m in range(KD):
        z(("ba", m))
        z(("bb", m))
    for m in range(4):
        for tt in range(NT):
            z(("out", m, tt))
        if m:
            order.append(("h2T", m - 1))
    order.extend([("h2T", 3), ("log",), ("pos",), ("cnt",), ("gT",)])
    order.extend(("b2", i) for i in range(4))
    bank, nth, used = {}, {}, [0] * 8
    turn = [0, 0]
    for name in order:
        lo = name in low
        b = turn[0] % 4 if lo else 4 + turn[1] % 4
        turn[0 if lo else 1] += 1
        bank[name], nth[name] = b, used[b]
        used[b] += 1
    return order, bank, nth, used


def bass_hybrid_gla_rwkv7_moe_block(
    nc, x, norm_mix_g, w_in, gla_gate_up, gla_gate_bias, gla_norm_g, rwkv_mu, rwkv_w0, rwkv_w2, rwkv_a0,
    rwkv_a2, rwkv_g2, rwkv_k_k, rwkv_k_a, rwkv_r_k, rwkv_ln_w, rwkv_ln_b, w_branch_a, w_branch_b, w_out,
    norm_ffn_g, router_w, router_b, expert_w1, expert_b1, expert_w2, expert_b2, norm_final_g, out, debug=None,
):
    order, bank_of, nth_of, fills = fill_order()
    blocks = weight_blocks()
    block_index = {b: n for n, b in enumerate(blocks)}

    with ExitStack() as ctx:
        def sem(name):
            return ctx.enter_context(nc.semaphore(name))

        def keep(name, shape, dt=F32):
            return ctx.enter_context(nc.sbuf_tensor(name, shape, dt))

        banks = [ctx.enter_context(nc.psum_tensor(f"bank{b}", [P, 512], F32)) for b in range(8)]

        xs = keep("xs", [P, NT, D])
        ident = keep("ident", [P, P])
        ones = keep("ones", [P, P])
        headones = keep("headones", [P, P])
        before = keep("before", [P, P])
        stat = keep("stat", [P, 24])
        ffn_col = keep("ffn_col", [P, KD])
        epsc = keep("epsc", [P, 4])

        mix = ExitStack()

        def sb(name, shape, dt=F32):
            return mix.enter_context(nc.sbuf_tensor(name, shape, dt))

        wring = sb("wring", [P, WRING, KD, 256])
        gates = sb("gates", [P, 16, T])
        yA = sb("yA", [P, KD, T])
        yB = sb("yB", [P, KD, T])
        kept_to_end = nc.sbuf_base
        hT = sb("hT", [P, KD, T])
        prow = sb("prow", [P, P])
        pcol = sb("pcol", [P, NROWS])
        w2a2 = sb("w2a2", [P, D])
        g2 = sb("g2", [P, D])
        gup = sb("gup", [RANK, 512])
        below = sb("below", [P, P])
        upto = sb("upto", [P, P])
        upto8 = sb("upto8", [P, P], U8)
        low8 = sb("low8", [P, len(LEVELS), P], U8)
        up8 = sb("up8", [P, len(LEVELS), P], U8)
        chunkmask = sb("chunkmask", [P, 2 * T])
        zl = sb("zl", [P, 2, T + 1])
        ul = sb("ul", [P, 2, T])
        zlr = sb("zlr", [RANK, T])
        zs = sb("zs", [P, 6, T + 1])
        dsh = sb("dsh", [P, 6, T])
        u = sb("u", [P, 4, T])
        uv = sb("uv", [P, 2, 2, T])
        gg = sb("gg", [P, 2, 2, T])
        sgw = sb("sgw", [P, 2, T])
        aa = sb("aa", [P, 2, T])
        cc = sb("cc", [P, 2, T])
        cm = sb("cm", [P, 2, T])
        Wc = cc
        Wi = sb("Wi", [P, 2, T])
        Wp = cm
        kk0 = sb("kk0", [P, 2, T])
        sq = sb("sq", [P, 2, T])
        km = sb("km", [P, 2, T])
        bp = sb("bp", [P, 2, T])
        bon = sb("bon", [P, 2, T])
        ch4 = {k: sb("ch" + k, [P, 4, P]) for k in "bkBK"}
        AR = sb("AR", [P, 4, 2, P])
        tm = {k: sb("tm" + k, [P, 4, P]) for k in "ABKV"}
        mats = {k: sb("m" + k, [P, 8, P]) for k in ("N", "T", "G", "Z", "Mrb", "Mrk")}
        mats["Lak"] = mats["Z"]
        Xs = sb("Xs", [P, 4, P])
        Qs = sb("Qs", [P, 4, P])
        PTs = sb("PTs", [P, 4, P])
        Us = Xs
        Ss = sb("Ss", [P, NCH - 1, 2, P])
        ys = sb("ys", [P, 2, T])
        gq = sb("gq", [P, 2, T])
        gk = sb("gk", [P, 2, T])
        gv = sb("gv", [P, 2, NT, T])
        og = sb("og", [P, 2, 2, T])
        gx = sb("gx", [P, 2, T])
        halves = {k: ch4[k][:, :, :].rearrange("p a t -> p (a t)").rearrange("p (a t) -> p a t", t=T) for k in "bk"}
        gprod = [halves["b"][:, 0, :], halves["b"][:, 1, :], halves["k"][:, 0, :], halves["k"][:, 1, :]]
        gtmp = [dsh[:, n, :] for n in (0, 1, 3, 4)]
        gsT = mats["N"][:, 0:2, :]
        gkt = mats["N"][:, 2:4, :]
        gSt = mats["Z"][:, :, :].rearrange("p (c a) t -> p c (a t)", a=2)

        ints = og[:, :, :, :].rearrange("p a b t -> p (a b t)").bitcast(I32).rearrange("p (a t) -> p a t", t=P)
        mix.close()

        moe = ctx.enter_context(ExitStack())

        def mb(name, shape, dt=F32):
            return moe.enter_context(nc.sbuf_tensor(name, shape, dt))

        h2 = mb("h2", [P, NT, D])
        h2T = mb("h2T", [P, KD, T])
        acc = xs
        lg = mb("lg", [P, NT, E])
        top = mb("top", [P, NT, 8])
        rt = mb("rt", [P, 6, NT, E])
        selM = mb("selM", [P, NT, E])
        posm = mb("posm", [P, E, NT])
        gatev = mb("gatev", [P, E, NT])
        gT = mb("gT", [E, T])
        rs = mb("rs", [P, 16])
        over = mb("over", [P, 1], I32)
        iota = mb("iota", [P, (PASSES + 1) * SLOTS])
        onesE = mb("onesE", [E, SLOTS])
        ehot = mb("ehot", [E, SLOTS])
        sel = mb("sel", [P, NT, SLOTS])
        selg = mb("selg", [P, NT, 2, SLOTS])
        selgT = mb("selgT", [P, NT, P])
        xg = mb("xg", [P, KD, SLOTS])
        glu = mb("glu", [P, 2, 256])
        sgm = mb("sgm", [P, 2, 256])
        lin = mb("lin", [P, 2, 256])
        act_s = mb("act_s", [P, 2, 256])
        actT = mb("actT", [P, 4, P])
        eo = mb("eo", [P, 512])
        mb("skipped", [P, (kept_to_end - nc.sbuf_base) // 4])
        w1s = mb("w1s", [P, KD, 2 * FF])
        w2s = mb("w2s", [P, FF // P, D])
        ffn_g = mb("ffn_g", [P, D])
        final_g = mb("final_g", [P, D])
        rw = mb("rw", [P, KD, E])
        rb = mb("rb", [P, E])
        b1s = mb("b1s", [E, 2 * FF])
        b2s = mb("b2s", [E, D])

        filled = [sem(f"bank{b}_filled") for b in range(8)]
        drained = [sem(f"bank{b}_drained") for b in range(8)]
        x_in, rows_in, lora_in, late_in = sem("x_in"), sem("rows_in"), sem("lora_in"), sem("late_in")
        w_in_ready = [sem(f"weights_in{s}") for s in range(WRING)]
        w_used = sem("weights_used")
        dve_step, act_step, pool_step = sem("dve_step"), sem("act_step"), sem("pool_step")
        raw_consts, mask_ready, consts_ready = sem("raw_consts"), sem("mask_ready"), sem("consts_ready")
        sumsq_ready, rstd_ready, xn_ready = sem("sumsq_ready"), sem("rstd_ready"), sem("xn_ready")
        lora_mixed, lora_act = sem("lora_mixed"), sem("lora_act")
        shifted = sem("shifted")
        cum_ready, exps_ready = sem("cum_ready"), sem("exps_ready")
        ksq_ready, bprod_ready, knorm_ready = sem("ksq_ready"), sem("bprod_ready"), sem("knorm_ready")
        prepared = sem("prepared")
        eye_ready, u0_ready = sem("eye_ready"), sem("u0_ready")
        ysq_ready, ystd_ready, yB_ready = sem("ysq_ready"), sem("ystd_ready"), sem("yB_ready")
        softplus_ready = sem("softplus_ready")
        b_ready, gexp_ready, gprep_ready = sem("b_ready"), sem("gexp_ready"), sem("gprep_ready")
        gsq_ready, gstd_ready, yA_ready = sem("gsq_ready"), sem("gstd_ready"), sem("yA_ready")
        merged_ready, x1_ready, h2_ready = sem("merged_ready"), sem("x1_ready"), sem("h2_ready")
        mask_sel, route_ready, gexpo = sem("mask_sel"), sem("route_ready"), sem("gexpo")
        mean_ready, last_sums = sem("mean_ready"), sem("last_sums")
        lmax_ready, gatev_ready = sem("lmax_ready"), sem("gatev_ready")
        moe_pool = sem("moe_pool")
        w1_in = [sem(f"w1_in{k}") for k in range(KD)]
        w2_in = [sem(f"w2_in{k}") for k in range(4)]
        w1_used, w2_used = sem("w1_used"), sem("w2_used")
        sel_ready, selg_ready = sem("sel_ready"), sem("selg_ready")
        gather_done, selT_done = sem("gather_done"), sem("selT_done")
        xg_ready, selgT_ready = sem("xg_ready"), sem("selgT_ready")
        hid_done, glu_ready, sgm_ready, act_ready = (
            sem("hid_done"), sem("glu_ready"), sem("sgm_ready"), sem("act_ready"))
        actT_done, actT_ready = sem("actT_done"), sem("actT_ready")
        eo_done, eo_ready = sem("eo_done"), sem("eo_ready")
        y_done, y_added = sem("y_done"), sem("y_added")
        final_ready, out_done = sem("final_ready"), sem("out_done")

        def view(name, *shape):
            b = banks[bank_of[name]][:, :]
            if len(shape) == 2:
                return b[:, 0:shape[0] * shape[1]].rearrange("p (a b) -> p a b", a=shape[0])
            if len(shape) == 3:
                return b[:, 0:shape[0] * shape[1] * shape[2]].rearrange("p (a b c) -> p a b c", a=shape[0], b=shape[1])
            return b[:, 0:shape[0]]

        def await_filled(eng, name):
            eng.wait_ge(filled[bank_of[name]], nth_of[name] + 1)

        def await_drained(eng, name):
            eng.wait_ge(drained[bank_of[name]], nth_of[name] + 1)

        def wait_after(eng, semaphore, value):
            if not (isinstance(value, int) and value == 0):
                eng.wait_ge(semaphore, value)

        ring_count, slot_total = [], [0] * WRING
        for n, (kind, _) in enumerate(blocks):
            slot_total[n % WRING] += 32 if kind == "qk" else 16
            ring_count.append(slot_total[n % WRING])

        def wslot(kind, it):
            return wring[:, block_index[(kind, it)] % WRING]

        def col(row):
            return pcol[:, row:row + 1]

        win = w_in[0].rearrange("(k p) n -> p k n", p=P)
        branch = {
            "wa": w_branch_a[0].rearrange("(k p) n -> p k n", p=P),
            "wb": w_branch_b[0].rearrange("(k p) n -> p k n", p=P),
            "wo": w_out[0].rearrange("(k p) n -> p k n", p=P),
        }

        ehot_ready, last_scattered, last_added = sem("ehot_ready"), sem("last_scattered"), sem("last_added")
        glu_half, lin_ready, gated_ready = sem("glu_half"), sem("lin_ready"), sem("gated_ready")

        block = ctx.enter_context(nc.Block())

        @block.sync
        def _(sp):
            sp.dma_start(xs[:, :, :], x[0].rearrange("(a p) d -> p a d", p=P)).then_inc(x_in, 16)
            rows = [
                (R_MIXG, 8, norm_mix_g[0]), (R_W0, 8, rwkv_w0[0]), (R_A0, 8, rwkv_a0[0]), (R_KK, 8, rwkv_k_k[0]),
                (R_KA, 8, rwkv_k_a[0]), (R_RK, 8, rwkv_r_k[0].rearrange("h n -> (h n)")), (R_LNW, 8, rwkv_ln_w[0]),
                (R_LNB, 8, rwkv_ln_b[0]), (R_MU, 26, rwkv_mu[0]), (R_GB, 4, gla_gate_bias[0]), (R_NG, 2, gla_norm_g[0]),
                (R_FFN, 8, norm_ffn_g[0]),
            ]
            for r0, n, src in rows:
                sp.dma_start(prow[r0:r0 + n, :], src.rearrange("(r c) -> r c", c=P)).then_inc(rows_in, 16)
            w1v = expert_w1[0].rearrange("e (k p) n -> e p k n", p=P)
            w2v = expert_w2[0].rearrange("e (k p) n -> e p k n", p=P)

            def load_slab(i, n):
                e = i if isinstance(i, int) else i % E
                if n < KD:
                    if not isinstance(i, int):
                        sp.wait_ge(w1_used, (i - 1) * KD + (n + 1))
                    sp.dma_start(w1s[:, n, :], w1v[bass.ds(e, 1), :, n, :].rearrange("a p n -> (a p) n")).then_inc(w1_in[n], 16)
                else:
                    k = n - KD
                    if not isinstance(i, int):
                        sp.wait_ge(w2_used, (i - 1) * 4 + (k + 1))
                    sp.dma_start(w2s[:, 2 * k:2 * k + 2, :],
                                 w2v[bass.ds(e, 1), :, 2 * k:2 * k + 2, :].rearrange("a p k n -> (a p) k n")).then_inc(w2_in[k], 16)

            first_spread = block_index[("wb", 1)]
            slabs_after = dict(zip(range(first_spread, len(blocks)), ((), (0,), (1,), (2,), (3,), (4,), (5, 6), (7, 8), (9, 10, 11))))

            for n, (kind, it) in enumerate(blocks):
                if n >= WRING:
                    sp.wait_ge(w_used, n - WRING + 1)
                dst = wring[:, n % WRING]
                ready = w_in_ready[n % WRING]
                if kind in branch:
                    sp.dma_start(dst, branch[kind][:, :, 256 * it:256 * it + 256]).then_inc(ready, 16)
                elif kind == "qk":
                    sp.dma_start(dst[:, :, 0:P], win[:, :, C_Q + P * it:C_Q + P * it + P]).then_inc(ready, 16)
                    sp.dma_start(dst[:, :, P:2 * P], win[:, :, C_K + P * it:C_K + P * it + P]).then_inc(ready, 16)
                else:
                    first = {"lora": C_LORA, "lr": C_LR, "rk": C_RK, "rr": C_R, "rv": C_RV, "gv": C_V, "og": C_OG,
                             "ga": C_GA, "gb": C_GB}[kind] + 256 * it
                    width = RANK if kind == "lr" else 256
                    sp.dma_start(dst[:, :, 0:width], win[:, :, first:first + width]).then_inc(ready, 16)
                for slab in slabs_after.get(n, ()):
                    load_slab(0, slab)
                if n == first_spread:
                    sp.wait_ge(yA_ready, ITERS)
                    sp.wait_ge(yB_ready, ITERS)
                    sp.dma_start(rw[:, :, :], router_w[0].rearrange("(k p) e -> p k e", p=P)).then_inc(late_in, 16)
                    sp.dma_start(rb[:, :], router_b.broadcast_to([P, E])).then_inc(late_in, 16)
                    sp.dma_start(ffn_g[:, :], norm_ffn_g.broadcast_to([P, D])).then_inc(late_in, 16)
                    sp.dma_start(final_g[:, :], norm_final_g.rearrange("(a d) -> a d", a=1).broadcast_to([P, D])).then_inc(late_in, 16)
                    sp.dma_start(b1s[:, :], expert_b1[0]).then_inc(late_in, 16)
                    sp.dma_start(b2s[:, :], expert_b2[0]).then_inc(late_in, 16)
                if n == 1:
                    sp.dma_start(w2a2[0:64, :], rwkv_w2[0]).then_inc(lora_in, 16)
                    sp.dma_start(w2a2[64:128, :], rwkv_a2[0]).then_inc(lora_in, 16)
                    sp.dma_start(g2[:, :], rwkv_g2[0]).then_inc(lora_in, 16)
                    sp.dma_start(gup[:, :], gla_gate_up[0]).then_inc(lora_in, 16)
            with sp.Fori(1, E) as i:
                for n in range(KD + 4):
                    load_slab(i, n)
            sp.wait_ge(route_ready, 1)
            most = sp.value_load(over[0:1, 0:1], min_val=0, max_val=T)
            with sp.If(most > SLOTS):
                with sp.Fori(E, PASSES * E) as i:
                    for n in range(KD + 4):
                        load_slab(i, n)
            fin = h2T[:, :, :].rearrange("p a b -> p (a b)").rearrange("p (a d) -> p a d", a=NT)
            for tt in range(NT):
                sp.wait_ge(final_ready, tt + 1)
                sp.dma_start(out[0, P * tt:P * tt + P, :], fin[:, tt, :]).then_inc(out_done, 16)
            sp.wait_ge(out_done, NT * 16)

        @block.gpsimd
        def _(pool):
            pool.memset(ones[:, :], 1.0).then_inc(raw_consts, 1)
            pool.iota(ints[:, 0, :], [[0, P]], 0, 1).then_inc(raw_consts, 1)
            pool.iota(ints[:, 1, :], [[1, P]], 0, 0).then_inc(raw_consts, 1)
            pool.memset(zs[:, :, 0:1], 0.0).then_inc(raw_consts, 1)
            pool.memset(zl[:, :, 0:1], 0.0).then_inc(raw_consts, 1)
            pool.memset(Ss[:, :, :, :], 0.0).then_inc(raw_consts, 1)
            pool.memset(chunkmask[:, :], 1.0).then_inc(raw_consts, 1)
            pool.wait_ge(raw_consts, 7)
            pool.memset(chunkmask[:, :].rearrange("p (c t) -> p c t", t=CH)[:, :, 0:1], 0.0).then_inc(raw_consts, 1)
            pool.memset(epsc[:, 0:1], RMS_EPS).then_inc(raw_consts, 1)
            pool.memset(epsc[:, 1:2], GLA_EPS).then_inc(raw_consts, 1)
            pool.memset(epsc[:, 2:3], GN_EPS).then_inc(raw_consts, 1)
            for it in range(ITERS):
                if it == 0:
                    pool.wait_ge(consts_ready, 1)
                else:
                    await_filled(pool, ("PT", it - 1))
                for k in "TG":
                    pool.tensor_copy(mats[k][:, :, :], ident[:, :].unsqueeze(1).broadcast_to([P, 8, P])).then_inc(eye_ready, 1)
            pool.wait_ge(x1_ready, 1)
            pool.iota(iota[:, :], [[1, (PASSES + 1) * SLOTS]], -4096, 0,
                      allow_small_or_imprecise_dtypes=True).then_inc(moe_pool, 1)
            pool.memset(onesE[:, :], 1.0).then_inc(moe_pool, 1)

        @block.scalar
        def _(act):
            steps = [0]

            def link(ins):
                steps[0] += 1
                ins.then_inc(act_step, 1)
                act.wait_ge(act_step, steps[0])

            def drains(ins, name):
                ins.then_inc(drained[bank_of[name]], 1)

            act.wait_ge(x_in, 16)
            act.wait_ge(raw_consts, 11)
            for tt in range(NT):
                act.activation(hT[:, 4 * tt:4 * tt + 4, :].rearrange("p a b -> p (a b)"), xs[:, tt, :], ACT.Square,
                               accum_out=stat[:, tt:tt + 1]).then_inc(sumsq_ready, 1)
            act.wait_ge(sumsq_ready, 2)
            act.activation(stat[:, 2:4], stat[:, 0:2], ACT.Sqrt, bias=epsc[:, 0:1], scale=1.0 / D).then_inc(sumsq_ready, 1)
            act.wait_ge(rstd_ready, 1)
            xn = yA[:, :, :].rearrange("p a b -> p (a b)").rearrange("p (a d) -> p a d", a=NT)
            for tt in range(NT):
                act.activation(xn[:, tt, :], xs[:, tt, :], ACT.Copy, scale=stat[:, 4 + tt:5 + tt]).then_inc(xn_ready, 1)

            def take(kind, it, j):
                par = it % 2
                if kind == "rk" and j == 0 and it:
                    act.wait_ge(shifted, it)
                if kind == "qk" and j == 0 and it >= 2:
                    act.wait_ge(yA_ready, it - 1)
                name = ("z", kind, it, j)
                await_filled(act, name)
                z = view(name, T)
                if kind == "lora":
                    drains(act.activation(zl[:, j, 1:T + 1], z, ACT.Copy), name)
                elif kind == "lr":
                    drains(act.activation(zlr[:, :], z[0:RANK, :], ACT.Copy), name)
                elif kind in ("rk", "rr", "rv"):
                    at = 2 * ("rk", "rr", "rv").index(kind) + j
                    drains(act.activation(zs[:, at, 1:T + 1], z, ACT.Copy), name)
                elif kind == "qk":
                    drains(act.activation((gq, gk)[j][:, par, :], z, ACT.Copy,
                                          scale=float(P) ** -0.5 if j == 0 else 1.0), name)
                elif kind == "gv":
                    drains(act.activation(gv[:, par, j, :], z, ACT.Copy), name)
                elif kind == "og":
                    drains(act.activation(og[:, par, j, :], z, ACT.Copy), name)
                else:
                    at = (0 if kind == "ga" else KD) + 2 * it + j
                    drains(act.activation(gates[:, at, :], z, ACT.Sigmoid), name)

            def ranks(it):
                par = it % 2
                if it == 0:
                    act.wait_ge(lora_mixed, 1)
                    act.activation(ul[0:64, 0, :], ul[0:64, 0, :], ACT.Tanh).then_inc(lora_act, 1)
                    act.activation(ul[:, 1, :], ul[:, 1, :], ACT.Sigmoid).then_inc(lora_act, 1)
                else:
                    act.wait_ge(prepared, it)
                for key, dst, r0 in (("lw", sgw, R_W0), ("la", aa, R_A0)):
                    await_filled(act, (key, it))
                    link(act.activation(dst[:, 0, :], view((key, it), 2, T)[:, 0, :], ACT.Sigmoid, bias=col(r0 + 2 * it)))
                    drains(act.activation(dst[:, 1, :], view((key, it), 2, T)[:, 1, :], ACT.Sigmoid,
                                          bias=col(r0 + 2 * it + 1)), (key, it))
                await_filled(act, ("lg", it))
                if it >= 2:
                    act.wait_ge(yB_ready, it - 1)
                drains(act.activation(gg[:, par, :, :], view(("lg", it), 2, T), ACT.Copy), ("lg", it))
                await_filled(act, ("gl", it))
                drains(act.activation(gx[:, par, :], view(("gl", it), T), ACT.Identity, bias=col(R_GB + it)), ("gl", it))

            kk_n = sq[:, :, :].rearrange("p a b -> p (a b)")
            y_std = Wi[:, :, :].rearrange("p a b -> p (a b)")

            def exps(it):
                await_filled(act, ("kn", it))
                act.activation(kk_n, view(("kn", it), 512), ACT.Sqrt).then_inc(drained[bank_of[("kn", it)]], 1)
                act.wait_ge(cum_ready, it + 1)
                if it >= 1:
                    act.wait_ge(yB_ready, it)
                act.activation(Wi[:, :, :], cc[:, :, :], ACT.Exp, scale=KAPPA).then_inc(exps_ready, 1)
                act.activation(Wc[:, :, :], cc[:, :, :], ACT.Exp, scale=-KAPPA).then_inc(exps_ready, 1)
                act.activation(Wp[:, :, :], cm[:, :, :], ACT.Exp, scale=-KAPPA).then_inc(exps_ready, 1)
                await_drained(act, ("gl", it))
                if it >= 1:
                    act.wait_ge(yA_ready, it)
                link(act.activation(dsh[:, 0, :], gx[:, it % 2, :], ACT.Abs))
                link(act.activation(dsh[:, 0, :], dsh[:, 0, :], ACT.Exp, scale=-1.0))
                act.activation(dsh[:, 1, :], dsh[:, 0, :], ACT.Ln, bias=1.0).then_inc(softplus_ready, 1)

            def round_(it):
                plan = between(it)

                def more(point):
                    for tile in plan[point]:
                        take(*tile)

                more("prep")
                for kind in "ABKV":
                    await_filled(act, ("tr", it, kind))
                    drains(act.activation(tm[kind][:, :, :], view(("tr", it, kind), 4, P), ACT.Copy), ("tr", it, kind))
                act.wait_ge(b_ready, it + 1)
                for k in range(4):
                    src = (dsh[:, 2, :], dsh[:, 2, :], dsh[:, 3, :], dsh[:, 4, :])[k]
                    act.activation(gtmp[k], src, ACT.Exp, scale=(-1.0 if k == 1 else 1.0) / TAU).then_inc(gexp_ready, 1)
                act.wait_ge(gexp_ready, 6 * it + 2)
                for j in range(2):
                    act.activation(dsh[:, 2 + 3 * j, :], og[:, it % 2, j, :], ACT.Sigmoid).then_inc(gexp_ready, 1)
                await_filled(act, ("X", it))
                drains(act.activation(Xs[:, :, :], view(("X", it), 4, P), ACT.Copy), ("X", it))
                for lev in LEVELS[1:]:
                    for g in range(4):
                        name = ("Z", it, lev, g)
                        await_filled(act, name)
                        drains(act.activation(mats["Z"][:, 2 * g:2 * g + 2, :], view(name, 2, P), ACT.Copy), name)
                for key, dst in (("Q", Qs), ("PT", PTs)):
                    await_filled(act, (key, it))
                    drains(act.activation(dst[:, :, :], view((key, it), 4, P), ACT.Copy), (key, it))
                more("pt")
                await_filled(act, ("gk", it))
                drains(act.activation(gkt, view(("gk", it), 2, P), ACT.Copy), ("gk", it))
                for point in ("s0", "u1", "s1"):
                    more(point)
                await_filled(act, ("go", it))
                act.activation(dsh[:, 2:4, :], view(("go", it), 2, T), ACT.Square).then_inc(gsq_ready, 1)
                more("u2")
                more("s2")
                await_filled(act, ("gn", it))
                drains(act.activation(dsh[:, 4, :], view(("gn", it), T), ACT.Sqrt, bias=epsc[:, 1:2], scale=1.0 / 256), ("gn", it))
                more("u3")
                await_filled(act, ("y", it))
                drains(act.activation(ys[:, :, :], view(("y", it), 2, T), ACT.Copy), ("y", it))
                if it + 1 < ITERS:
                    ranks(it + 1)
                more("y")
                more("mean")
                await_filled(act, ("var", it))
                drains(act.activation(y_std, view(("var", it), 512), ACT.Sqrt, bias=epsc[:, 2:3], scale=1.0 / HN), ("var", it))
                more("var")
                if it + 1 < ITERS:
                    exps(it + 1)

            act.wait_ge(consts_ready, 1)
            for j in range(2):
                take("lora", 0, j)
            take("lr", 0, 0)
            for kind in ROUND:
                for j in range(2):
                    take(kind, 0, j)
            ranks(0)
            exps(0)
            for it in range(ITERS):
                round_(it)
            for m in range(4):
                for tt in range(NT):
                    await_drained(act, ("out", m, tt))
                    act.activation(gates[:, KD + 2 * m + tt, :], xs[:, tt, 256 * m:256 * m + 256], ACT.Square,
                                   accum_out=stat[:, 16 + 4 * tt + m:17 + 4 * tt + m]).then_inc(sumsq_ready, 1)
            act.wait_ge(mean_ready, 1)
            act.activation(stat[:, 8:10], stat[:, 6:8], ACT.Sqrt, bias=epsc[:, 0:1], scale=1.0 / D).then_inc(sumsq_ready, 1)
            act.wait_ge(lmax_ready, 1)
            for tt in range(NT):
                act.activation(rt[:, 4, tt, :], lg[:, tt, :], ACT.Exp, bias=rs[:, tt:tt + 1]).then_inc(gexpo, 1)

            act.preload_act_table(ACT.Sigmoid)

            def gathered(i):
                act.wait_ge(gather_done, i + 1)
                act.activation(xg[:, :, :], banks[0][:, :].rearrange("p (k s) -> p k s", k=KD), ACT.Copy).then_inc(xg_ready, 1)

            def expert(i):
                act.wait_ge(glu_ready, i + 1)
                act.activation(sgm[:, :, :], glu[:, :, :], ACT.Sigmoid, scale=1.702).then_inc(sgm_ready, 1)
                gathered(i + 1)
                act.wait_ge(actT_done, i + 1)
                act.activation(actT[:, :, :], banks[4][:, :].rearrange("p (k s) -> p k s", k=4), ACT.Copy).then_inc(actT_ready, 1)
                act.wait_ge(eo_done, i + 1)
                act.activation(eo[:, :], banks[5][:, :], ACT.Copy).then_inc(eo_ready, 1)

            gathered(0)
            expert(0)
            with act.Fori(1, E) as i:
                expert(i)
            act.wait_ge(route_ready, 1)
            most = act.value_load(over[0:1, 0:1], min_val=0, max_val=T)
            with act.If(most > SLOTS):
                with act.Fori(E, PASSES * E) as i:
                    expert(i)
            for tt in range(NT):
                act.wait_ge(last_added, 2 * tt + 2)
                act.activation(h2[:, tt, :], xs[:, tt, :], ACT.Square, accum_out=stat[:, 10 + tt:11 + tt]).then_inc(last_sums, 1)
                act.wait_ge(last_sums, 2 * tt + 1)
                act.activation(stat[:, 12 + tt:13 + tt], stat[:, 10 + tt:11 + tt], ACT.Sqrt, bias=epsc[:, 0:1],
                               scale=1.0 / D).then_inc(last_sums, 1)

        @block.vector
        def _(dve):
            steps = [0]

            def link(ins):
                steps[0] += 1
                ins.then_inc(dve_step, 1)
                dve.wait_ge(dve_step, steps[0])

            def drains(ins, name):
                ins.then_inc(drained[bank_of[name]], 1)
                dve.wait_ge(drained[bank_of[name]], nth_of[name] + 1)

            dve.wait_ge(raw_consts, 11)
            diff = gates[:, :, :].rearrange("p a b -> p (a b)").rearrange("p (a t) -> p a t", t=P)
            for k in range(7):
                link(dve.tensor_scalar(ints[:, 2, :], ints[:, 0, :], k, None, ALU.arith_shift_right))
                link(dve.tensor_scalar(ints[:, 3, :], ints[:, 1, :], k, None, ALU.arith_shift_right))
                link(dve.tensor_tensor(diff[:, k, :], ints[:, 2, :], ints[:, 3, :], ALU.subtract))
            link(dve.tensor_scalar(ident[:, :], diff[:, 0, :], 0.0, None, ALU.is_equal))
            link(dve.tensor_scalar(before[:, :], diff[:, 0, :], 0.0, None, ALU.is_lt))
            link(dve.tensor_scalar(headones[:, :], diff[:, 6, :], 0.0, None, ALU.is_equal))
            link(dve.tensor_tensor(below[:, :], before[:, :], headones[:, :], ALU.mult))
            link(dve.tensor_tensor(upto[:, :], below[:, :], ident[:, :], ALU.add))
            link(dve.tensor_copy(upto8[:, :], upto[:, :]))
            for k in range(len(LEVELS)):
                link(dve.tensor_scalar(diff[:, 8, :], diff[:, k + 1, :], 0.0, None, ALU.is_equal))
                link(dve.scalar_tensor_tensor(out=low8[:, k, :], in0=diff[:, k, :], scalar=1.0, in1=diff[:, 8, :],
                                              op0=ALU.is_equal, op1=ALU.mult))
                link(dve.scalar_tensor_tensor(out=up8[:, k, :], in0=diff[:, k, :], scalar=-1.0, in1=diff[:, 8, :],
                                              op0=ALU.is_equal, op1=ALU.mult))
            dve.sem_inc(consts_ready, 1)

            dve.wait_ge(sumsq_ready, 3)
            dve.reciprocal(stat[:, 4:6], stat[:, 2:4]).then_inc(rstd_ready, 1)
            await_filled(dve, ("par",))
            link(dve.tensor_copy(ffn_col[:, :], view(("par",), NROWS)[:, R_FFN:R_FFN + KD]))
            drains(dve.tensor_copy(pcol[:, :], view(("par",), NROWS)), ("par",))
            for c in range(KD // 2):
                name = ("hT", c)
                await_filled(dve, name)
                link(dve.tensor_scalar(hT[:, 2 * c, :], view(name, 2, T)[:, 0, :], col(R_MIXG + 2 * c), None, ALU.mult))
                drains(dve.tensor_scalar(hT[:, 2 * c + 1, :], view(name, 2, T)[:, 1, :], col(R_MIXG + 2 * c + 1), None,
                                         ALU.mult), name)

            def shift_lora():
                await_drained(dve, ("z", "lora", 0, 1))
                link(dve.tensor_tensor(dsh[:, 0:2, :], zl[:, :, 0:T], zl[:, :, 1:T + 1], ALU.subtract))
                link(dve.scalar_tensor_tensor(out=ul[:, 0, :], in0=dsh[:, 0, :], scalar=col(MU_L), in1=zl[:, 0, 1:T + 1],
                                              op0=ALU.mult, op1=ALU.add))
                dve.scalar_tensor_tensor(out=ul[:, 1, :], in0=dsh[:, 1, :], scalar=col(MU_L + 1),
                                         in1=zl[:, 1, 1:T + 1], op0=ALU.mult, op1=ALU.add).then_inc(lora_mixed, 1)

            def shift(it):
                par = it % 2
                await_drained(dve, ("z", "rv", it, 1))
                link(dve.tensor_tensor(u[:, :, :], zs[:, 0:4, 0:T], zs[:, 0:4, 1:T + 1], ALU.subtract))
                link(dve.tensor_tensor(uv[:, par, :, :], zs[:, 4:6, 0:T], zs[:, 4:6, 1:T + 1], ALU.subtract))
                for n in range(6):
                    kind, j = n // 2, n % 2
                    dst = u[:, n, :] if n < 4 else uv[:, par, j, :]
                    mu = (MU_K, MU_R, MU_V)[kind] + 2 * it + j
                    ins = dve.scalar_tensor_tensor(out=dst, in0=dst, scalar=col(mu), in1=zs[:, n, 1:T + 1],
                                                   op0=ALU.mult, op1=ALU.add)
                    if n < 5:
                        link(ins)
                    else:
                        ins.then_inc(shifted, 1)
                        dve.wait_ge(shifted, it + 1)
                for j in range(2):
                    link(dve.tensor_scalar(kk0[:, j, :], u[:, j, :], col(R_KK + 2 * it + j), None, ALU.mult))
                dve.tensor_tensor(sq[:, :, :], kk0[:, :, :], kk0[:, :, :], ALU.mult).then_inc(ksq_ready, 1)
                dve.wait_ge(ksq_ready, it + 1)

            def modify(it):
                await_drained(dve, ("la", it))
                for j in range(2):
                    link(dve.tensor_scalar(km[:, j, :], aa[:, j, :], -1.0, col(R_KA + 2 * it + j), ALU.add, ALU.mult))
                link(dve.scalar_tensor_tensor(out=km[:, :, :], in0=km[:, :, :], scalar=1.0, in1=u[:, 0:2, :],
                                              op0=ALU.add, op1=ALU.mult))
                link(dve.scalar_tensor_tensor(out=bp[:, 0, :], in0=u[:, 2, :], scalar=col(R_RK + 2 * it), in1=km[:, 0, :],
                                              op0=ALU.mult, op1=ALU.mult))
                dve.scalar_tensor_tensor(out=bp[:, 1, :], in0=u[:, 3, :], scalar=col(R_RK + 2 * it + 1), in1=km[:, 1, :],
                                         op0=ALU.mult, op1=ALU.mult).then_inc(bprod_ready, 1)
                dve.wait_ge(bprod_ready, it + 1)

            def second_half(it):
                await_drained(dve, ("la", it))
                link(dve.tensor_tensor_scan(cc[:, :, :].rearrange("p a b -> p (a b)"), chunkmask[:, :],
                                            sgw[:, :, :].rearrange("p a b -> p (a b)"), 0.0, ALU.mult, ALU.add))
                dve.tensor_tensor(cm[:, :, :], cc[:, :, :], sgw[:, :, :], ALU.subtract).then_inc(cum_ready, 1)
                dve.wait_ge(cum_ready, it + 1)
                await_drained(dve, ("kn", it))
                link(dve.tensor_scalar(sq[:, :, :], sq[:, :, :], 1e-12, None, ALU.max))
                link(dve.reciprocal(sq[:, :, :], sq[:, :, :]))
                link(dve.tensor_tensor(kk0[:, :, :], kk0[:, :, :], sq[:, :, :], ALU.mult))
                await_filled(dve, ("bo", it))
                drains(dve.tensor_tensor(bon[:, :, :], view(("bo", it), 2, T), uv[:, it % 2, :, :], ALU.mult), ("bo", it))
                dve.wait_ge(exps_ready, 3 * (it + 1))
                w4 = [w[:, :, :].rearrange("p j (a t) -> p (j a) t", t=P) for w in (Wc, Wi, Wp)]
                kk4 = kk0[:, :, :].rearrange("p j (a t) -> p (j a) t", t=P)
                link(dve.scalar_tensor_tensor(out=AR[:, :, 0, :], in0=kk4, scalar=-1.0, in1=w4[2], op0=ALU.mult, op1=ALU.mult))
                link(dve.tensor_tensor(AR[:, :, 1, :], u[:, 2:4, :].rearrange("p j (a t) -> p (j a) t", t=P), w4[0], ALU.mult))
                link(dve.tensor_tensor(aa[:, :, :], kk0[:, :, :], aa[:, :, :], ALU.mult))
                link(dve.tensor_tensor(ch4["b"][:, :, :], aa[:, :, :].rearrange("p j (a t) -> p (j a) t", t=P), w4[1], ALU.mult))
                link(dve.tensor_tensor(ch4["k"][:, :, :], km[:, :, :].rearrange("p j (a t) -> p (j a) t", t=P), w4[1], ALU.mult))
                ends = Wc[:, :, :].rearrange("p j (c t) -> p (j c) t", t=CH)[:, :, CH - 1:CH].broadcast_to([P, 2 * NCH, CH])
                for n, k in enumerate("bk"):
                    ins = dve.tensor_tensor(ch4[k.upper()][:, :, :].rearrange("p a (c t) -> p (a c) t", t=CH),
                                            ch4[k][:, :, :].rearrange("p a (c t) -> p (a c) t", t=CH), ends, ALU.mult)
                    if n == 0:
                        link(ins)
                    else:
                        ins.then_inc(prepared, 1)
                        dve.wait_ge(prepared, it + 1)

            def gla_decay(it):
                dve.wait_ge(softplus_ready, it + 1)
                link(dve.scalar_tensor_tensor(out=dsh[:, 2, :], in0=gx[:, it % 2, :], scalar=0.0, in1=dsh[:, 1, :],
                                              op0=ALU.min, op1=ALU.subtract))
                link(dve.tensor_tensor_scan(dsh[:, 3, :], chunkmask[:, 0:T], dsh[:, 2, :], 0.0, ALU.mult, ALU.add))
                b4 = dsh[:, 3, :].rearrange("p (c t) -> p c t", t=CH)
                link(dve.tensor_tensor(dsh[:, 2, :].rearrange("p (c t) -> p c t", t=CH), b4,
                                       b4[:, :, CH // 2:CH // 2 + 1].broadcast_to([P, NCH, CH]), ALU.subtract))
                dve.tensor_tensor(dsh[:, 4, :].rearrange("p (c t) -> p c t", t=CH),
                                  b4[:, :, CH - 1:CH].broadcast_to([P, NCH, CH]), b4, ALU.subtract).then_inc(b_ready, 1)

            def gla_state(it, c):
                name = ("gS", it, c)
                await_filled(dve, name)
                if c == 0:
                    drains(dve.tensor_copy(gSt[:, 0, :], view(name, T)), name)
                else:
                    drains(dve.scalar_tensor_tensor(out=gSt[:, c, :], in0=gSt[:, c - 1, :],
                                                    scalar=gtmp[2][:, CH * c + CH - 1:CH * c + CH], in1=view(name, T),
                                                    op0=ALU.mult, op1=ALU.add), name)

            def state(it, c):
                name = ("S", it, c)
                await_filled(dve, name)
                for n in range(4):
                    j, hh = n // 2, n % 2
                    r = slice(HN * hh, HN * hh + HN)
                    src = view(name, 2, P)[r, j, HN * hh:HN * hh + HN]
                    dst = Ss[r, c, j, HN * hh:HN * hh + HN]
                    if c == 0:
                        ins = dve.tensor_copy(dst, src)
                    else:
                        ins = dve.scalar_tensor_tensor(
                            out=dst, in0=Ss[r, c - 1, j, HN * hh:HN * hh + HN],
                            scalar=Wc[r, j, CH * c + CH - 1:CH * c + CH], in1=src, op0=ALU.mult, op1=ALU.add)
                    if n < 3:
                        link(ins)
                    else:
                        drains(ins, name)

            def update(it, c):
                Q4 = Qs[:, :, :].rearrange("p (j a) i -> p j a i", a=NT)
                U4 = Us[:, :, :].rearrange("p (j a) i -> p j a i", a=NT)
                tt, h = c // 2, slice(CH * (c % 2), CH * (c % 2) + CH)
                if c == 0:
                    dve.tensor_copy(U4[h, :, tt, :], Q4[h, :, tt, :]).then_inc(u0_ready, 1)
                    dve.wait_ge(u0_ready, it + 1)
                else:
                    name = ("U", it, c)
                    await_filled(dve, name)
                    drains(dve.tensor_tensor(U4[h, :, tt, :], view(name, 2, P)[h], Q4[h, :, tt, :], ALU.add), name)

            def round_(it):
                par = it % 2
                below2 = below[:, :].unsqueeze(1).broadcast_to([P, 2, P])
                upto2 = upto[:, :].unsqueeze(1).broadcast_to([P, 2, P])
                for kind, strict, incl in (("B", "N", "Mrb"), ("K", "Lak", "Mrk")):
                    for hh in range(2):
                        for uu in range(2):
                            name = ("L" + kind, it, hh, uu)
                            await_filled(dve, name)
                            i0 = 4 * hh + 2 * uu
                            link(dve.tensor_tensor(mats[strict][:, i0:i0 + 2, :], view(name, 2, 2, P)[:, :, 0, :], below2, ALU.mult))
                            drains(dve.tensor_tensor(mats[incl][:, i0:i0 + 2, :], view(name, 2, 2, P)[:, :, 1, :], upto2,
                                                     ALU.mult), name)
                dve.wait_ge(eye_ready, 2 * (it + 1))
                for hh in range(2):
                    name = ("LL", it, hh)
                    await_filled(dve, name)
                    m4 = [m[:, 0, :].unsqueeze(1).broadcast_to([P, 4, P]) for m in (low8, up8)]
                    link(dve.copy_predicated(mats["G"][:, 4 * hh:4 * hh + 4, :], m4[1], mats["N"][:, 4 * hh:4 * hh + 4, :]))
                    drains(dve.copy_predicated(mats["T"][:, 4 * hh:4 * hh + 4, :], m4[0], view(name, 4, P)), name)
                for n, lev in enumerate(LEVELS[1:]):
                    for g in range(4):
                        name = ("TG", it, lev, g)
                        await_filled(dve, name)
                        m2 = [m[:, n + 1, :].unsqueeze(1).broadcast_to([P, 2, P]) for m in (low8, up8)]
                        if n + 1 < len(LEVELS) - 1:
                            link(dve.copy_predicated(mats["T"][:, 2 * g:2 * g + 2, :], m2[0], view(name, 4, P)[:, 0:2, :]))
                        drains(dve.copy_predicated(mats["G"][:, 2 * g:2 * g + 2, :], m2[1], view(name, 4, P)[:, 2:4, :]), name)
                await_drained(dve, ("Q", it))
                update(it, 0)
                dve.wait_ge(gexp_ready, 6 * (it + 1))
                link(dve.tensor_tensor(gprod[0], gq[:, par, :], gtmp[0], ALU.mult))
                link(dve.tensor_tensor(gprod[1], gk[:, par, :], gtmp[1], ALU.mult))
                link(dve.tensor_tensor(gprod[3], gk[:, par, :], gtmp[3], ALU.mult))
                dve.tensor_tensor(gprod[2], gq[:, par, :], gtmp[2], ALU.mult).then_inc(gprep_ready, 1)
                dve.wait_ge(gprep_ready, it + 1)
                for j in range(2):
                    link(dve.tensor_tensor(og[:, par, j, :], og[:, par, j, :], dsh[:, 2 + 3 * j, :], ALU.mult))
                link(dve.memset(gsT, 0.0))
                name = ("gs", it)
                await_filled(dve, name)
                drains(dve.copy_predicated(gsT, upto8[:, :].unsqueeze(1).broadcast_to([P, NT, P]), view(name, 2, P)), name)
                state(it, 0)
                gla_state(it, 0)
                update(it, 1)
                gla_state(it, 1)
                state(it, 1)
                gla_state(it, 2)
                update(it, 2)
                state(it, 2)
                if it + 1 < ITERS:
                    shift(it + 1)
                update(it, 3)
                await_drained(dve, ("gn", it))
                link(dve.reciprocal(dsh[:, 4, :], dsh[:, 4, :]))
                name = ("go", it)
                await_filled(dve, name)
                drains(dve.tensor_tensor(dsh[:, 2:4, :], view(name, 2, T), dsh[:, 4:5, :].broadcast_to([P, 2, T]), ALU.mult), name)
                for j in range(2):
                    ins = dve.scalar_tensor_tensor(out=yA[:, 2 * it + j, :], in0=dsh[:, 2 + j, :], scalar=col(R_NG + j),
                                                   in1=og[:, par, j, :], op0=ALU.mult, op1=ALU.mult)
                    if j == 0:
                        link(ins)
                    else:
                        ins.then_inc(yA_ready, 1)
                        dve.wait_ge(yA_ready, it + 1)
                await_drained(dve, ("y", it))
                name = ("mean", it)
                await_filled(dve, name)
                drains(dve.scalar_tensor_tensor(out=ys[:, :, :], in0=view(name, 2, T), scalar=-1.0 / HN, in1=ys[:, :, :],
                                                op0=ALU.mult, op1=ALU.add), name)
                dve.tensor_tensor(Wi[:, :, :], ys[:, :, :], ys[:, :, :], ALU.mult).then_inc(ysq_ready, 1)
                dve.wait_ge(ysq_ready, it + 1)
                if it + 1 < ITERS:
                    modify(it + 1)
                await_drained(dve, ("var", it))
                link(dve.reciprocal(Wi[:, :, :], Wi[:, :, :]))
                link(dve.tensor_tensor(ys[:, :, :], ys[:, :, :], Wi[:, :, :], ALU.mult))
                for j in range(2):
                    link(dve.tensor_scalar(ys[:, j, :], ys[:, j, :], col(R_LNW + 2 * it + j), col(R_LNB + 2 * it + j),
                                           ALU.mult, ALU.add))
                link(dve.tensor_tensor(ys[:, :, :], ys[:, :, :], bon[:, :, :], ALU.add))
                dve.tensor_tensor(yB[:, 2 * it:2 * it + 2, :], ys[:, :, :], gg[:, par, :, :], ALU.mult).then_inc(yB_ready, 1)
                dve.wait_ge(yB_ready, it + 1)
                if it + 1 < ITERS:
                    second_half(it + 1)
                    gla_decay(it + 1)

            shift_lora()
            shift(0)
            modify(0)
            second_half(0)
            gla_decay(0)
            for it in range(ITERS):
                round_(it)

            for m in range(KD):
                await_filled(dve, ("ba", m))
                drains(dve.tensor_tensor(gates[:, m, :], gates[:, m, :], view(("ba", m), T), ALU.mult), ("ba", m))
                await_filled(dve, ("bb", m))
                drains(dve.tensor_tensor(gates[:, KD + m, :], gates[:, KD + m, :], view(("bb", m), T), ALU.mult), ("bb", m))
                dve.tensor_tensor(gates[:, m, :], gates[:, m, :], gates[:, KD + m, :], ALU.add).then_inc(merged_ready, 1)
            for m in range(4):
                for tt in range(NT):
                    name = ("out", m, tt)
                    await_filled(dve, name)
                    drains(dve.tensor_tensor(xs[:, tt, 256 * m:256 * m + 256], xs[:, tt, 256 * m:256 * m + 256], view(name, T),
                                             ALU.add), name)
                if m:
                    name = ("h2T", m - 1)
                    await_filled(dve, name)
                    drains(dve.tensor_copy(h2T[:, 2 * m - 2:2 * m, :], view(name, 2, T)), name)
            dve.wait_ge(late_in, 6 * 16)
            for k in range(KD):
                link(dve.tensor_scalar(rw[:, k, :], rw[:, k, :], ffn_col[:, k:k + 1], None, ALU.mult))
            dve.sem_inc(x1_ready, 1)
            dve.wait_ge(sumsq_ready, 3 + 8)
            dve.tensor_reduce(stat[:, 6:8], stat[:, 16:24].rearrange("p (a m) -> p a m", a=NT), AX_X, ALU.add).then_inc(mean_ready, 1)
            name = ("h2T", 3)
            await_filled(dve, name)
            drains(dve.tensor_copy(h2T[:, 6:8, :], view(name, 2, T)), name)
            dve.wait_ge(sumsq_ready, 3 + 9)
            link(dve.reciprocal(stat[:, 8:10], stat[:, 8:10]))
            name = ("log",)
            await_filled(dve, name)
            for tt in range(NT):
                ins = dve.scalar_tensor_tensor(out=lg[:, tt, :], in0=view(name, NT, E)[:, tt, :], scalar=stat[:, 8 + tt:9 + tt],
                                               in1=rb[:, :], op0=ALU.mult, op1=ALU.add)
                if tt < NT - 1:
                    link(ins)
                else:
                    drains(ins, name)
            for tt in range(NT):
                link(dve.max(top[:, tt, :], lg[:, tt, :]))
            dve.tensor_scalar(rs[:, 0:2].unsqueeze(2), top[:, :, 0:1], -1.0, None, ALU.mult).then_inc(lmax_ready, 1)
            fourth = top[:, :, TOPK - 1:TOPK].broadcast_to([P, NT, E])
            link(dve.tensor_tensor(rt[:, 0, :, :], lg[:, :, :], fourth, ALU.is_gt))
            link(dve.tensor_tensor(rt[:, 1, :, :], lg[:, :, :], fourth, ALU.is_equal))
            link(dve.tensor_reduce(rs[:, 2:4], rt[:, 0, :, :], AX_X, ALU.add))
            for tt in range(NT):
                link(dve.tensor_tensor_scan(rt[:, 2, tt, :], ones[:, 0:E], rt[:, 1, tt, :], rs[:, 2 + tt:3 + tt], ALU.mult, ALU.add))
            link(dve.scalar_tensor_tensor(out=rt[:, 2, :, :], in0=rt[:, 2, :, :], scalar=float(TOPK), in1=rt[:, 1, :, :],
                                          op0=ALU.is_le, op1=ALU.mult))
            dve.tensor_tensor(selM[:, :, :], rt[:, 2, :, :], rt[:, 0, :, :], ALU.add).then_inc(mask_sel, 1)
            for tt in range(NT):
                dve.scalar_tensor_tensor(out=h2[:, tt, :], in0=xs[:, tt, :], scalar=stat[:, 8 + tt:9 + tt], in1=ffn_g[:, :],
                                         op0=ALU.mult, op1=ALU.mult).then_inc(h2_ready, 1)
            name = ("pos",)
            await_filled(dve, name)
            dve.wait_ge(mask_sel, 1)
            drains(dve.scalar_tensor_tensor(out=posm[:, :, :].rearrange("p e a -> p a e"), in0=selM[:, :, :], scalar=-4096.0,
                                            in1=view(name, NT, E), op0=ALU.mult, op1=ALU.add), name)

            def gates_and_counts():
                dve.wait_ge(gexpo, 2)
                link(dve.tensor_tensor(rt[:, 4, :, :], rt[:, 4, :, :], selM[:, :, :], ALU.mult))
                link(dve.tensor_reduce(rs[:, 4:6], rt[:, 4, :, :], AX_X, ALU.add))
                link(dve.reciprocal(rs[:, 6:8], rs[:, 4:6]))
                for tt in range(NT):
                    link(dve.tensor_scalar(rt[:, 5, tt, :], rt[:, 4, tt, :], rs[:, 6 + tt:7 + tt], None, ALU.mult))
                dve.tensor_copy(gatev[:, :, :].rearrange("p e a -> p a e"), rt[:, 5, :, :]).then_inc(gatev_ready, 1)
                name = ("cnt",)
                await_filled(dve, name)
                drains(dve.tensor_reduce(rs[:, 8:9], view(name, E), AX_X, ALU.max), name)
                dve.tensor_copy(over[:, :], rs[:, 8:9]).then_inc(route_ready, 1)
                name = ("gT",)
                await_filled(dve, name)
                drains(dve.tensor_copy(gT[:, :], view(name, T)[0:E, :]), name)
                for n in range(4):
                    name = ("b2", n)
                    await_filled(dve, name)
                    drains(dve.tensor_tensor(acc[:, n // 2, 512 * (n % 2):512 * (n % 2) + 512],
                                             acc[:, n // 2, 512 * (n % 2):512 * (n % 2) + 512], view(name, 512), ALU.add), name)

            def choose(i):
                if isinstance(i, int):
                    e, s0 = i, 0
                else:
                    e, s0 = i % E, (i // E) * SLOTS
                wait_after(dve, gather_done, i)
                dve.tensor_tensor(sel[:, :, :], iota[:, bass.ds(s0, SLOTS)].unsqueeze(1).broadcast_to([P, NT, SLOTS]),
                                  posm[:, bass.ds(e, 1), :].rearrange("p a b -> p (a b)").unsqueeze(2).broadcast_to([P, NT, SLOTS]),
                                  ALU.is_equal).then_inc(sel_ready, 1)

            def gate(i):
                e, s0 = (i, 0) if isinstance(i, int) else (i % E, (i // E) * SLOTS)
                wait_after(dve, selT_done, i)
                for tt in range(NT):
                    dve.tensor_scalar(selg[:, tt, :, :], iota[:, bass.ds(s0, SLOTS)].unsqueeze(1).broadcast_to([P, 2, SLOTS]),
                                      posm[:, bass.ds(e, 1), tt], gatev[:, bass.ds(e, 1), tt],
                                      ALU.is_equal, ALU.mult).then_inc(selg_ready, 1)

            def point(i):
                e = i if isinstance(i, int) else i % E
                wait_after(dve, hid_done, i)
                dve.tensor_scalar(ehot[:, :], onesE[:, :], ident[0:E, bass.ds(e, 1)], None, ALU.mult).then_inc(ehot_ready, 1)

            def turn(i):
                dve.wait_ge(selT_done, i + 1)
                dve.tensor_copy(selgT[:, :, :], banks[3][:, 0:T].rearrange("p (a t) -> p a t", a=NT)).then_inc(selgT_ready, 1)

            def expert(i):
                hid = [banks[1 + q][:, :].rearrange("p (m two) -> p m two", two=2) for q in range(2)]
                point(i + 1)
                wait_after(dve, act_ready, i)
                for q in range(2):
                    dve.tensor_scalar(glu[:, q, :], hid[q][:, :, 0], 7.0, None, ALU.min).then_inc(glu_half, 1) if q == 0 else \
                        dve.tensor_scalar(glu[:, q, :], hid[q][:, :, 0], 7.0, None, ALU.min).then_inc(glu_ready, 1)
                for q in range(2):
                    dve.tensor_scalar(lin[:, q, :], hid[q][:, :, 1], 7.0, -7.0, ALU.min, ALU.max).then_inc(lin_ready, 1)
                dve.wait_ge(glu_ready, i + 1)
                dve.wait_ge(lin_ready, i * 2 + 2)
                dve.scalar_tensor_tensor(out=lin[:, :, :], in0=lin[:, :, :], scalar=1.0, in1=glu[:, :, :], op0=ALU.add,
                                         op1=ALU.mult).then_inc(gated_ready, 1)
                dve.wait_ge(gated_ready, i + 1)
                dve.wait_ge(sgm_ready, i + 1)
                wait_after(dve, actT_done, i)
                dve.tensor_tensor(act_s[:, :, :], lin[:, :, :], sgm[:, :, :], ALU.mult).then_inc(act_ready, 1)
                choose(i + 2)
                if not (isinstance(i, int) and i == 0):
                    add(i - 1)
                turn(i)
                gate(i + 1)

            def add(i):
                for n in range(NT):
                    dve.wait_ge(y_done, i * NT + (n + 1))
                    for h in range(2):
                        add_bank(n, h).then_inc(y_added, 1)

            def add_bank(n, h):
                return dve.tensor_tensor(acc[:, n, 512 * h:512 * h + 512], acc[:, n, 512 * h:512 * h + 512],
                                         banks[6 + h][:, :], ALU.add)

            dve.wait_ge(moe_pool, 2)
            choose(0)
            point(0)
            gates_and_counts()
            gate(0)
            choose(1)
            expert(0)
            with dve.Fori(1, E) as i:
                expert(i)
            dve.wait_ge(route_ready, 1)
            most = dve.value_load(over[0:1, 0:1], min_val=0, max_val=T)
            with dve.If(most > SLOTS):
                with dve.Fori(E, PASSES * E) as i:
                    expert(i)
                dve.wait_ge(y_added, 4 * (PASSES * E - 1))
            for tt in range(NT):
                dve.wait_ge(last_scattered, tt + 1)
                for h in range(2):
                    add_bank(tt, h).then_inc(last_added, 1)
            fin = h2T[:, :, :].rearrange("p a b -> p (a b)").rearrange("p (a d) -> p a d", a=NT)
            dve.wait_ge(last_added, 2 * NT)
            for tt in range(NT):
                dve.wait_ge(last_sums, 2 * tt + 2)
                link(dve.reciprocal(stat[:, 14 + tt:15 + tt], stat[:, 12 + tt:13 + tt]))
                dve.scalar_tensor_tensor(out=fin[:, tt, :], in0=xs[:, tt, :], scalar=stat[:, 14 + tt:15 + tt],
                                         in1=final_g[:, :], op0=ALU.mult, op1=ALU.mult).then_inc(final_ready, 1)

        @block.tensor
        def _(pe):
            at = [0]

            def begin(name):
                assert order[at[0]] == name, (order[at[0]], name)
                at[0] += 1
                if nth_of[name]:
                    pe.wait_ge(drained[bank_of[name]], nth_of[name])

            def end(ins, name):
                ins.then_inc(filled[bank_of[name]], 1)

            pe.wait_ge(rows_in, 12 * 16)
            pe.wait_ge(consts_ready, 1)
            begin(("par",))
            end(pe.transpose(view(("par",), NROWS), prow[0:NROWS, :], ident[0:NROWS, 0:NROWS]), ("par",))
            xn = yA[:, :, :].rearrange("p a b -> p (a b)").rearrange("p (a d) -> p a d", a=NT)
            pe.wait_ge(xn_ready, 2)
            for c in range(KD // 2):
                name = ("hT", c)
                begin(name)
                for k in range(2):
                    for tt in range(NT):
                        d0 = P * (2 * c + k)
                        last = pe.transpose(view(name, 2, NT, P)[:, k, tt, :], xn[:, tt, d0:d0 + P], ident[:, :])
                end(last, name)
            await_drained(pe, ("hT", KD // 2 - 1))

            def weights(kind, it):
                n = block_index[(kind, it)]
                pe.wait_ge(w_in_ready[n % WRING], ring_count[n])
                return wslot(kind, it)

            def tile(name, w, j, token_major, more=None):
                begin(name)
                for k in range(KD):
                    if token_major:
                        last = pe.matmul(view(name, T), hT[:, k, P * j:P * j + P], w[:, k, :], start=(k == 0), stop=(k == KD - 1))
                    elif name[1] == "lr":
                        last = pe.matmul(view(name, T)[0:RANK, :], w[:, k, 0:RANK], hT[:, k, :], start=(k == 0), stop=(k == KD - 1))
                    else:
                        last = pe.matmul(view(name, T), w[:, k, P * j:P * j + P], hT[:, k, :], start=(k == 0), stop=(k == KD - 1))
                end(last, name)

            used = [0]

            def release(name):
                await_filled(pe, name)
                pe.sem_inc(w_used, 1)

            def project(kind, it, j):
                name = ("z", kind, it, j)
                tile(name, weights(kind, it), j, kind == "gv")
                if j == 1 or kind == "lr":
                    release(name)

            def ranks(it):
                if it == 0:
                    pe.wait_ge(lora_in, 4 * 16)
                    pe.wait_ge(lora_act, 2)
                for key in ("lw", "la", "lg"):
                    name = (key, it)
                    begin(name)
                    for j in range(2):
                        c0 = P * (2 * it + j)
                        if key == "lg":
                            last = pe.matmul(view(name, 2, T)[:, j, :], g2[:, c0:c0 + P], ul[:, 1, :], start=True, stop=True)
                        else:
                            r = slice(0, 64) if key == "lw" else slice(64, 128)
                            last = pe.matmul(view(name, 2, T)[:, j, :], w2a2[r, c0:c0 + P], ul[r, 0, :], start=True, stop=True)
                    end(last, name)
                name = ("gl", it)
                begin(name)
                await_drained(pe, ("z", "lr", 0, 0))
                end(pe.matmul(view(name, T), gup[:, P * it:P * it + P], zlr[:, :], start=True, stop=True), name)

            def norms(it):
                name = ("kn", it)
                begin(name)
                pe.wait_ge(ksq_ready, it + 1)
                end(pe.matmul(view(name, 512), headones[:, :], sq[:, :, :], start=True, stop=True), name)
                name = ("bo", it)
                begin(name)
                pe.wait_ge(bprod_ready, it + 1)
                end(pe.matmul(view(name, 512), headones[:, :], bp[:, :, :], start=True, stop=True), name)

            def round_(it):
                par = it % 2
                plan = between(it)

                def more(point):
                    for t in plan[point]:
                        project(*t)

                more("prep")
                pe.wait_ge(prepared, it + 1)
                for kind in "ABKV":
                    name = ("tr", it, kind)
                    begin(name)
                    for jt in range(4):
                        src = {"A": AR[:, jt, 0, :], "B": ch4["B"][:, jt, :], "K": ch4["K"][:, jt, :],
                               "V": uv[:, par, jt // 2, P * (jt % 2):P * (jt % 2) + P]}[kind]
                        last = pe.transpose(view(name, 4, P)[:, jt, :], src, ident[:, :])
                    end(last, name)
                for kind in "BK":
                    for hh in range(2):
                        r = slice(HN * hh, HN * hh + HN)
                        for uu in range(2):
                            name = ("L" + kind, it, hh, uu)
                            begin(name)
                            for n in range(2):
                                jt = 2 * uu + n
                                last = pe.matmul(view(name, 2, 2 * P)[:, n, :], ch4[kind.lower()][r, jt, :],
                                                 AR[r, jt, :, :], start=True, stop=True)
                            end(last, name)
                for hh in range(2):
                    r = slice(HN * hh, HN * hh + HN)
                    name = ("LL", it, hh)
                    begin(name)
                    for jt in range(4):
                        last = pe.matmul(view(name, 4, P)[:, jt, :], AR[r, jt, 0, :], ch4["b"][r, jt, :], start=True, stop=True)
                    end(last, name)

                def items(hh_first=False):
                    return [(hh, jt, 4 * hh + jt) for hh in range(2) for jt in range(4)]

                name = ("X", it)
                begin(name)
                await_drained(pe, ("LK", it, 1, 1))
                await_drained(pe, ("tr", it, "V"))
                for hh, jt, i in items():
                    c = slice(HN * hh, HN * hh + HN)
                    last = pe.matmul(view(name, 4, P)[:, jt, c], mats["Lak"][:, i, :], tm["V"][:, jt, c], start=True, stop=True)
                end(last, name)
                before_lev = None
                for lev in LEVELS[1:]:
                    for g in range(4):
                        name = ("Z", it, lev, g)
                        begin(name)
                        if before_lev is None:
                            await_drained(pe, ("LL", it, g // 2))
                        else:
                            await_drained(pe, ("TG", it, before_lev, g))
                        for n in range(2):
                            last = pe.matmul(view(name, 2, P)[:, n, :], mats["N"][:, 2 * g + n, :], mats["T"][:, 2 * g + n, :],
                                             start=True, stop=True)
                        end(last, name)
                    for g in range(4):
                        name = ("TG", it, lev, g)
                        begin(name)
                        await_drained(pe, ("Z", it, lev, g))
                        for n in range(2):
                            Gm, Zm = mats["G"][:, 2 * g + n, :], mats["Z"][:, 2 * g + n, :]
                            if lev != LEVELS[-1]:
                                pe.matmul(view(name, 4, P)[:, n, :], Gm, Zm, start=True, stop=True)
                            last = pe.matmul(view(name, 4, P)[:, 2 + n, :], Zm, Gm, start=True, stop=True)
                        end(last, name)
                    before_lev = lev
                name = ("Q", it)
                begin(name)
                for g in range(4):
                    await_drained(pe, ("TG", it, LEVELS[-1], g))
                await_drained(pe, ("X", it))
                for hh, jt, i in items():
                    c = slice(HN * hh, HN * hh + HN)
                    last = pe.matmul(view(name, 4, P)[:, jt, c], mats["G"][:, i, :], Xs[:, jt, c], start=True, stop=True)
                end(last, name)
                name = ("PT", it)
                begin(name)
                await_drained(pe, ("tr", it, "A"))
                for hh, jt, i in items():
                    c = slice(HN * hh, HN * hh + HN)
                    last = pe.matmul(view(name, 4, P)[c, jt, :], tm["A"][:, jt, c], mats["G"][:, i, :], start=True, stop=True)
                end(last, name)
                more("pt")

                def update(c):
                    tt, h = c // 2, slice(CH * (c % 2), CH * (c % 2) + CH)
                    name = ("U", it, c)
                    begin(name)
                    await_drained(pe, ("PT", it))
                    await_drained(pe, ("S", it, c - 1))
                    for j in range(2):
                        last = pe.matmul(view(name, 2, P)[h, j, :], PTs[:, 2 * j + tt, h], Ss[:, c - 1, j, :], start=True, stop=True)
                    end(last, name)

                def state(c):
                    tt, h = c // 2, slice(CH * (c % 2), CH * (c % 2) + CH)
                    name = ("S", it, c)
                    begin(name)
                    if c == 0:
                        pe.wait_ge(u0_ready, it + 1)
                    else:
                        await_drained(pe, ("U", it, c))
                    for j in range(2):
                        o = view(name, 2, P)[:, j, :]
                        pe.matmul(o, tm["K"][h, 2 * j + tt, :], tm["V"][h, 2 * j + tt, :], start=True, stop=False)
                        last = pe.matmul(o, tm["B"][h, 2 * j + tt, :], Us[h, 2 * j + tt, :], start=False, stop=True)
                    end(last, name)

                gla_scores(it)
                state(0)
                gla_state(it, 0)
                more("s0")
                update(1)
                gla_state(it, 1)
                more("u1")
                state(1)
                gla_state(it, 2)
                more("s1")
                update(2)
                gla_out(it)
                more("u2")
                state(2)
                more("s2")
                update(3)
                gla_norm(it)
                more("u3")
                name = ("y", it)
                begin(name)
                await_drained(pe, ("U", it, NCH - 1))
                for jt in range(4):
                    j, tt = jt // 2, jt % 2
                    for hh in range(2):
                        c = slice(HN * hh, HN * hh + HN)
                        pe.matmul(view(name, 4, P)[c, jt, :], tm["V"][:, jt, c], mats["Mrk"][:, 4 * hh + jt, :],
                                  start=True, stop=False, skip_group_check=True)
                    for c in range(max(1, 2 * tt), 2 * tt + 2):
                        h = slice(CH * (c % 2), CH * (c % 2) + CH)
                        pe.matmul(view(name, 4, P)[:, jt, h], Ss[:, c - 1, j, :], AR[:, jt, 1, h], start=False, stop=False,
                                  skip_group_check=True)
                    for hh in range(2):
                        c = slice(HN * hh, HN * hh + HN)
                        last = pe.matmul(view(name, 4, P)[c, jt, :], Us[:, jt, c], mats["Mrb"][:, 4 * hh + jt, :],
                                         start=False, stop=True, skip_group_check=True)
                end(last, name)
                if it + 1 < ITERS:
                    ranks(it + 1)
                more("y")
                name = ("mean", it)
                begin(name)
                await_drained(pe, ("y", it))
                end(pe.matmul(view(name, 512), headones[:, :], ys[:, :, :], start=True, stop=True), name)
                more("mean")
                name = ("var", it)
                begin(name)
                pe.wait_ge(ysq_ready, it + 1)
                end(pe.matmul(view(name, 512), headones[:, :], Wi[:, :, :], start=True, stop=True), name)
                more("var")
                if it + 1 < ITERS:
                    norms(it + 1)

            def gla_scores(it):
                name = ("gs", it)
                begin(name)
                pe.wait_ge(gprep_ready, it + 1)
                for tt in range(NT):
                    c = slice(P * tt, P * tt + P)
                    last = pe.matmul(view(name, 2, P)[:, tt, :], gprod[1][:, c], gprod[0][:, c], start=True, stop=True)
                end(last, name)
                name = ("gk", it)
                begin(name)
                for tt in range(NT):
                    last = pe.transpose(view(name, 2, P)[:, tt, :], gprod[3][:, P * tt:P * tt + P], ident[:, :])
                end(last, name)

            def gla_state(it, c):
                tt, h = c // 2, slice(CH * (c % 2), CH * (c % 2) + CH)
                name = ("gS", it, c)
                begin(name)
                await_drained(pe, ("gk", it))
                end(pe.matmul(view(name, T), gkt[h, tt, :], gv[h, it % 2, tt, :], start=True, stop=True), name)

            def gla_out(it):
                par = it % 2
                name = ("go", it)
                begin(name)
                await_drained(pe, ("gs", it))
                await_drained(pe, ("gS", it, NCH - 2))
                for dv in range(2):
                    for tt in range(NT):
                        o = view(name, 2, T)[:, dv, P * tt:P * tt + P]
                        last = pe.matmul(o, gv[:, par, tt, P * dv:P * dv + P], gsT[:, tt, :], start=True, stop=False,
                                         skip_group_check=True)
                        for c in range(max(1, 2 * tt), 2 * tt + 2):
                            last = pe.matmul(view(name, 2, T)[:, dv, CH * c:CH * c + CH], gSt[:, c - 1, P * dv:P * dv + P],
                                             gprod[2][:, CH * c:CH * c + CH], start=False, stop=True, skip_group_check=True)
                end(last, name)

            def gla_norm(it):
                name = ("gn", it)
                begin(name)
                pe.wait_ge(gsq_ready, it + 1)
                for dv in range(2):
                    last = pe.matmul(view(name, T), ones[:, :], dsh[:, 2 + dv, :], start=(dv == 0), stop=(dv == 1))
                end(last, name)

            for j in range(2):
                project("lora", 0, j)
            project("lr", 0, 0)
            for kind in ROUND:
                for j in range(2):
                    project(kind, 0, j)
            ranks(0)
            norms(0)
            for it in range(ITERS):
                round_(it)
            pe.wait_ge(yA_ready, ITERS)
            pe.wait_ge(yB_ready, ITERS)
            for m in range(KD):
                for key, kind, src in (("ba", "wa", yA), ("bb", "wb", yB)):
                    w = weights(kind, m // 2)
                    name = (key, m)
                    begin(name)
                    for k in range(KD):
                        last = pe.matmul(view(name, T), w[:, k, P * (m % 2):P * (m % 2) + P], src[:, k, :],
                                         start=(k == 0), stop=(k == KD - 1))
                    end(last, name)
                if m % 2:
                    release(("ba", m))
                    release(("bb", m))
            def turn_x(c):
                name = ("h2T", c)
                begin(name)
                for tt in range(NT):
                    await_drained(pe, ("out", c, tt))
                for k in range(2):
                    for tt in range(NT):
                        d0 = P * (2 * c + k)
                        last = pe.transpose(view(name, 2, NT, P)[:, k, tt, :], xs[:, tt, d0:d0 + P], ident[:, :])
                end(last, name)

            pe.wait_ge(merged_ready, KD)
            for m in range(4):
                w = weights("wo", m)
                for tt in range(NT):
                    name = ("out", m, tt)
                    begin(name)
                    for k in range(KD):
                        last = pe.matmul(view(name, T), gates[:, k, P * tt:P * tt + P], w[:, k, :],
                                         start=(k == 0), stop=(k == KD - 1))
                    end(last, name)
                release(("out", m, 1))
                if m:
                    turn_x(m - 1)

            turn_x(3)
            pe.wait_ge(x1_ready, 1)
            name = ("log",)
            begin(name)
            for c in range(4):
                await_drained(pe, ("h2T", c))
            for tt in range(NT):
                for k in range(KD):
                    last = pe.matmul(view(name, NT, E)[:, tt, :], h2T[:, k, P * tt:P * tt + P], rw[:, k, :],
                                     start=(k == 0), stop=(k == KD - 1))
            end(last, name)
            pe.wait_ge(mask_sel, 1)
            name = ("pos",)
            begin(name)
            pe.matmul(view(name, NT, E)[:, 0, :], before[:, :], selM[:, 0, :], start=True, stop=True)
            pe.matmul(view(name, NT, E)[:, 1, :], ones[:, :], selM[:, 0, :], start=True, stop=False)
            end(pe.matmul(view(name, NT, E)[:, 1, :], before[:, :], selM[:, 1, :], start=False, stop=True), name)
            def gather(i):
                pe.wait_ge(sel_ready, i + 1)
                wait_after(pe, xg_ready, i)
                o = banks[0][:, :].rearrange("p (k s) -> p k s", k=KD)
                for k in range(KD):
                    for tt in range(NT):
                        last = pe.matmul(o[:, k, :], h2[:, tt, P * k:P * k + P], sel[:, tt, :], start=(tt == 0), stop=(tt == NT - 1))
                last.then_inc(gather_done, 1)

            def counts_and_biases():
                name = ("cnt",)
                begin(name)
                pe.matmul(view(name, E), ones[:, :], selM[:, 0, :], start=True, stop=False)
                end(pe.matmul(view(name, E), ones[:, :], selM[:, 1, :], start=False, stop=True), name)
                name = ("gT",)
                begin(name)
                pe.wait_ge(gatev_ready, 1)
                for tt in range(NT):
                    last = pe.transpose(view(name, T)[0:E, P * tt:P * tt + P], rt[:, 5, tt, :], ident[:, :])
                end(last, name)
                for n in range(4):
                    name = ("b2", n)
                    begin(name)
                    await_drained(pe, ("gT",))
                    end(pe.matmul(view(name, 512), gT[:, P * (n // 2):P * (n // 2) + P],
                                  b2s[:, 512 * (n % 2):512 * (n % 2) + 512], start=True, stop=True), name)
                for b in range(8):
                    pe.wait_ge(drained[b], fills[b])

            def turn(i):
                pe.wait_ge(selg_ready, i * 2 + 2)
                wait_after(pe, selgT_ready, i)
                for tt in range(NT):
                    last = pe.transpose(banks[3][:, P * tt:P * tt + P], selg[:, tt, :, :].rearrange("p a b -> p (a b)"), ident[:, :])
                last.then_inc(selT_done, 1)

            def expert(i):
                wait_after(pe, lin_ready, i * 2)
                pe.wait_ge(xg_ready, i + 1)
                pe.wait_ge(ehot_ready, i + 1)
                for j in range(4):
                    pe.matmul(banks[1 + j // 2][64 * (j % 2):64 * (j % 2) + 64, :], ehot[:, :], b1s[:, 512 * j:512 * j + 512],
                              start=True, stop=False)
                for k in range(KD):
                    pe.wait_ge(w1_in[k], i * 16 + 16)
                    for j in range(4):
                        last = pe.matmul(banks[1 + j // 2][64 * (j % 2):64 * (j % 2) + 64, :], xg[:, k, :],
                                         w1s[:, k, 512 * j:512 * j + 512], start=False, stop=(k == KD - 1))
                    if k < KD - 1:
                        last.then_inc(w1_used, 1)
                    else:
                        last.then_inc(hid_done, 1)
                        pe.wait_ge(hid_done, i + 1)
                        pe.sem_inc(w1_used, 1)
                gather(i + 1)
                pe.wait_ge(act_ready, i + 1)
                wait_after(pe, actT_ready, i)
                for q in range(2):
                    for b in range(2):
                        n = 2 * q + b
                        last = pe.transpose(banks[4][:, P * n:P * n + P], act_s[:, q, P * b:P * b + P], ident[:, :])
                last.then_inc(actT_done, 1)
                first = isinstance(i, int) and i == 0
                if not first:
                    scatter(i - 1, 0)
                pe.wait_ge(actT_ready, i + 1)
                wait_after(pe, eo_ready, i)
                for f in range(FF // P):
                    if f == FF // P // 2:
                        if not first:
                            scatter(i - 1, 1)
                        turn(i)
                    q, half, b = f // 4, f // 2 % 2, f % 2
                    if f % 2 == 0:
                        pe.wait_ge(w2_in[f // 2], i * 16 + 16)
                    for dh in range(2):
                        last = pe.matmul(banks[5][64 * dh:64 * dh + 64, :], actT[:, 2 * q + b, 64 * half:64 * half + 64],
                                         w2s[:, f, 512 * dh:512 * dh + 512], start=(f == 0), stop=(f == FF // P - 1))
                    if f % 2:
                        if f < FF // P - 1:
                            last.then_inc(w2_used, 1)
                        else:
                            last.then_inc(eo_done, 1)
                            pe.wait_ge(eo_done, i + 1)
                            pe.sem_inc(w2_used, 1)

            def scatter(i, tt):
                if tt == 0:
                    pe.wait_ge(eo_ready, i + 1)
                    pe.wait_ge(selgT_ready, i + 1)
                if not (isinstance(i, int) and i == 0 and tt == 0):
                    pe.wait_ge(y_added, i * 4 + 2 * tt)
                spread(tt).then_inc(y_done, 1)

            def spread(tt):
                for dh in range(2):
                    r = slice(64 * dh, 64 * dh + 64)
                    last = pe.matmul(banks[6 + dh][:, :], selgT[r, tt, :], eo[r, :], start=True, stop=True)
                return last

            pe.wait_ge(late_in, 6 * 16)
            pe.wait_ge(h2_ready, 2)
            gather(0)
            counts_and_biases()
            expert(0)
            with pe.Fori(1, E) as i:
                expert(i)
            pe.wait_ge(route_ready, 1)
            most = pe.value_load(over[0:1, 0:1], min_val=0, max_val=T)
            with pe.If(most > SLOTS):
                with pe.Fori(E, PASSES * E) as i:
                    expert(i)
                pe.wait_ge(eo_ready, PASSES * E)
                pe.wait_ge(selgT_ready, PASSES * E)
                pe.wait_ge(y_added, 4 * (PASSES * E - 1))
            pe.wait_ge(eo_ready, E)
            pe.wait_ge(selgT_ready, E)
            pe.wait_ge(y_added, 4 * (E - 1))
            for tt in range(NT):
                if tt:
                    pe.wait_ge(last_added, 2 * tt)
                spread(tt).then_inc(last_scattered, 1)


_INS = ['x', 'norm_mix_g', 'w_in', 'gla_gate_up', 'gla_gate_bias', 'gla_norm_g', 'rwkv_mu', 'rwkv_w0', 'rwkv_w2', 'rwkv_a0',
        'rwkv_a2', 'rwkv_g2', 'rwkv_k_k', 'rwkv_k_a', 'rwkv_r_k', 'rwkv_ln_w', 'rwkv_ln_b', 'w_branch_a', 'w_branch_b',
        'w_out', 'norm_ffn_g', 'router_w', 'router_b', 'expert_w1', 'expert_b1', 'expert_w2', 'expert_b2', 'norm_final_g']
_OUTS = [((1, 256, 1024), 'float32')]


def kernel(**inputs):
    import numpy as _np
    import concourse.bacc as _bacc
    from concourse import mybir as _mybir
    from concourse.bass_utils import run_bass_kernel_spmd as _run

    nc = _bacc.Bacc("TRN2", target_bir_lowering=False, num_devices=1)
    arrays, args = {}, []
    for name in _INS:
        a = _np.ascontiguousarray(inputs[name])
        arrays[f"in_{name}_dram"] = a
        args.append(nc.dram_tensor(f"in_{name}_dram", a.shape, _mybir.dt.from_np(a.dtype), kind="ExternalInput").ap())
    for i, (shape, dtype) in enumerate(_OUTS):
        dt = _mybir.dt.from_np(_np.dtype(dtype))
        args.append(nc.dram_tensor(f"out_{i}_dram", shape, dt, kind="ExternalOutput").ap())
    bass_hybrid_gla_rwkv7_moe_block(nc, *args)
    r = _run(nc, [arrays], core_ids=[0])
    got = tuple(r.results[0][f"out_{i}_dram"] for i in range(len(_OUTS)))
    return got[0]
```

```python
from contextlib import ExitStack

import numpy as np

import concourse.bass as bass
from concourse import mybir

ALU = mybir.AluOpType
ACT = mybir.ActivationFunctionType
F32 = mybir.dt.float32
I32 = mybir.dt.int32
F32R = mybir.dt.float32r
U8 = mybir.dt.uint8
AX_X = mybir.AxisListType.X

P = 128
T = 256
NT = T // P
D = 1024
KD = D // P
ITERS = 4
CH = 64
NCH = T // CH
HN = 64
E = 32
FF = 1024
TOPK = 4
SLOTS = 64
PASSES = T // SLOTS
KAPPA = float(np.exp(-0.5))
RMS_EPS, GLA_EPS, GN_EPS = 1e-6, 1e-5, 64e-5
TAU = 16.0
LEVELS = (1, 2, 4, 8, 16, 32)

C_Q, C_K, C_V, C_LR, C_OG = 0, 512, 1024, 2048, 2064
C_RW = 3088
C_R, C_RK, C_RV, C_LORA = C_RW, C_RW + 1024, C_RW + 2048, C_RW + 3072
C_GA, C_GB = C_RW + 3328, C_RW + 3328 + 1024
RANK = 16

R_MIXG, R_W0, R_A0, R_KK, R_KA, R_RK, R_LNW, R_LNB, R_MU, R_GB, R_NG, R_FFN = 0, 8, 16, 24, 32, 40, 48, 56, 64, 90, 94, 96
NROWS = 104
MU_R, MU_K, MU_V, MU_L = R_MU, R_MU + 8, R_MU + 16, R_MU + 24

WRING = 3
ROUND = ("rk", "rr", "rv", "qk", "gv", "og")
GATES = ("ga", "gb")
RANKS_AFTER, NORMS_AFTER = "rv", "gv"

POINTS = ("prep", "pt", "s0", "u1", "s1", "u2", "s2", "u3", "y", "mean", "var")
SHARE = (
    (2, 1, 1, 1, 1, 1, 1, 2, 0, 1, 1),
    (3, 1, 1, 1, 1, 1, 1, 1, 0, 1, 1),
    (2, 1, 1, 1, 1, 1, 1, 2, 0, 1, 1),
    (4, 1, 1, 1, 1, 1, 1, 1, 1, 1, 3),
)
VECTOR_SPLITS = (("rk", 0), ("rv", 0))


LAST_BANKS = (6, 1)


def weight_blocks():
    blocks = [("lora", 0), ("lr", 0)]
    blocks += [(kind, it) for it in range(ITERS) for kind in ROUND]
    blocks += [(kind, it) for it in range(ITERS) for kind in GATES]
    for m in range(4):
        blocks += [("wa", m), ("wb", m)]
    return blocks + [("wo", m) for m in range(4)]


def between(it):
    last = it == ITERS - 1
    if last:
        tiles = [(kind, n, j) for n in range(ITERS) for kind in GATES for j in range(2)]
    else:
        tiles = [(kind, it + 1, j) for kind in ROUND for j in range(2)]
    plan = {}
    for point, count in zip(POINTS, SHARE[it]):
        plan[point], tiles = tiles[:count], tiles[count:]
    assert not tiles
    return plan


def fill_order():
    low, order = set(), []

    def z(name):
        low.add(name)
        order.append(name)

    order.append(("par",))
    order.extend(("hT", c) for c in range(KD // 2))

    def ranks(it):
        order.extend([("lw", it), ("la", it), ("lg", it), ("gl", it)])

    for j in range(2):
        z(("z", "lora", 0, j))
    z(("z", "lr", 0, 0))
    for kind in ROUND:
        for j in range(2):
            z(("z", kind, 0, j))
        if kind == RANKS_AFTER:
            ranks(0)
        if kind == NORMS_AFTER:
            order.extend([("kn", 0), ("bo", 0)])
    for it in range(ITERS):
        plan = between(it)

        def more(point):
            for kind, n, j in plan[point]:
                z(("z", kind, n, j))

        more("prep")
        order.extend((("tr", it, kind) for kind in "ABKV"))
        for kind in "BK":
            for hh in range(2):
                for u in range(2):
                    order.append(("L" + kind, it, hh, u))
        order.extend(("LL", it, hh) for hh in range(2))
        order.append(("X", it))
        for lev in LEVELS[1:]:
            order.extend(("Z", it, lev, g) for g in range(4))
            order.extend(("TG", it, lev, g) for g in range(4))
        order.extend([("Q", it), ("PT", it)])
        more("pt")
        order.extend([("gs", it), ("gk", it), ("S", it, 0), ("gS", it, 0)])
        more("s0")
        order.extend([("U", it, 1), ("gS", it, 1)])
        more("u1")
        order.extend([("S", it, 1), ("gS", it, 2)])
        more("s1")
        order.extend([("U", it, 2), ("go", it)])
        if it + 1 < ITERS:
            ranks(it + 1)
        more("u2")
        order.append(("S", it, 2))
        more("s2")
        order.extend([("U", it, 3), ("gn", it)])
        more("u3")
        if it + 1 < ITERS:
            order.append(("kn", it + 1))
        order.append(("y", it))
        if it + 1 < ITERS:
            order.append(("bo", it + 1))
        more("y")
        order.append(("mean", it))
        more("mean")
        order.append(("var", it))
        more("var")
    for m in range(KD):
        z(("ba", m))
        z(("bb", m))
    for m in range(4):
        for tt in range(NT):
            z(("out", m, tt))
        if m:
            order.append(("h2T", m - 1))
    order.extend([("h2T", 3), ("log",), ("pos",), ("cnt",)])
    bank, nth, used = {}, {}, [0] * 8
    turn = [0, 0]
    for name in order:
        lo = name in low
        b = turn[0] % 4 if lo else 4 + turn[1] % 4
        turn[0 if lo else 1] += 1
        bank[name], nth[name] = b, used[b]
        used[b] += 1
    return order, bank, nth, used


def bass_hybrid_gla_rwkv7_moe_block(
    nc, x, norm_mix_g, w_in, gla_gate_up, gla_gate_bias, gla_norm_g, rwkv_mu, rwkv_w0, rwkv_w2, rwkv_a0,
    rwkv_a2, rwkv_g2, rwkv_k_k, rwkv_k_a, rwkv_r_k, rwkv_ln_w, rwkv_ln_b, w_branch_a, w_branch_b, w_out,
    norm_ffn_g, router_w, router_b, expert_w1, expert_b1, expert_w2, expert_b2, norm_final_g, out, debug=None,
):
    order, bank_of, nth_of, fills = fill_order()
    blocks = weight_blocks()
    block_index = {b: n for n, b in enumerate(blocks)}

    with ExitStack() as ctx:
        def sem(name):
            return ctx.enter_context(nc.semaphore(name))

        def keep(name, shape, dt=F32):
            return ctx.enter_context(nc.sbuf_tensor(name, shape, dt))

        banks = [ctx.enter_context(nc.psum_tensor(f"bank{b}", [P, 512], F32)) for b in range(8)]

        def over_next(name, shape):
            with nc.sbuf_tensor(name, shape, F32R) as t:
                return t

        hT_hi = over_next("hT_hi", [P, KD, T])
        xs = keep("xs", [P, NT, D])
        ident = keep("ident", [P, P])
        ones = keep("ones", [P, P])
        headones = keep("headones", [P, P])
        before = keep("before", [P, P])
        stat = keep("stat", [P, 24])
        ffn_col = keep("ffn_col", [P, KD])
        epsc = keep("epsc", [P, 4])

        mix = ExitStack()

        def sb(name, shape, dt=F32):
            return mix.enter_context(nc.sbuf_tensor(name, shape, dt))

        w_lo = over_next("w_lo", [P, WRING, KD, 256])
        wring = sb("wring", [P, WRING, KD, 256])
        w_hi = over_next("w_hi", [P, 2, KD, 256])
        gates = sb("gates", [P, 16, T])
        gates_end = nc.sbuf_base
        yA = sb("yA", [P, KD, T])
        yB = sb("yB", [P, KD, T])
        kept_to_end = nc.sbuf_base
        hT_lo = over_next("hT_lo", [P, KD, T])
        hT = sb("hT", [P, KD, T])
        prow = sb("prow", [P, P])
        pcol = sb("pcol", [P, NROWS])
        w2a2 = sb("w2a2", [P, D])
        g2 = sb("g2", [P, D])
        gup = sb("gup", [RANK, 512])
        below = sb("below", [P, P])
        upto = sb("upto", [P, P])
        upto8 = sb("upto8", [P, P], U8)
        low8 = sb("low8", [P, len(LEVELS), P], U8)
        up8 = sb("up8", [P, len(LEVELS), P], U8)
        chunkmask = sb("chunkmask", [P, 2 * T])
        zl = sb("zl", [P, 2, T + 1])
        ul = sb("ul", [P, 2, T])
        zlr = sb("zlr", [RANK, T])
        zs = sb("zs", [P, 6, T + 1])
        dsh = sb("dsh", [P, 6, T])
        u = sb("u", [P, 4, T])
        uv = sb("uv", [P, 2, 2, T])
        gg = sb("gg", [P, 2, 2, T])
        sgw = sb("sgw", [P, 2, T])
        aa = sb("aa", [P, 2, T])
        cc = sb("cc", [P, 2, T])
        cm = sb("cm", [P, 2, T])
        Wc = cc
        Wi = sb("Wi", [P, 2, T])
        Wp = cm
        kk0 = sb("kk0", [P, 2, T])
        sq = sb("sq", [P, 2, T])
        km = sb("km", [P, 2, T])
        bp = sb("bp", [P, 2, T])
        bon = sb("bon", [P, 2, T])
        ch4 = {k: sb("ch" + k, [P, 4, P]) for k in "bkBK"}
        AR = sb("AR", [P, 4, 2, P])
        tm = {k: sb("tm" + k, [P, 4, P]) for k in "ABKV"}
        mats = {k: sb("m" + k, [P, 8, P]) for k in ("N", "T", "G", "Z", "Mrb", "Mrk")}
        mats["Lak"] = mats["Z"]
        Xs = sb("Xs", [P, 4, P])
        Qs = sb("Qs", [P, 4, P])
        PTs = sb("PTs", [P, 4, P])
        Us = Xs
        Ss = sb("Ss", [P, NCH - 1, 2, P])
        ys = sb("ys", [P, 2, T])
        gq = sb("gq", [P, 2, T])
        gk = sb("gk", [P, 2, T])
        gv = sb("gv", [P, 2, NT, T])
        og = sb("og", [P, 2, 2, T])
        gx = sb("gx", [P, 2, T])
        halves = {k: ch4[k][:, :, :].rearrange("p a t -> p (a t)").rearrange("p (a t) -> p a t", t=T) for k in "bk"}
        gprod = [halves["b"][:, 0, :], halves["b"][:, 1, :], halves["k"][:, 0, :], halves["k"][:, 1, :]]
        gtmp = [dsh[:, n, :] for n in (0, 1, 3, 4)]
        gsT = mats["N"][:, 0:2, :]
        gkt = mats["N"][:, 2:4, :]
        gSt = mats["Z"][:, :, :].rearrange("p (c a) t -> p c (a t)", a=2)
        gos = mats["N"][:, 4:8, :]
        xn = yA[:, :, :].rearrange("p a b -> p (a b)").rearrange("p (a d) -> p a d", a=NT)
        ys4 = ys[:, :, :].rearrange("p j (a t) -> p (j a) t", t=P)
        ysd = mats["Z"][:, 0:4, :]

        ints = og[:, :, :, :].rearrange("p a b t -> p (a b t)").bitcast(I32).rearrange("p (a t) -> p a t", t=P)
        mix.close()

        moe = ctx.enter_context(ExitStack())

        def mb(name, shape, dt=F32):
            return moe.enter_context(nc.sbuf_tensor(name, shape, dt))

        h2 = mb("h2", [P, NT, D])
        h2T = mb("h2T", [P, KD, T])
        acc = xs
        lg = mb("lg", [P, NT, E])
        top = mb("top", [P, NT, 8])
        rt = mb("rt", [P, 6, NT, E])
        selM = mb("selM", [P, NT, E])
        posm = mb("posm", [P, E, NT])
        gatev = mb("gatev", [P, E, NT])
        rs = mb("rs", [P, 16])
        over = mb("over", [P, 1], I32)
        iota = mb("iota", [P, (PASSES + 1) * SLOTS])
        onesE = mb("onesE", [E, SLOTS])
        ehot = mb("ehot", [E, SLOTS])
        sel = mb("sel", [P, NT, SLOTS])
        selg = mb("selg", [P, NT, 2, SLOTS])
        selgT = mb("selgT", [P, NT, P])
        xg = mb("xg", [P, KD, SLOTS])
        glu = mb("glu", [P, 2, 256])
        sgm = mb("sgm", [P, 2, 256])
        lin = mb("lin", [P, 2, 256])
        act_s = mb("act_s", [P, 2, 256])
        actT = mb("actT", [P, 4, P])
        eo = mb("eo", [P, 512])
        mb("skipped_gates", [P, (gates_end - nc.sbuf_base) // 4])
        b1s = mb("b1s", [E, 2 * FF])
        b2s = mb("b2s", [E, D])
        mb("skipped_branches", [P, (kept_to_end - nc.sbuf_base) // 4])
        w1s = mb("w1s", [P, KD, 2 * FF])
        w2s = mb("w2s", [P, FF // P, D])
        w2s_1 = mb("w2s_1", [P, FF // P, D])
        ffn_g = mb("ffn_g", [P, D])
        final_g = mb("final_g", [P, D])
        rw = mb("rw", [P, KD, E])
        rb = mb("rb", [P, E])

        filled = [sem(f"bank{b}_filled") for b in range(8)]
        drained = [sem(f"bank{b}_drained") for b in range(8)]
        x_in, rows_in, lora_in, late_in = sem("x_in"), sem("rows_in"), sem("lora_in"), sem("late_in")
        w_in_ready = [sem(f"weights_in{s}") for s in range(WRING)]
        w_lo_by_vector = sem("w_lo_by_vector")
        hi_ready, w_hi_ready, w_lo_ready, whole = sem("hi_ready"), sem("w_hi_ready"), sem("w_lo_ready"), sem("whole")
        dve_step, act_step, pool_step = sem("dve_step"), sem("act_step"), sem("pool_step")
        raw_consts, consts_ready = sem("raw_consts"), sem("consts_ready")
        ident_ready, bon_ready = sem("ident_ready"), sem("bon_ready")
        sumsq_ready, rstd_ready, xn_ready = sem("sumsq_ready"), sem("rstd_ready"), sem("xn_ready")
        lora_mixed, lora_act = sem("lora_mixed"), sem("lora_act")
        shifted = sem("shifted")
        cum_ready, exps_ready = sem("cum_ready"), sem("exps_ready")
        ksq_ready, bprod_ready = sem("ksq_ready"), sem("bprod_ready")
        prepared = sem("prepared")
        eye_ready, u0_ready = sem("eye_ready"), sem("u0_ready")
        ysq_ready, ystd_ready, yB_ready = sem("ysq_ready"), sem("ystd_ready"), sem("yB_ready")
        softplus_ready = sem("softplus_ready")
        b_ready, gexp_ready, gprep_ready = sem("b_ready"), sem("gexp_ready"), sem("gprep_ready")
        gsq_ready, gstd_ready, yA_ready = sem("gsq_ready"), sem("gstd_ready"), sem("yA_ready")
        merged_ready, x1_ready, h2_ready = sem("merged_ready"), sem("x1_ready"), sem("h2_ready")
        mask_sel, route_ready, gexpo = sem("mask_sel"), sem("route_ready"), sem("gexpo")
        mean_ready, last_sums = sem("mean_ready"), sem("last_sums")
        lmax_ready, gatev_ready = sem("lmax_ready"), sem("gatev_ready")
        moe_pool = sem("moe_pool")
        w1_in = [sem(f"w1_in{k}") for k in range(KD)]
        w2_in = [sem(f"w2_in{k}") for k in range(4)]
        w2_1_in, bias_in, rw_ready = sem("w2_1_in"), sem("bias_in"), sem("rw_ready")
        w1_used, w2_used = sem("w1_used"), sem("w2_used")
        sel_ready, selg_ready = sem("sel_ready"), sem("selg_ready")
        gather_done, selT_done = sem("gather_done"), sem("selT_done")
        xg_ready, selgT_ready = sem("xg_ready"), sem("selgT_ready")
        hid_done, glu_ready, sgm_ready, act_ready = (
            sem("hid_done"), sem("glu_ready"), sem("sgm_ready"), sem("act_ready"))
        actT_done, actT_ready = sem("actT_done"), sem("actT_ready")
        eo_done, eo_ready = sem("eo_done"), sem("eo_ready")
        y_done, y_added = sem("y_done"), sem("y_added")
        final_ready, out_done = sem("final_ready"), sem("out_done")

        def view(name, *shape):
            b = banks[bank_of[name]][:, :]
            if len(shape) == 2:
                return b[:, 0:shape[0] * shape[1]].rearrange("p (a b) -> p a b", a=shape[0])
            if len(shape) == 3:
                return b[:, 0:shape[0] * shape[1] * shape[2]].rearrange("p (a b c) -> p a b c", a=shape[0], b=shape[1])
            return b[:, 0:shape[0]]

        def await_filled(eng, name):
            eng.wait_ge(filled[bank_of[name]], nth_of[name] + 1)

        def await_drained(eng, name):
            eng.wait_ge(drained[bank_of[name]], nth_of[name] + 1)

        def wait_after(eng, semaphore, value):
            if not (isinstance(value, int) and value == 0):
                eng.wait_ge(semaphore, value)

        ring_count, slot_total = [], [0] * WRING
        for n, (kind, _) in enumerate(blocks):
            slot_total[n % WRING] += 32 if kind == "qk" else 16
            ring_count.append(slot_total[n % WRING])

        def last_tile(kind, it):
            if kind in branch:
                return {"wa": ("ba", 2 * it + 1), "wb": ("bb", 2 * it + 1), "wo": ("out", it, NT - 1)}[kind]
            return ("z", kind, it, 0 if kind == "lr" else 1)

        split_blocks = block_index[("ga", 0)]

        def await_lo(eng, n):
            if blocks[n] in VECTOR_SPLITS:
                eng.wait_ge(w_lo_by_vector, VECTOR_SPLITS.index(blocks[n]) + 1)
            else:
                eng.wait_ge(w_lo_ready, sum(b not in VECTOR_SPLITS for b in blocks[:n + 1]))

        def join(eng, half):
            await_filled(eng, ("z", "og", ITERS - 1, 1))
            k = slice(KD // 2 * half, KD // 2 * half + KD // 2)
            eng.tensor_tensor(hT[:, k, :], hT_lo[:, k, :].bitcast(F32), hT_hi[:, k, :].bitcast(F32), ALU.add).then_inc(whole, 1)

        def w_parts(n):
            width = RANK if blocks[n][0] == "lr" else 256
            return w_hi[:, n % 2, :, 0:width], w_lo[:, n % WRING, :, 0:width], wring[:, n % WRING, :, 0:width]

        def wslot(kind, it):
            return wring[:, block_index[(kind, it)] % WRING]

        def col(row):
            return pcol[:, row:row + 1]

        win = w_in[0].rearrange("(k p) n -> p k n", p=P)
        branch = {
            "wa": w_branch_a[0].rearrange("(k p) n -> p k n", p=P),
            "wb": w_branch_b[0].rearrange("(k p) n -> p k n", p=P),
            "wo": w_out[0].rearrange("(k p) n -> p k n", p=P),
        }

        ehot_ready, last_scattered, last_added = sem("ehot_ready"), sem("last_scattered"), sem("last_added")
        glu_half, lin_ready, gated_ready = sem("glu_half"), sem("lin_ready"), sem("gated_ready")

        block = ctx.enter_context(nc.Block())

        @block.sync
        def _(sp):
            sp.dma_start(xs[:, :, :], x[0].rearrange("(a p) d -> p a d", p=P)).then_inc(x_in, 16)
            rows = [
                (R_MIXG, 8, norm_mix_g[0]), (R_W0, 8, rwkv_w0[0]), (R_A0, 8, rwkv_a0[0]), (R_KK, 8, rwkv_k_k[0]),
                (R_KA, 8, rwkv_k_a[0]), (R_RK, 8, rwkv_r_k[0].rearrange("h n -> (h n)")), (R_LNW, 8, rwkv_ln_w[0]),
                (R_LNB, 8, rwkv_ln_b[0]), (R_MU, 26, rwkv_mu[0]), (R_GB, 4, gla_gate_bias[0]), (R_NG, 2, gla_norm_g[0]),
                (R_FFN, 8, norm_ffn_g[0]),
            ]
            for r0, n, src in rows:
                sp.dma_start(prow[r0:r0 + n, :], src.rearrange("(r c) -> r c", c=P)).then_inc(rows_in, 16)
            w1v = expert_w1[0].rearrange("e (k p) n -> e p k n", p=P)
            w2v = expert_w2[0].rearrange("e (k p) n -> e p k n", p=P)

            def load_slab(i, n):
                e = i if isinstance(i, int) else i % E
                if n < KD:
                    if not (isinstance(i, int) and i == 0):
                        sp.wait_ge(w1_used, (i - 1) * KD + (n + 1))
                    sp.dma_start(w1s[:, n, :], w1v[bass.ds(e, 1), :, n, :].rearrange("a p n -> (a p) n")).then_inc(w1_in[n], 16)
                else:
                    k = n - KD
                    if not isinstance(i, int):
                        sp.wait_ge(w2_used, (i - 2) * 4 + (k + 1))
                    sp.dma_start(w2s[:, 2 * k:2 * k + 2, :],
                                 w2v[bass.ds(e, 1), :, 2 * k:2 * k + 2, :].rearrange("a p k n -> (a p) k n")).then_inc(w2_in[k], 16)

            first_spread = block_index[("wb", 1)]
            slabs_after = dict(zip(range(first_spread, len(blocks)), ((), (0,), (1,), (2,), (3,), (4,), (5, 6), (7, 8), (9, 10, 11))))

            for n, (kind, it) in enumerate(blocks):
                if n >= WRING:
                    await_filled(sp, last_tile(*blocks[n - WRING]))
                if (kind, it) == ("wa", 0):
                    sp.wait_ge(whole, 2)
                    sp.dma_start(xs[:, :, :], x[0].rearrange("(a p) d -> p a d", p=P)).then_inc(x_in, 16)
                dst = wring[:, n % WRING]
                ready = w_in_ready[n % WRING]
                if kind in branch:
                    sp.dma_start(dst, branch[kind][:, :, 256 * it:256 * it + 256]).then_inc(ready, 16)
                elif kind == "qk":
                    sp.dma_start(dst[:, :, 0:P], win[:, :, C_Q + P * it:C_Q + P * it + P]).then_inc(ready, 16)
                    sp.dma_start(dst[:, :, P:2 * P], win[:, :, C_K + P * it:C_K + P * it + P]).then_inc(ready, 16)
                else:
                    first = {"lora": C_LORA, "lr": C_LR, "rk": C_RK, "rr": C_R, "rv": C_RV, "gv": C_V, "og": C_OG,
                             "ga": C_GA, "gb": C_GB}[kind] + 256 * it
                    width = RANK if kind == "lr" else 256
                    sp.dma_start(dst[:, :, 0:width], win[:, :, first:first + width]).then_inc(ready, 16)
                for slab in slabs_after.get(n, ()):
                    load_slab(0, slab)
                if n == first_spread:
                    sp.wait_ge(yA_ready, ITERS)
                    sp.wait_ge(yB_ready, ITERS)
                    sp.dma_start(rw[:, :, :], router_w[0].rearrange("(k p) e -> p k e", p=P)).then_inc(late_in, 16)
                    sp.dma_start(rb[:, :], router_b.broadcast_to([P, E])).then_inc(late_in, 16)
                    sp.dma_start(ffn_g[:, :], norm_ffn_g.broadcast_to([P, D])).then_inc(late_in, 16)
                    sp.dma_start(final_g[:, :], norm_final_g.rearrange("(a d) -> a d", a=1).broadcast_to([P, D])).then_inc(late_in, 16)
                if (kind, it) == ("wo", 2):
                    sp.dma_start(b1s[:, :], expert_b1[0]).then_inc(bias_in, 16)
                    sp.dma_start(b2s[:, :], expert_b2[0]).then_inc(bias_in, 16)
                if n == 1:
                    sp.dma_start(w2a2[0:64, :], rwkv_w2[0]).then_inc(lora_in, 16)
                    sp.dma_start(w2a2[64:128, :], rwkv_a2[0]).then_inc(lora_in, 16)
                    sp.dma_start(g2[:, :], rwkv_g2[0]).then_inc(lora_in, 16)
                    sp.dma_start(gup[:, :], gla_gate_up[0]).then_inc(lora_in, 16)
            for k in range(2):
                sp.dma_start(w2s_1[:, 4 * k:4 * k + 4, :], w2v[1, :, 4 * k:4 * k + 4, :]).then_inc(w2_1_in, 16)
            for n in range(KD):
                load_slab(1, n)
            with sp.Fori(2, E) as i:
                for n in range(KD + 4):
                    load_slab(i, n)
            sp.wait_ge(route_ready, 1)
            most = sp.value_load(over[0:1, 0:1], min_val=0, max_val=T)
            with sp.If(most > SLOTS):
                with sp.Fori(E, PASSES * E) as i:
                    for n in range(KD + 4):
                        load_slab(i, n)
            fin = h2T[:, :, :].rearrange("p a b -> p (a b)").rearrange("p (a d) -> p a d", a=NT)
            for tt in range(NT):
                sp.wait_ge(final_ready, tt + 1)
                sp.dma_start(out[0, P * tt:P * tt + P, :], fin[:, tt, :]).then_inc(out_done, 16)
            sp.wait_ge(out_done, NT * 16)

        @block.gpsimd
        def _(pool):
            steps = [0]

            def link(ins):
                steps[0] += 1
                ins.then_inc(pool_step, 1)
                pool.wait_ge(pool_step, steps[0])

            pool.memset(ones[:, :], 1.0).then_inc(raw_consts, 1)
            pool.iota(ints[:, 0, :], [[0, P]], 0, 1).then_inc(raw_consts, 1)
            pool.iota(ints[:, 1, :], [[1, P]], 0, 0).then_inc(raw_consts, 1)
            pool.memset(zs[:, :, 0:1], 0.0).then_inc(raw_consts, 1)
            pool.memset(zl[:, :, 0:1], 0.0).then_inc(raw_consts, 1)
            pool.memset(Ss[:, :, :, :], 0.0).then_inc(raw_consts, 1)
            pool.memset(chunkmask[:, :], 1.0).then_inc(raw_consts, 1)
            pool.wait_ge(raw_consts, 7)
            pool.memset(chunkmask[:, :].rearrange("p (c t) -> p c t", t=CH)[:, :, 0:1], 0.0).then_inc(raw_consts, 1)
            pool.memset(epsc[:, 0:1], RMS_EPS).then_inc(raw_consts, 1)
            pool.memset(epsc[:, 1:2], GLA_EPS).then_inc(raw_consts, 1)
            pool.memset(epsc[:, 2:3], GN_EPS).then_inc(raw_consts, 1)

            def inverses_start(it):
                if it:
                    await_filled(pool, ("PT", it - 1))
                for k in "TG":
                    pool.tensor_copy(mats[k][:, :, :], ident[:, :].unsqueeze(1).broadcast_to([P, 8, P])).then_inc(eye_ready, 1)

            def gla_end(it):
                await_drained(pool, ("go", it))
                link(pool.tensor_tensor(og[:, it % 2, :, :], og[:, it % 2, :, :], gos.rearrange("p (j a) t -> p j (a t)", a=2), ALU.mult))
                pool.wait_ge(gstd_ready, it + 1)
                link(pool.tensor_tensor(dsh[:, 2:4, :], og[:, it % 2, :, :], dsh[:, 4:5, :].broadcast_to([P, 2, T]), ALU.mult))
                for j in range(2):
                    ins = pool.tensor_scalar(yA[:, 2 * it + j, :], dsh[:, 2 + j, :], col(R_NG + j), None, ALU.mult)
                    if j == 0:
                        link(ins)
                    else:
                        ins.then_inc(yA_ready, 1)

            def bonus(it):
                await_drained(pool, ("bo", it))
                pool.tensor_tensor(bon[:, :, :], bp[:, :, :], uv[:, it % 2, :, :], ALU.mult).then_inc(bon_ready, 1)

            def rwkv_end(it):
                pool.wait_ge(ystd_ready, it + 1)
                pool.wait_ge(bon_ready, it + 1)
                link(pool.tensor_tensor(ys4, ys4, ysd, ALU.mult))
                for j in range(2):
                    link(pool.tensor_scalar(ys[:, j, :], ys[:, j, :], col(R_LNW + 2 * it + j), col(R_LNB + 2 * it + j),
                                            ALU.mult, ALU.add))
                link(pool.tensor_tensor(ys[:, :, :], ys[:, :, :], bon[:, :, :], ALU.add))
                pool.tensor_tensor(yB[:, 2 * it:2 * it + 2, :], ys[:, :, :], gg[:, it % 2, :, :], ALU.mult).then_inc(yB_ready, 1)

            def split_lo(kind, it):
                if (kind, it) in VECTOR_SPLITS or (kind, it) not in block_index or block_index[(kind, it)] >= split_blocks:
                    return
                n = block_index[(kind, it)]
                pool.wait_ge(w_hi_ready, n + 1)
                hi, lo, slot = w_parts(n)
                pool.tensor_tensor(lo, slot, hi.bitcast(F32), ALU.subtract).then_inc(w_lo_ready, 1)

            for kind in ("lora", "lr") + ROUND:
                split_lo(kind, 0)
            split_lo("rk", 1)
            pool.wait_ge(ident_ready, 1)
            inverses_start(0)
            bonus(0)
            split_lo("rr", 1)
            for it in range(ITERS):
                split_lo("rv", it + 1)
                split_lo("qk", it + 1)
                if it + 1 < ITERS:
                    inverses_start(it + 1)
                split_lo("gv", it + 1)
                split_lo("og", it + 1)
                split_lo("rk", it + 2)
                gla_end(it)
                split_lo("rr", it + 2)
                if it + 2 == ITERS:
                    join(pool, 0)
                rwkv_end(it)
                if it + 1 < ITERS:
                    pool.wait_ge(yB_ready, it + 1)
                    bonus(it + 1)
            pool.wait_ge(late_in, 4 * 16)
            for k in range(KD):
                pool.tensor_scalar(rw[:, k, :], rw[:, k, :], ffn_col[:, k:k + 1], None, ALU.mult).then_inc(rw_ready, 1)
            pool.wait_ge(x1_ready, 1)
            pool.iota(iota[:, :], [[1, (PASSES + 1) * SLOTS]], -4096, 0,
                      allow_small_or_imprecise_dtypes=True).then_inc(moe_pool, 1)
            pool.memset(onesE[:, :], 1.0).then_inc(moe_pool, 1)

        @block.scalar
        def _(act):
            steps = [0]

            def link(ins):
                steps[0] += 1
                ins.then_inc(act_step, 1)
                act.wait_ge(act_step, steps[0])

            def drains(ins, name):
                ins.then_inc(drained[bank_of[name]], 1)

            def split_hi(n):
                if n >= split_blocks:
                    return
                act.wait_ge(w_in_ready[n % WRING], ring_count[n])
                if n >= 2:
                    await_filled(act, last_tile(*blocks[n - 2]))
                hi, _, slot = w_parts(n)
                act.activation(hi, slot, ACT.Copy).then_inc(w_hi_ready, 1)

            act.wait_ge(x_in, 16)
            act.wait_ge(raw_consts, 11)
            for tt in range(NT):
                act.activation(hT[:, 4 * tt:4 * tt + 4, :].rearrange("p a b -> p (a b)"), xs[:, tt, :], ACT.Square,
                               accum_out=stat[:, tt:tt + 1]).then_inc(sumsq_ready, 1)
            act.wait_ge(sumsq_ready, 2)
            act.activation(stat[:, 2:4], stat[:, 0:2], ACT.Sqrt, bias=epsc[:, 0:1], scale=1.0 / D).then_inc(sumsq_ready, 1)
            act.wait_ge(rstd_ready, 1)
            act.activation(xn[:, 0, :], xs[:, 0, :], ACT.Copy, scale=stat[:, 4:5]).then_inc(xn_ready, 1)
            split_hi(0)
            split_hi(1)
            await_drained(act, ("par",))
            act.wait_ge(xn_ready, 2)
            for c in range(KD // 2):
                name = ("hT", c)
                await_filled(act, name)
                for k in range(2):
                    act.activation(hT_hi[:, 2 * c + k, :], view(name, 2, T)[:, k, :], ACT.Copy,
                                   scale=col(R_MIXG + 2 * c + k)).then_inc(hi_ready, 1)

            def take(kind, it, j):
                par = it % 2
                if kind == "rk" and j == 0 and it:
                    act.wait_ge(shifted, it)
                if kind == "qk" and j == 0 and it >= 2:
                    act.wait_ge(yA_ready, it - 1)
                name = ("z", kind, it, j)
                await_filled(act, name)
                z = view(name, T)
                if kind == "lora":
                    drains(act.activation(zl[:, j, 1:T + 1], z, ACT.Copy), name)
                elif kind == "lr":
                    drains(act.activation(zlr[:, :], z[0:RANK, :], ACT.Copy), name)
                elif kind in ("rk", "rr", "rv"):
                    at = 2 * ("rk", "rr", "rv").index(kind) + j
                    drains(act.activation(zs[:, at, 1:T + 1], z, ACT.Copy), name)
                elif kind == "qk":
                    drains(act.activation((gq, gk)[j][:, par, :], z, ACT.Copy,
                                          scale=float(P) ** -0.5 if j == 0 else 1.0), name)
                elif kind == "gv":
                    drains(act.activation(gv[:, par, j, :], z, ACT.Copy), name)
                elif kind == "og":
                    drains(act.activation(og[:, par, j, :], z, ACT.Copy), name)
                else:
                    at = (0 if kind == "ga" else KD) + 2 * it + j
                    drains(act.activation(gates[:, at, :], z, ACT.Sigmoid), name)
                if name == last_tile(kind, it):
                    split_hi(block_index[(kind, it)] + 2)

            def ranks(it):
                par = it % 2
                if it:
                    act.wait_ge(prepared, it)
                for key, dst, r0 in (("lw", sgw, R_W0), ("la", aa, R_A0)):
                    await_filled(act, (key, it))
                    link(act.activation(dst[:, 0, :], view((key, it), 2, T)[:, 0, :], ACT.Sigmoid, bias=col(r0 + 2 * it)))
                    drains(act.activation(dst[:, 1, :], view((key, it), 2, T)[:, 1, :], ACT.Sigmoid,
                                          bias=col(r0 + 2 * it + 1)), (key, it))
                await_filled(act, ("lg", it))
                if it >= 2:
                    act.wait_ge(yB_ready, it - 1)
                drains(act.activation(gg[:, par, :, :], view(("lg", it), 2, T), ACT.Copy), ("lg", it))
                await_filled(act, ("gl", it))
                drains(act.activation(gx[:, par, :], view(("gl", it), T), ACT.Identity, bias=col(R_GB + it)), ("gl", it))

            kk_n = sq[:, :, :].rearrange("p a b -> p (a b)")
            y_std = mats["Z"][:, 0:4, :].rearrange("p a b -> p (a b)")

            def key_root(it):
                await_filled(act, ("kn", it))
                act.activation(kk_n, view(("kn", it), 512), ACT.Sqrt).then_inc(drained[bank_of[("kn", it)]], 1)

            def decays(it):
                act.wait_ge(cum_ready, it + 1)
                act.activation(Wi[:, :, :], cc[:, :, :], ACT.Exp, scale=KAPPA).then_inc(exps_ready, 1)
                act.activation(Wc[:, :, :], cc[:, :, :], ACT.Exp, scale=-KAPPA).then_inc(exps_ready, 1)
                act.activation(Wp[:, :, :], cm[:, :, :], ACT.Exp, scale=-KAPPA).then_inc(exps_ready, 1)

            def bonus_sums(it):
                await_filled(act, ("bo", it))
                drains(act.activation(bp[:, :, :], view(("bo", it), 2, T), ACT.Copy), ("bo", it))

            def softplus(it):
                await_drained(act, ("gl", it))
                if it >= 1:
                    act.wait_ge(yA_ready, it)
                link(act.activation(dsh[:, 0, :], gx[:, it % 2, :], ACT.Abs))
                link(act.activation(dsh[:, 0, :], dsh[:, 0, :], ACT.Exp, scale=-1.0))
                act.activation(dsh[:, 1, :], dsh[:, 0, :], ACT.Ln, bias=1.0).then_inc(softplus_ready, 1)

            def round_(it):
                plan = between(it)

                def more(point):
                    for tile in plan[point]:
                        take(*tile)

                more("prep")
                for kind in "ABKV":
                    await_filled(act, ("tr", it, kind))
                    drains(act.activation(tm[kind][:, :, :], view(("tr", it, kind), 4, P), ACT.Copy), ("tr", it, kind))
                act.wait_ge(b_ready, it + 1)
                for k in range(4):
                    src = (dsh[:, 2, :], dsh[:, 2, :], dsh[:, 3, :], dsh[:, 4, :])[k]
                    act.activation(gtmp[k], src, ACT.Exp, scale=(-1.0 if k == 1 else 1.0) / TAU).then_inc(gexp_ready, 1)
                act.wait_ge(gexp_ready, 6 * it + 2)
                for j in range(2):
                    act.activation(dsh[:, 2 + 3 * j, :], og[:, it % 2, j, :], ACT.Sigmoid).then_inc(gexp_ready, 1)
                await_filled(act, ("X", it))
                drains(act.activation(Xs[:, :, :], view(("X", it), 4, P), ACT.Copy), ("X", it))
                for lev in LEVELS[1:]:
                    for g in range(4):
                        name = ("Z", it, lev, g)
                        await_filled(act, name)
                        drains(act.activation(mats["Z"][:, 2 * g:2 * g + 2, :], view(name, 2, P), ACT.Copy), name)
                for key, dst in (("Q", Qs), ("PT", PTs)):
                    await_filled(act, (key, it))
                    drains(act.activation(dst[:, :, :], view((key, it), 4, P), ACT.Copy), (key, it))
                more("pt")
                await_filled(act, ("gk", it))
                drains(act.activation(gkt, view(("gk", it), 2, P), ACT.Copy), ("gk", it))
                for point in ("s0", "u1", "s1"):
                    more(point)
                await_filled(act, ("go", it))
                act.activation(dsh[:, 2:4, :], view(("go", it), 2, T), ACT.Square).then_inc(gsq_ready, 1)
                drains(act.activation(gos, view(("go", it), 4, P), ACT.Copy), ("go", it))
                if it + 1 < ITERS:
                    ranks(it + 1)
                more("u2")
                more("s2")
                await_filled(act, ("gn", it))
                drains(act.activation(dsh[:, 4, :], view(("gn", it), T), ACT.Sqrt, bias=epsc[:, 1:2], scale=1.0 / 256), ("gn", it))
                more("u3")
                if it + 1 < ITERS:
                    key_root(it + 1)
                await_filled(act, ("y", it))
                if it:
                    act.wait_ge(yB_ready, it)
                drains(act.activation(ys[:, :, :], view(("y", it), 2, T), ACT.Copy), ("y", it))
                if it + 1 < ITERS:
                    decays(it + 1)
                    bonus_sums(it + 1)
                more("y")
                more("mean")
                await_filled(act, ("var", it))
                drains(act.activation(y_std, view(("var", it), 512), ACT.Sqrt, bias=epsc[:, 2:3], scale=1.0 / HN), ("var", it))
                more("var")
                if it + 1 < ITERS:
                    softplus(it + 1)

            for j in range(2):
                take("lora", 0, j)
            take("lr", 0, 0)
            for kind in ROUND:
                for j in range(2):
                    take(kind, 0, j)
                if kind == ROUND[0]:
                    act.wait_ge(lora_mixed, 1)
                    act.activation(ul[0:64, 0, :], ul[0:64, 0, :], ACT.Tanh).then_inc(lora_act, 1)
                    act.activation(ul[:, 1, :], ul[:, 1, :], ACT.Sigmoid).then_inc(lora_act, 1)
                if kind == RANKS_AFTER:
                    ranks(0)
                if kind == NORMS_AFTER:
                    key_root(0)
                    decays(0)
                    bonus_sums(0)
                    softplus(0)
            for it in range(ITERS):
                round_(it)
            for m in range(4):
                for tt in range(NT):
                    await_drained(act, ("out", m, tt))
                    act.activation(gates[:, KD + 2 * m + tt, :], xs[:, tt, 256 * m:256 * m + 256], ACT.Square,
                                   accum_out=stat[:, 16 + 4 * tt + m:17 + 4 * tt + m]).then_inc(sumsq_ready, 1)
            act.wait_ge(mean_ready, 1)
            act.activation(stat[:, 8:10], stat[:, 6:8], ACT.Sqrt, bias=epsc[:, 0:1], scale=1.0 / D).then_inc(sumsq_ready, 1)
            act.wait_ge(lmax_ready, 1)
            for tt in range(NT):
                act.activation(rt[:, 4, tt, :], lg[:, tt, :], ACT.Exp, bias=rs[:, tt:tt + 1]).then_inc(gexpo, 1)

            act.preload_act_table(ACT.Sigmoid)

            def gathered(i):
                act.wait_ge(gather_done, i + 1)
                act.activation(xg[:, :, :], banks[0][:, :].rearrange("p (k s) -> p k s", k=KD), ACT.Copy).then_inc(xg_ready, 1)

            def expert(i):
                act.wait_ge(glu_ready, i + 1)
                act.activation(sgm[:, :, :], glu[:, :, :], ACT.Sigmoid, scale=1.702).then_inc(sgm_ready, 1)
                gathered(i + 1)
                act.wait_ge(actT_done, i + 1)
                act.activation(actT[:, :, :], banks[4][:, :].rearrange("p (k s) -> p k s", k=4), ACT.Copy).then_inc(actT_ready, 1)
                act.wait_ge(eo_done, i + 1)
                act.activation(eo[:, :], banks[5][:, :], ACT.Copy).then_inc(eo_ready, 1)

            gathered(0)
            expert(0)
            with act.Fori(1, E) as i:
                expert(i)
            act.wait_ge(route_ready, 1)
            most = act.value_load(over[0:1, 0:1], min_val=0, max_val=T)
            with act.If(most > SLOTS):
                with act.Fori(E, PASSES * E) as i:
                    expert(i)
            act.preload_act_table(ACT.Sqrt)
            for tt in range(NT):
                act.wait_ge(last_added, 2 * tt + 2)
                act.activation(h2[:, tt, :], xs[:, tt, :], ACT.Square, accum_out=stat[:, 10 + tt:11 + tt]).then_inc(last_sums, 1)
                act.wait_ge(last_sums, 2 * tt + 1)
                act.activation(stat[:, 12 + tt:13 + tt], stat[:, 10 + tt:11 + tt], ACT.Sqrt, bias=epsc[:, 0:1],
                               scale=1.0 / D).then_inc(last_sums, 1)

        @block.vector
        def _(dve):
            steps = [0]

            def link(ins):
                steps[0] += 1
                ins.then_inc(dve_step, 1)
                dve.wait_ge(dve_step, steps[0])

            def drains(ins, name):
                ins.then_inc(drained[bank_of[name]], 1)
                dve.wait_ge(drained[bank_of[name]], nth_of[name] + 1)

            dve.wait_ge(raw_consts, 11)
            diff = yB[:, :, :].rearrange("p a b -> p (a b)").rearrange("p (a t) -> p a t", t=P)
            for k in range(7):
                link(dve.tensor_scalar(ints[:, 2, :], ints[:, 0, :], k, None, ALU.arith_shift_right))
                link(dve.tensor_scalar(ints[:, 3, :], ints[:, 1, :], k, None, ALU.arith_shift_right))
                link(dve.tensor_tensor(diff[:, k, :], ints[:, 2, :], ints[:, 3, :], ALU.subtract))
                if k == 0:
                    dve.tensor_scalar(ident[:, :], diff[:, 0, :], 0.0, None, ALU.is_equal).then_inc(ident_ready, 1)

            dve.wait_ge(sumsq_ready, 3)
            dve.reciprocal(stat[:, 4:6], stat[:, 2:4]).then_inc(rstd_ready, 1)
            dve.wait_ge(rstd_ready, 1)
            dve.tensor_scalar(xn[:, 1, :], xs[:, 1, :], stat[:, 5:6], None, ALU.mult).then_inc(xn_ready, 1)
            await_filled(dve, ("par",))
            link(dve.tensor_copy(ffn_col[:, :], view(("par",), NROWS)[:, R_FFN:R_FFN + KD]))
            drains(dve.tensor_copy(pcol[:, :], view(("par",), NROWS)), ("par",))
            for c in range(KD // 2):
                name = ("hT", c)
                await_filled(dve, name)
                for k in range(2):
                    dve.wait_ge(hi_ready, 2 * c + 2)
                    ins = dve.scalar_tensor_tensor(out=hT_lo[:, 2 * c + k, :], in0=view(name, 2, T)[:, k, :],
                                                   scalar=col(R_MIXG + 2 * c + k), in1=hT_hi[:, 2 * c + k, :].bitcast(F32),
                                                   op0=ALU.mult, op1=ALU.subtract)
                    if k == 0:
                        link(ins)
                    else:
                        drains(ins, name)

            def shift_lora():
                await_drained(dve, ("z", "lora", 0, 1))
                link(dve.tensor_tensor(dsh[:, 0:2, :], zl[:, :, 0:T], zl[:, :, 1:T + 1], ALU.subtract))
                link(dve.scalar_tensor_tensor(out=ul[:, 0, :], in0=dsh[:, 0, :], scalar=col(MU_L), in1=zl[:, 0, 1:T + 1],
                                              op0=ALU.mult, op1=ALU.add))
                dve.scalar_tensor_tensor(out=ul[:, 1, :], in0=dsh[:, 1, :], scalar=col(MU_L + 1),
                                         in1=zl[:, 1, 1:T + 1], op0=ALU.mult, op1=ALU.add).then_inc(lora_mixed, 1)

            def shift(it):
                par = it % 2
                await_drained(dve, ("z", "rv", it, 1))
                link(dve.tensor_tensor(u[:, :, :], zs[:, 0:4, 0:T], zs[:, 0:4, 1:T + 1], ALU.subtract))
                link(dve.tensor_tensor(uv[:, par, :, :], zs[:, 4:6, 0:T], zs[:, 4:6, 1:T + 1], ALU.subtract))
                for n in range(6):
                    kind, j = n // 2, n % 2
                    dst = u[:, n, :] if n < 4 else uv[:, par, j, :]
                    mu = (MU_K, MU_R, MU_V)[kind] + 2 * it + j
                    ins = dve.scalar_tensor_tensor(out=dst, in0=dst, scalar=col(mu), in1=zs[:, n, 1:T + 1],
                                                   op0=ALU.mult, op1=ALU.add)
                    if n < 5:
                        link(ins)
                    else:
                        ins.then_inc(shifted, 1)
                        dve.wait_ge(shifted, it + 1)
                for j in range(2):
                    link(dve.tensor_scalar(kk0[:, j, :], u[:, j, :], col(R_KK + 2 * it + j), None, ALU.mult))
                dve.tensor_tensor(sq[:, :, :], kk0[:, :, :], kk0[:, :, :], ALU.mult).then_inc(ksq_ready, 1)
                dve.wait_ge(ksq_ready, it + 1)

            def modify(it):
                await_drained(dve, ("la", it))
                for j in range(2):
                    link(dve.tensor_scalar(km[:, j, :], aa[:, j, :], -1.0, col(R_KA + 2 * it + j), ALU.add, ALU.mult))
                link(dve.scalar_tensor_tensor(out=km[:, :, :], in0=km[:, :, :], scalar=1.0, in1=u[:, 0:2, :],
                                              op0=ALU.add, op1=ALU.mult))
                if it:
                    dve.wait_ge(bon_ready, it)
                link(dve.scalar_tensor_tensor(out=bp[:, 0, :], in0=u[:, 2, :], scalar=col(R_RK + 2 * it), in1=km[:, 0, :],
                                              op0=ALU.mult, op1=ALU.mult))
                dve.scalar_tensor_tensor(out=bp[:, 1, :], in0=u[:, 3, :], scalar=col(R_RK + 2 * it + 1), in1=km[:, 1, :],
                                         op0=ALU.mult, op1=ALU.mult).then_inc(bprod_ready, 1)
                dve.wait_ge(bprod_ready, it + 1)

            def cumulate(it):
                await_drained(dve, ("la", it))
                link(dve.tensor_tensor_scan(cc[:, :, :].rearrange("p a b -> p (a b)"), chunkmask[:, :],
                                            sgw[:, :, :].rearrange("p a b -> p (a b)"), 0.0, ALU.mult, ALU.add))
                dve.tensor_tensor(cm[:, :, :], cc[:, :, :], sgw[:, :, :], ALU.subtract).then_inc(cum_ready, 1)
                dve.wait_ge(cum_ready, it + 1)

            def normalise(it):
                await_drained(dve, ("kn", it))
                link(dve.tensor_scalar(sq[:, :, :], sq[:, :, :], 1e-12, None, ALU.max))
                link(dve.reciprocal(sq[:, :, :], sq[:, :, :]))
                link(dve.tensor_tensor(kk0[:, :, :], kk0[:, :, :], sq[:, :, :], ALU.mult))

            def second_half(it):
                dve.wait_ge(exps_ready, 3 * (it + 1))
                w4 = [w[:, :, :].rearrange("p j (a t) -> p (j a) t", t=P) for w in (Wc, Wi, Wp)]
                kk4 = kk0[:, :, :].rearrange("p j (a t) -> p (j a) t", t=P)
                link(dve.scalar_tensor_tensor(out=AR[:, :, 0, :], in0=kk4, scalar=-1.0, in1=w4[2], op0=ALU.mult, op1=ALU.mult))
                link(dve.tensor_tensor(AR[:, :, 1, :], u[:, 2:4, :].rearrange("p j (a t) -> p (j a) t", t=P), w4[0], ALU.mult))
                link(dve.tensor_tensor(aa[:, :, :], kk0[:, :, :], aa[:, :, :], ALU.mult))
                link(dve.tensor_tensor(ch4["b"][:, :, :], aa[:, :, :].rearrange("p j (a t) -> p (j a) t", t=P), w4[1], ALU.mult))
                link(dve.tensor_tensor(ch4["k"][:, :, :], km[:, :, :].rearrange("p j (a t) -> p (j a) t", t=P), w4[1], ALU.mult))
                ends = Wc[:, :, :].rearrange("p j (c t) -> p (j c) t", t=CH)[:, :, CH - 1:CH].broadcast_to([P, 2 * NCH, CH])
                for n, k in enumerate("bk"):
                    ins = dve.tensor_tensor(ch4[k.upper()][:, :, :].rearrange("p a (c t) -> p (a c) t", t=CH),
                                            ch4[k][:, :, :].rearrange("p a (c t) -> p (a c) t", t=CH), ends, ALU.mult)
                    if n == 0:
                        link(ins)
                    else:
                        ins.then_inc(prepared, 1)
                        dve.wait_ge(prepared, it + 1)

            def gla_decay(it):
                dve.wait_ge(softplus_ready, it + 1)
                link(dve.scalar_tensor_tensor(out=dsh[:, 2, :], in0=gx[:, it % 2, :], scalar=0.0, in1=dsh[:, 1, :],
                                              op0=ALU.min, op1=ALU.subtract))
                link(dve.tensor_tensor_scan(dsh[:, 3, :], chunkmask[:, 0:T], dsh[:, 2, :], 0.0, ALU.mult, ALU.add))
                b4 = dsh[:, 3, :].rearrange("p (c t) -> p c t", t=CH)
                link(dve.tensor_tensor(dsh[:, 2, :].rearrange("p (c t) -> p c t", t=CH), b4,
                                       b4[:, :, CH // 2:CH // 2 + 1].broadcast_to([P, NCH, CH]), ALU.subtract))
                dve.tensor_tensor(dsh[:, 4, :].rearrange("p (c t) -> p c t", t=CH),
                                  b4[:, :, CH - 1:CH].broadcast_to([P, NCH, CH]), b4, ALU.subtract).then_inc(b_ready, 1)

            def gla_state(it, c):
                name = ("gS", it, c)
                await_filled(dve, name)
                if c == 0:
                    drains(dve.tensor_copy(gSt[:, 0, :], view(name, T)), name)
                else:
                    drains(dve.scalar_tensor_tensor(out=gSt[:, c, :], in0=gSt[:, c - 1, :],
                                                    scalar=gtmp[2][:, CH * c + CH - 1:CH * c + CH], in1=view(name, T),
                                                    op0=ALU.mult, op1=ALU.add), name)

            def state(it, c):
                name = ("S", it, c)
                await_filled(dve, name)
                for n in range(4):
                    j, hh = n // 2, n % 2
                    r = slice(HN * hh, HN * hh + HN)
                    src = view(name, 2, P)[r, j, HN * hh:HN * hh + HN]
                    dst = Ss[r, c, j, HN * hh:HN * hh + HN]
                    if c == 0:
                        ins = dve.tensor_copy(dst, src)
                    else:
                        ins = dve.scalar_tensor_tensor(
                            out=dst, in0=Ss[r, c - 1, j, HN * hh:HN * hh + HN],
                            scalar=Wc[r, j, CH * c + CH - 1:CH * c + CH], in1=src, op0=ALU.mult, op1=ALU.add)
                    if n < 3:
                        link(ins)
                    else:
                        drains(ins, name)

            def update(it, c):
                Q4 = Qs[:, :, :].rearrange("p (j a) i -> p j a i", a=NT)
                U4 = Us[:, :, :].rearrange("p (j a) i -> p j a i", a=NT)
                tt, h = c // 2, slice(CH * (c % 2), CH * (c % 2) + CH)
                if c == 0:
                    dve.tensor_copy(U4[h, :, tt, :], Q4[h, :, tt, :]).then_inc(u0_ready, 1)
                    dve.wait_ge(u0_ready, it + 1)
                else:
                    name = ("U", it, c)
                    await_filled(dve, name)
                    drains(dve.tensor_tensor(U4[h, :, tt, :], view(name, 2, P)[h], Q4[h, :, tt, :], ALU.add), name)

            def round_(it):
                par = it % 2
                below2 = below[:, :].unsqueeze(1).broadcast_to([P, 2, P])
                upto2 = upto[:, :].unsqueeze(1).broadcast_to([P, 2, P])
                for kind, strict, incl in (("B", "N", "Mrb"), ("K", "Lak", "Mrk")):
                    if kind == "K" and it:
                        dve.wait_ge(yB_ready, it)
                    for hh in range(2):
                        for uu in range(2):
                            name = ("L" + kind, it, hh, uu)
                            await_filled(dve, name)
                            i0 = 4 * hh + 2 * uu
                            link(dve.tensor_tensor(mats[strict][:, i0:i0 + 2, :], view(name, 2, 2, P)[:, :, 0, :], below2, ALU.mult))
                            drains(dve.tensor_tensor(mats[incl][:, i0:i0 + 2, :], view(name, 2, 2, P)[:, :, 1, :], upto2,
                                                     ALU.mult), name)
                dve.wait_ge(eye_ready, 2 * (it + 1))
                for hh in range(2):
                    name = ("LL", it, hh)
                    await_filled(dve, name)
                    m4 = [m[:, 0, :].unsqueeze(1).broadcast_to([P, 4, P]) for m in (low8, up8)]
                    link(dve.copy_predicated(mats["G"][:, 4 * hh:4 * hh + 4, :], m4[1], mats["N"][:, 4 * hh:4 * hh + 4, :]))
                    drains(dve.copy_predicated(mats["T"][:, 4 * hh:4 * hh + 4, :], m4[0], view(name, 4, P)), name)
                for n, lev in enumerate(LEVELS[1:]):
                    for g in range(4):
                        name = ("TG", it, lev, g)
                        await_filled(dve, name)
                        m2 = [m[:, n + 1, :].unsqueeze(1).broadcast_to([P, 2, P]) for m in (low8, up8)]
                        if n + 1 < len(LEVELS) - 1:
                            link(dve.copy_predicated(mats["T"][:, 2 * g:2 * g + 2, :], m2[0], view(name, 4, P)[:, 0:2, :]))
                        drains(dve.copy_predicated(mats["G"][:, 2 * g:2 * g + 2, :], m2[1], view(name, 4, P)[:, 2:4, :]), name)
                await_drained(dve, ("Q", it))
                update(it, 0)
                dve.wait_ge(gexp_ready, 6 * (it + 1))
                link(dve.tensor_tensor(gprod[0], gq[:, par, :], gtmp[0], ALU.mult))
                link(dve.tensor_tensor(gprod[1], gk[:, par, :], gtmp[1], ALU.mult))
                link(dve.tensor_tensor(gprod[3], gk[:, par, :], gtmp[3], ALU.mult))
                dve.tensor_tensor(gprod[2], gq[:, par, :], gtmp[2], ALU.mult).then_inc(gprep_ready, 1)
                dve.wait_ge(gprep_ready, it + 1)
                for j in range(2):
                    link(dve.tensor_tensor(og[:, par, j, :], og[:, par, j, :], dsh[:, 2 + 3 * j, :], ALU.mult))
                link(dve.memset(gsT, 0.0))
                name = ("gs", it)
                await_filled(dve, name)
                drains(dve.copy_predicated(gsT, upto8[:, :].unsqueeze(1).broadcast_to([P, NT, P]), view(name, 2, P)), name)
                state(it, 0)
                gla_state(it, 0)
                update(it, 1)
                gla_state(it, 1)
                state(it, 1)
                gla_state(it, 2)
                update(it, 2)
                state(it, 2)
                if it + 1 < ITERS:
                    shift(it + 1)
                update(it, 3)
                await_drained(dve, ("gn", it))
                dve.reciprocal(dsh[:, 4, :], dsh[:, 4, :]).then_inc(gstd_ready, 1)
                if it + 1 < ITERS:
                    modify(it + 1)
                    cumulate(it + 1)
                    normalise(it + 1)
                await_drained(dve, ("y", it))
                name = ("mean", it)
                await_filled(dve, name)
                drains(dve.scalar_tensor_tensor(out=ys[:, :, :], in0=view(name, 2, T), scalar=-1.0 / HN, in1=ys[:, :, :],
                                                op0=ALU.mult, op1=ALU.add), name)
                dve.tensor_tensor(ysd, ys4, ys4, ALU.mult).then_inc(ysq_ready, 1)
                dve.wait_ge(ysq_ready, it + 1)
                if it + 1 < ITERS:
                    second_half(it + 1)
                if it + 2 == ITERS:
                    join(dve, 1)
                await_drained(dve, ("var", it))
                dve.reciprocal(ysd, ysd).then_inc(ystd_ready, 1)
                if it + 1 < ITERS:
                    gla_decay(it + 1)

            dve.wait_ge(ident_ready, 1)
            link(dve.tensor_scalar(before[:, :], diff[:, 0, :], 0.0, None, ALU.is_lt))
            link(dve.tensor_scalar(headones[:, :], diff[:, 6, :], 0.0, None, ALU.is_equal))
            link(dve.tensor_tensor(below[:, :], before[:, :], headones[:, :], ALU.mult))
            link(dve.tensor_tensor(upto[:, :], below[:, :], ident[:, :], ALU.add))
            link(dve.tensor_copy(upto8[:, :], upto[:, :]))
            for k in range(len(LEVELS)):
                link(dve.tensor_scalar(diff[:, 8, :], diff[:, k + 1, :], 0.0, None, ALU.is_equal))
                link(dve.scalar_tensor_tensor(out=low8[:, k, :], in0=diff[:, k, :], scalar=1.0, in1=diff[:, 8, :],
                                              op0=ALU.is_equal, op1=ALU.mult))
                link(dve.scalar_tensor_tensor(out=up8[:, k, :], in0=diff[:, k, :], scalar=-1.0, in1=diff[:, 8, :],
                                              op0=ALU.is_equal, op1=ALU.mult))
            dve.sem_inc(consts_ready, 1)
            shift_lora()
            for kind, it in VECTOR_SPLITS:
                n = block_index[(kind, it)]
                dve.wait_ge(w_hi_ready, n + 1)
                hi, lo, slot = w_parts(n)
                dve.tensor_tensor(lo, slot, hi.bitcast(F32), ALU.subtract).then_inc(w_lo_by_vector, 1)
            shift(0)
            modify(0)
            cumulate(0)
            normalise(0)
            second_half(0)
            gla_decay(0)
            for it in range(ITERS):
                round_(it)

            for m in range(KD):
                await_filled(dve, ("ba", m))
                drains(dve.tensor_tensor(gates[:, m, :], gates[:, m, :], view(("ba", m), T), ALU.mult), ("ba", m))
                await_filled(dve, ("bb", m))
                drains(dve.tensor_tensor(gates[:, KD + m, :], gates[:, KD + m, :], view(("bb", m), T), ALU.mult), ("bb", m))
                dve.tensor_tensor(gates[:, m, :], gates[:, m, :], gates[:, KD + m, :], ALU.add).then_inc(merged_ready, 1)
            dve.wait_ge(x_in, 2 * 16)
            for m in range(4):
                for tt in range(NT):
                    name = ("out", m, tt)
                    await_filled(dve, name)
                    drains(dve.tensor_tensor(xs[:, tt, 256 * m:256 * m + 256], xs[:, tt, 256 * m:256 * m + 256], view(name, T),
                                             ALU.add), name)
                if m:
                    name = ("h2T", m - 1)
                    await_filled(dve, name)
                    drains(dve.tensor_copy(h2T[:, 2 * m - 2:2 * m, :], view(name, 2, T)), name)
            dve.sem_inc(x1_ready, 1)
            dve.wait_ge(sumsq_ready, 3 + 8)
            dve.tensor_reduce(stat[:, 6:8], stat[:, 16:24].rearrange("p (a m) -> p a m", a=NT), AX_X, ALU.add).then_inc(mean_ready, 1)
            name = ("h2T", 3)
            await_filled(dve, name)
            drains(dve.tensor_copy(h2T[:, 6:8, :], view(name, 2, T)), name)
            dve.wait_ge(sumsq_ready, 3 + 9)
            link(dve.reciprocal(stat[:, 8:10], stat[:, 8:10]))
            dve.wait_ge(late_in, 4 * 16)
            for tt in range(NT):
                dve.scalar_tensor_tensor(out=h2[:, tt, :], in0=xs[:, tt, :], scalar=stat[:, 8 + tt:9 + tt], in1=ffn_g[:, :],
                                         op0=ALU.mult, op1=ALU.mult).then_inc(h2_ready, 1)
            name = ("log",)
            await_filled(dve, name)
            for tt in range(NT):
                ins = dve.scalar_tensor_tensor(out=lg[:, tt, :], in0=view(name, NT, E)[:, tt, :], scalar=stat[:, 8 + tt:9 + tt],
                                               in1=rb[:, :], op0=ALU.mult, op1=ALU.add)
                if tt < NT - 1:
                    link(ins)
                else:
                    drains(ins, name)
            for tt in range(NT):
                link(dve.max(top[:, tt, :], lg[:, tt, :]))
            dve.tensor_scalar(rs[:, 0:2].unsqueeze(2), top[:, :, 0:1], -1.0, None, ALU.mult).then_inc(lmax_ready, 1)
            fourth = top[:, :, TOPK - 1:TOPK].broadcast_to([P, NT, E])
            link(dve.tensor_tensor(rt[:, 0, :, :], lg[:, :, :], fourth, ALU.is_gt))
            link(dve.tensor_tensor(rt[:, 1, :, :], lg[:, :, :], fourth, ALU.is_equal))
            link(dve.tensor_reduce(rs[:, 2:4], rt[:, 0, :, :], AX_X, ALU.add))
            for tt in range(NT):
                link(dve.tensor_tensor_scan(rt[:, 2, tt, :], ones[:, 0:E], rt[:, 1, tt, :], rs[:, 2 + tt:3 + tt], ALU.mult, ALU.add))
            link(dve.scalar_tensor_tensor(out=rt[:, 2, :, :], in0=rt[:, 2, :, :], scalar=float(TOPK), in1=rt[:, 1, :, :],
                                          op0=ALU.is_le, op1=ALU.mult))
            dve.tensor_tensor(selM[:, :, :], rt[:, 2, :, :], rt[:, 0, :, :], ALU.add).then_inc(mask_sel, 1)
            name = ("pos",)
            await_filled(dve, name)
            dve.wait_ge(mask_sel, 1)
            drains(dve.scalar_tensor_tensor(out=posm[:, :, :].rearrange("p e a -> p a e"), in0=selM[:, :, :], scalar=-4096.0,
                                            in1=view(name, NT, E), op0=ALU.mult, op1=ALU.add), name)

            def gate_values():
                dve.wait_ge(gexpo, 2)
                link(dve.tensor_tensor(rt[:, 4, :, :], rt[:, 4, :, :], selM[:, :, :], ALU.mult))
                link(dve.tensor_reduce(rs[:, 4:6], rt[:, 4, :, :], AX_X, ALU.add))
                link(dve.reciprocal(rs[:, 6:8], rs[:, 4:6]))
                for tt in range(NT):
                    dve.tensor_scalar(gatev[:, :, tt], rt[:, 4, tt, :], rs[:, 6 + tt:7 + tt], None, ALU.mult).then_inc(gatev_ready, 1)
                dve.wait_ge(gatev_ready, 2)

            def most_tokens():
                name = ("cnt",)
                await_filled(dve, name)
                drains(dve.tensor_reduce(rs[:, 8:9], view(name, E), AX_X, ALU.max), name)
                dve.tensor_copy(over[:, :], rs[:, 8:9]).then_inc(route_ready, 1)

            def choose(i):
                if isinstance(i, int):
                    e, s0 = i, 0
                else:
                    e, s0 = i % E, (i // E) * SLOTS
                wait_after(dve, gather_done, i)
                dve.tensor_tensor(sel[:, :, :], iota[:, bass.ds(s0, SLOTS)].unsqueeze(1).broadcast_to([P, NT, SLOTS]),
                                  posm[:, bass.ds(e, 1), :].rearrange("p a b -> p (a b)").unsqueeze(2).broadcast_to([P, NT, SLOTS]),
                                  ALU.is_equal).then_inc(sel_ready, 1)

            def gate(i):
                e, s0 = (i, 0) if isinstance(i, int) else (i % E, (i // E) * SLOTS)
                wait_after(dve, selT_done, i)
                for tt in range(NT):
                    dve.tensor_scalar(selg[:, tt, :, :], iota[:, bass.ds(s0, SLOTS)].unsqueeze(1).broadcast_to([P, 2, SLOTS]),
                                      posm[:, bass.ds(e, 1), tt], gatev[:, bass.ds(e, 1), tt],
                                      ALU.is_equal, ALU.mult).then_inc(selg_ready, 1)

            def point(i):
                e = i if isinstance(i, int) else i % E
                wait_after(dve, hid_done, i)
                dve.tensor_scalar(ehot[:, :], onesE[:, :], ident[0:E, bass.ds(e, 1)], None, ALU.mult).then_inc(ehot_ready, 1)

            def turn(i):
                dve.wait_ge(selT_done, i + 1)
                dve.tensor_copy(selgT[:, :, :], banks[3][:, 0:T].rearrange("p (a t) -> p a t", a=NT)).then_inc(selgT_ready, 1)

            def expert(i):
                hid = [banks[1 + q][:, :].rearrange("p (m two) -> p m two", two=2) for q in range(2)]
                point(i + 1)
                wait_after(dve, act_ready, i)
                for q in range(2):
                    dve.tensor_scalar(glu[:, q, :], hid[q][:, :, 0], 7.0, None, ALU.min).then_inc(glu_half, 1) if q == 0 else \
                        dve.tensor_scalar(glu[:, q, :], hid[q][:, :, 0], 7.0, None, ALU.min).then_inc(glu_ready, 1)
                for q in range(2):
                    dve.tensor_scalar(lin[:, q, :], hid[q][:, :, 1], 7.0, -7.0, ALU.min, ALU.max).then_inc(lin_ready, 1)
                dve.wait_ge(glu_ready, i + 1)
                dve.wait_ge(lin_ready, i * 2 + 2)
                dve.scalar_tensor_tensor(out=lin[:, :, :], in0=lin[:, :, :], scalar=1.0, in1=glu[:, :, :], op0=ALU.add,
                                         op1=ALU.mult).then_inc(gated_ready, 1)
                dve.wait_ge(gated_ready, i + 1)
                dve.wait_ge(sgm_ready, i + 1)
                wait_after(dve, actT_done, i)
                dve.tensor_tensor(act_s[:, :, :], lin[:, :, :], sgm[:, :, :], ALU.mult).then_inc(act_ready, 1)
                choose(i + 2)
                if not (isinstance(i, int) and i == 0):
                    add(i - 1)
                turn(i)
                gate(i + 1)

            def add(i):
                for n in range(NT):
                    dve.wait_ge(y_done, i * NT + (n + 1))
                    for h in range(2):
                        add_bank(n, h, 6).then_inc(y_added, 1)

            def add_bank(n, h, bank):
                return dve.tensor_tensor(acc[:, n, 512 * h:512 * h + 512], acc[:, n, 512 * h:512 * h + 512],
                                         banks[bank + h][:, :], ALU.add)

            dve.wait_ge(moe_pool, 2)
            choose(0)
            point(0)
            most_tokens()
            gate_values()
            gate(0)
            choose(1)
            expert(0)
            with dve.Fori(1, E) as i:
                expert(i)
            dve.wait_ge(route_ready, 1)
            most = dve.value_load(over[0:1, 0:1], min_val=0, max_val=T)
            with dve.If(most > SLOTS):
                with dve.Fori(E, PASSES * E) as i:
                    expert(i)
                dve.wait_ge(y_added, 4 * (PASSES * E - 1))
            for tt in range(NT):
                dve.wait_ge(last_scattered, tt + 1)
                for h in range(2):
                    add_bank(tt, h, LAST_BANKS[tt]).then_inc(last_added, 1)
            fin = h2T[:, :, :].rearrange("p a b -> p (a b)").rearrange("p (a d) -> p a d", a=NT)
            dve.wait_ge(last_added, 2 * NT)
            for tt in range(NT):
                dve.wait_ge(last_sums, 2 * tt + 2)
                link(dve.reciprocal(stat[:, 14 + tt:15 + tt], stat[:, 12 + tt:13 + tt]))
                dve.scalar_tensor_tensor(out=fin[:, tt, :], in0=xs[:, tt, :], scalar=stat[:, 14 + tt:15 + tt],
                                         in1=final_g[:, :], op0=ALU.mult, op1=ALU.mult).then_inc(final_ready, 1)

        @block.tensor
        def _(pe):
            at = [0]

            def begin(name):
                assert order[at[0]] == name, (order[at[0]], name)
                at[0] += 1
                if nth_of[name]:
                    pe.wait_ge(drained[bank_of[name]], nth_of[name])

            def end(ins, name):
                ins.then_inc(filled[bank_of[name]], 1)

            pe.wait_ge(rows_in, 12 * 16)
            pe.wait_ge(ident_ready, 1)
            begin(("par",))
            end(pe.transpose(view(("par",), NROWS), prow[0:NROWS, :], ident[0:NROWS, 0:NROWS]), ("par",))
            pe.wait_ge(xn_ready, 2)
            for c in range(KD // 2):
                name = ("hT", c)
                begin(name)
                for k in range(2):
                    for tt in range(NT):
                        d0 = P * (2 * c + k)
                        last = pe.transpose(view(name, 2, NT, P)[:, k, tt, :], xn[:, tt, d0:d0 + P], ident[:, :])
                end(last, name)
            for c in range(KD // 2):
                await_drained(pe, ("hT", c))

            def weights(kind, it):
                n = block_index[(kind, it)]
                pe.wait_ge(w_in_ready[n % WRING], ring_count[n])
                return wslot(kind, it)

            def tile(name, kind, it, j):
                begin(name)
                n = block_index[(kind, it)]
                token_major = kind == "gv"
                if n < split_blocks:
                    await_lo(pe, n)
                    hi, lo, _ = w_parts(n)
                    parts = [(hi, hT_hi), (hi, hT_lo), (lo, hT_hi)]
                else:
                    pe.wait_ge(whole, 2)
                    parts = [(weights(kind, it), hT[:, :, :])]
                o = view(name, T)[0:RANK, :] if kind == "lr" else view(name, T)
                cols = slice(0, RANK) if kind == "lr" else slice(P * j, P * j + P)
                for k in range(KD):
                    for m, (w, h) in enumerate(parts):
                        first, end_ = k == 0 and m == 0, k == KD - 1 and m == len(parts) - 1
                        if token_major:
                            last = pe.matmul(o, h[:, k, P * j:P * j + P], w[:, k, :], start=first, stop=end_)
                        else:
                            last = pe.matmul(o, w[:, k, cols], h[:, k, :], start=first, stop=end_)
                end(last, name)

            def project(kind, it, j):
                name = ("z", kind, it, j)
                tile(name, kind, it, j)

            def ranks(it):
                if it == 0:
                    pe.wait_ge(lora_in, 4 * 16)
                    pe.wait_ge(lora_act, 2)
                for key in ("lw", "la", "lg"):
                    name = (key, it)
                    begin(name)
                    for j in range(2):
                        c0 = P * (2 * it + j)
                        if key == "lg":
                            last = pe.matmul(view(name, 2, T)[:, j, :], g2[:, c0:c0 + P], ul[:, 1, :], start=True, stop=True)
                        else:
                            r = slice(0, 64) if key == "lw" else slice(64, 128)
                            last = pe.matmul(view(name, 2, T)[:, j, :], w2a2[r, c0:c0 + P], ul[r, 0, :], start=True, stop=True)
                    end(last, name)
                name = ("gl", it)
                begin(name)
                await_drained(pe, ("z", "lr", 0, 0))
                end(pe.matmul(view(name, T), gup[:, P * it:P * it + P], zlr[:, :], start=True, stop=True), name)

            def key_norm(it):
                name = ("kn", it)
                begin(name)
                pe.wait_ge(ksq_ready, it + 1)
                end(pe.matmul(view(name, 512), headones[:, :], sq[:, :, :], start=True, stop=True), name)

            def bonus(it):
                name = ("bo", it)
                begin(name)
                pe.wait_ge(bprod_ready, it + 1)
                end(pe.matmul(view(name, 512), headones[:, :], bp[:, :, :], start=True, stop=True), name)

            def round_(it):
                par = it % 2
                plan = between(it)

                def more(point):
                    for t in plan[point]:
                        project(*t)

                more("prep")
                pe.wait_ge(prepared, it + 1)
                for kind in "ABKV":
                    name = ("tr", it, kind)
                    begin(name)
                    for jt in range(4):
                        src = {"A": AR[:, jt, 0, :], "B": ch4["B"][:, jt, :], "K": ch4["K"][:, jt, :],
                               "V": uv[:, par, jt // 2, P * (jt % 2):P * (jt % 2) + P]}[kind]
                        last = pe.transpose(view(name, 4, P)[:, jt, :], src, ident[:, :])
                    end(last, name)
                for kind in "BK":
                    for hh in range(2):
                        r = slice(HN * hh, HN * hh + HN)
                        for uu in range(2):
                            name = ("L" + kind, it, hh, uu)
                            begin(name)
                            for n in range(2):
                                jt = 2 * uu + n
                                last = pe.matmul(view(name, 2, 2 * P)[:, n, :], ch4[kind.lower()][r, jt, :],
                                                 AR[r, jt, :, :], start=True, stop=True)
                            end(last, name)
                for hh in range(2):
                    r = slice(HN * hh, HN * hh + HN)
                    name = ("LL", it, hh)
                    begin(name)
                    for jt in range(4):
                        last = pe.matmul(view(name, 4, P)[:, jt, :], AR[r, jt, 0, :], ch4["b"][r, jt, :], start=True, stop=True)
                    end(last, name)

                def items(hh_first=False):
                    return [(hh, jt, 4 * hh + jt) for hh in range(2) for jt in range(4)]

                name = ("X", it)
                begin(name)
                await_drained(pe, ("LK", it, 1, 1))
                await_drained(pe, ("tr", it, "V"))
                for hh, jt, i in items():
                    c = slice(HN * hh, HN * hh + HN)
                    last = pe.matmul(view(name, 4, P)[:, jt, c], mats["Lak"][:, i, :], tm["V"][:, jt, c], start=True, stop=True)
                end(last, name)
                before_lev = None
                for lev in LEVELS[1:]:
                    for g in range(4):
                        name = ("Z", it, lev, g)
                        begin(name)
                        if before_lev is None:
                            await_drained(pe, ("LL", it, g // 2))
                        else:
                            await_drained(pe, ("TG", it, before_lev, g))
                        for n in range(2):
                            last = pe.matmul(view(name, 2, P)[:, n, :], mats["N"][:, 2 * g + n, :], mats["T"][:, 2 * g + n, :],
                                             start=True, stop=True)
                        end(last, name)
                    for g in range(4):
                        name = ("TG", it, lev, g)
                        begin(name)
                        await_drained(pe, ("Z", it, lev, g))
                        for n in range(2):
                            Gm, Zm = mats["G"][:, 2 * g + n, :], mats["Z"][:, 2 * g + n, :]
                            if lev != LEVELS[-1]:
                                pe.matmul(view(name, 4, P)[:, n, :], Gm, Zm, start=True, stop=True)
                            last = pe.matmul(view(name, 4, P)[:, 2 + n, :], Zm, Gm, start=True, stop=True)
                        end(last, name)
                    before_lev = lev
                name = ("Q", it)
                begin(name)
                for g in range(4):
                    await_drained(pe, ("TG", it, LEVELS[-1], g))
                await_drained(pe, ("X", it))
                for hh, jt, i in items():
                    c = slice(HN * hh, HN * hh + HN)
                    last = pe.matmul(view(name, 4, P)[:, jt, c], mats["G"][:, i, :], Xs[:, jt, c], start=True, stop=True)
                end(last, name)
                name = ("PT", it)
                begin(name)
                await_drained(pe, ("tr", it, "A"))
                for hh, jt, i in items():
                    c = slice(HN * hh, HN * hh + HN)
                    last = pe.matmul(view(name, 4, P)[c, jt, :], tm["A"][:, jt, c], mats["G"][:, i, :], start=True, stop=True)
                end(last, name)
                more("pt")

                def update(c):
                    tt, h = c // 2, slice(CH * (c % 2), CH * (c % 2) + CH)
                    name = ("U", it, c)
                    begin(name)
                    await_drained(pe, ("PT", it))
                    await_drained(pe, ("S", it, c - 1))
                    for j in range(2):
                        last = pe.matmul(view(name, 2, P)[h, j, :], PTs[:, 2 * j + tt, h], Ss[:, c - 1, j, :], start=True, stop=True)
                    end(last, name)

                def state(c):
                    tt, h = c // 2, slice(CH * (c % 2), CH * (c % 2) + CH)
                    name = ("S", it, c)
                    begin(name)
                    if c == 0:
                        pe.wait_ge(u0_ready, it + 1)
                    else:
                        await_drained(pe, ("U", it, c))
                    for j in range(2):
                        o = view(name, 2, P)[:, j, :]
                        pe.matmul(o, tm["K"][h, 2 * j + tt, :], tm["V"][h, 2 * j + tt, :], start=True, stop=False)
                        last = pe.matmul(o, tm["B"][h, 2 * j + tt, :], Us[h, 2 * j + tt, :], start=False, stop=True)
                    end(last, name)

                gla_scores(it)
                state(0)
                gla_state(it, 0)
                more("s0")
                update(1)
                gla_state(it, 1)
                more("u1")
                state(1)
                gla_state(it, 2)
                more("s1")
                update(2)
                gla_out(it)
                if it + 1 < ITERS:
                    ranks(it + 1)
                more("u2")
                state(2)
                more("s2")
                update(3)
                gla_norm(it)
                more("u3")
                if it + 1 < ITERS:
                    key_norm(it + 1)
                name = ("y", it)
                begin(name)
                await_drained(pe, ("U", it, NCH - 1))
                for jt in range(4):
                    j, tt = jt // 2, jt % 2
                    for hh in range(2):
                        c = slice(HN * hh, HN * hh + HN)
                        pe.matmul(view(name, 4, P)[c, jt, :], tm["V"][:, jt, c], mats["Mrk"][:, 4 * hh + jt, :],
                                  start=True, stop=False, skip_group_check=True)
                    for c in range(max(1, 2 * tt), 2 * tt + 2):
                        h = slice(CH * (c % 2), CH * (c % 2) + CH)
                        pe.matmul(view(name, 4, P)[:, jt, h], Ss[:, c - 1, j, :], AR[:, jt, 1, h], start=False, stop=False,
                                  skip_group_check=True)
                    for hh in range(2):
                        c = slice(HN * hh, HN * hh + HN)
                        last = pe.matmul(view(name, 4, P)[c, jt, :], Us[:, jt, c], mats["Mrb"][:, 4 * hh + jt, :],
                                         start=False, stop=True, skip_group_check=True)
                end(last, name)
                if it + 1 < ITERS:
                    bonus(it + 1)
                more("y")
                name = ("mean", it)
                begin(name)
                await_drained(pe, ("y", it))
                end(pe.matmul(view(name, 512), headones[:, :], ys[:, :, :], start=True, stop=True), name)
                more("mean")
                name = ("var", it)
                begin(name)
                pe.wait_ge(ysq_ready, it + 1)
                end(pe.matmul(view(name, 512), headones[:, :], ysd, start=True, stop=True), name)
                more("var")

            def gla_scores(it):
                name = ("gs", it)
                begin(name)
                pe.wait_ge(gprep_ready, it + 1)
                for tt in range(NT):
                    c = slice(P * tt, P * tt + P)
                    last = pe.matmul(view(name, 2, P)[:, tt, :], gprod[1][:, c], gprod[0][:, c], start=True, stop=True)
                end(last, name)
                name = ("gk", it)
                begin(name)
                for tt in range(NT):
                    last = pe.transpose(view(name, 2, P)[:, tt, :], gprod[3][:, P * tt:P * tt + P], ident[:, :])
                end(last, name)

            def gla_state(it, c):
                tt, h = c // 2, slice(CH * (c % 2), CH * (c % 2) + CH)
                name = ("gS", it, c)
                begin(name)
                await_drained(pe, ("gk", it))
                end(pe.matmul(view(name, T), gkt[h, tt, :], gv[h, it % 2, tt, :], start=True, stop=True), name)

            def gla_out(it):
                par = it % 2
                name = ("go", it)
                begin(name)
                await_drained(pe, ("gs", it))
                await_drained(pe, ("gS", it, NCH - 2))
                for dv in range(2):
                    for tt in range(NT):
                        o = view(name, 2, T)[:, dv, P * tt:P * tt + P]
                        last = pe.matmul(o, gv[:, par, tt, P * dv:P * dv + P], gsT[:, tt, :], start=True, stop=False,
                                         skip_group_check=True)
                        for c in range(max(1, 2 * tt), 2 * tt + 2):
                            last = pe.matmul(view(name, 2, T)[:, dv, CH * c:CH * c + CH], gSt[:, c - 1, P * dv:P * dv + P],
                                             gprod[2][:, CH * c:CH * c + CH], start=False, stop=True, skip_group_check=True)
                end(last, name)

            def gla_norm(it):
                name = ("gn", it)
                begin(name)
                pe.wait_ge(gsq_ready, it + 1)
                for dv in range(2):
                    last = pe.matmul(view(name, T), ones[:, :], dsh[:, 2 + dv, :], start=(dv == 0), stop=(dv == 1))
                end(last, name)

            for j in range(2):
                project("lora", 0, j)
            project("lr", 0, 0)
            for kind in ROUND:
                for j in range(2):
                    project(kind, 0, j)
                if kind == RANKS_AFTER:
                    ranks(0)
                if kind == NORMS_AFTER:
                    pe.wait_ge(consts_ready, 1)
                    key_norm(0)
                    bonus(0)
            for it in range(ITERS):
                round_(it)
            pe.wait_ge(yA_ready, ITERS)
            pe.wait_ge(yB_ready, ITERS)
            for m in range(KD):
                for key, kind, src in (("ba", "wa", yA), ("bb", "wb", yB)):
                    w = weights(kind, m // 2)
                    name = (key, m)
                    begin(name)
                    for k in range(KD):
                        last = pe.matmul(view(name, T), w[:, k, P * (m % 2):P * (m % 2) + P], src[:, k, :],
                                         start=(k == 0), stop=(k == KD - 1))
                    end(last, name)

            def turn_x(c):
                name = ("h2T", c)
                begin(name)
                for tt in range(NT):
                    await_drained(pe, ("out", c, tt))
                for k in range(2):
                    for tt in range(NT):
                        d0 = P * (2 * c + k)
                        last = pe.transpose(view(name, 2, NT, P)[:, k, tt, :], xs[:, tt, d0:d0 + P], ident[:, :])
                end(last, name)

            pe.wait_ge(merged_ready, KD)
            for m in range(4):
                w = weights("wo", m)
                for tt in range(NT):
                    name = ("out", m, tt)
                    begin(name)
                    for k in range(KD):
                        last = pe.matmul(view(name, T), gates[:, k, P * tt:P * tt + P], w[:, k, :],
                                         start=(k == 0), stop=(k == KD - 1))
                    end(last, name)
                if m:
                    turn_x(m - 1)

            def keep_clock(n):
                for _ in range(n):
                    pe.matmul(banks[1][:, :], ident[:, :], h2T[:, 0:2, :], start=True, stop=True)

            turn_x(3)
            pe.wait_ge(rw_ready, KD)
            name = ("log",)
            begin(name)
            for c in range(4):
                await_drained(pe, ("h2T", c))
            for tt in range(NT):
                for k in range(KD):
                    last = pe.matmul(view(name, NT, E)[:, tt, :], h2T[:, k, P * tt:P * tt + P], rw[:, k, :],
                                     start=(k == 0), stop=(k == KD - 1))
            end(last, name)
            pe.wait_ge(drained[1], fills[1])
            keep_clock(4)
            pe.wait_ge(mask_sel, 1)
            name = ("pos",)
            begin(name)
            pe.matmul(view(name, NT, E)[:, 0, :], before[:, :], selM[:, 0, :], start=True, stop=True)
            pe.matmul(view(name, NT, E)[:, 1, :], ones[:, :], selM[:, 0, :], start=True, stop=False)
            end(pe.matmul(view(name, NT, E)[:, 1, :], before[:, :], selM[:, 1, :], start=False, stop=True), name)
            name = ("cnt",)
            begin(name)
            pe.matmul(view(name, E), ones[:, :], selM[:, 0, :], start=True, stop=False)
            end(pe.matmul(view(name, E), ones[:, :], selM[:, 1, :], start=False, stop=True), name)
            def gather(i):
                pe.wait_ge(sel_ready, i + 1)
                wait_after(pe, xg_ready, i)
                o = banks[0][:, :].rearrange("p (k s) -> p k s", k=KD)
                for k in range(KD):
                    for tt in range(NT):
                        last = pe.matmul(o[:, k, :], h2[:, tt, P * k:P * k + P], sel[:, tt, :], start=(tt == 0), stop=(tt == NT - 1))
                last.then_inc(gather_done, 1)

            def turn(i):
                pe.wait_ge(selg_ready, i * 2 + 2)
                wait_after(pe, selgT_ready, i)
                for tt in range(NT):
                    last = pe.transpose(banks[3][:, P * tt:P * tt + P], selg[:, tt, :, :].rearrange("p a b -> p (a b)"), ident[:, :])
                last.then_inc(selT_done, 1)

            def expert(i):
                wait_after(pe, lin_ready, i * 2)
                pe.wait_ge(xg_ready, i + 1)
                pe.wait_ge(ehot_ready, i + 1)
                for j in range(4):
                    pe.matmul(banks[1 + j // 2][64 * (j % 2):64 * (j % 2) + 64, :], ehot[:, :], b1s[:, 512 * j:512 * j + 512],
                              start=True, stop=False)
                for k in range(KD):
                    if k == KD - 1:
                        wait_after(pe, eo_ready, i)
                        for dh in range(2):
                            pe.matmul(banks[5][64 * dh:64 * dh + 64, :], ehot[:, :], b2s[:, 512 * dh:512 * dh + 512],
                                      start=True, stop=False)
                    pe.wait_ge(w1_in[k], i * 16 + 16)
                    for j in range(4):
                        last = pe.matmul(banks[1 + j // 2][64 * (j % 2):64 * (j % 2) + 64, :], xg[:, k, :],
                                         w1s[:, k, 512 * j:512 * j + 512], start=False, stop=(k == KD - 1))
                    if k < KD - 1:
                        last.then_inc(w1_used, 1)
                    else:
                        last.then_inc(hid_done, 1)
                        pe.wait_ge(hid_done, i + 1)
                        pe.sem_inc(w1_used, 1)
                first = isinstance(i, int) and i == 0
                gather(i + 1)
                pe.wait_ge(act_ready, i + 1)
                wait_after(pe, actT_ready, i)
                for q in range(2):
                    for b in range(2):
                        n = 2 * q + b
                        last = pe.transpose(banks[4][:, P * n:P * n + P], act_s[:, q, P * b:P * b + P], ident[:, :])
                last.then_inc(actT_done, 1)
                if not first:
                    scatter(i - 1, 0)
                pe.wait_ge(actT_ready, i + 1)
                for f in range(FF // P):
                    if f == FF // P // 2:
                        if not first:
                            scatter(i - 1, 1)
                        turn(i)
                    q, half, b = f // 4, f // 2 % 2, f % 2
                    w2 = w2s
                    if isinstance(i, int) and i == 1:
                        w2 = w2s_1
                        pe.wait_ge(w2_1_in, 2 * 16)
                    elif f % 2 == 0:
                        pe.wait_ge(w2_in[f // 2], 16 if first else i * 16)
                    for dh in range(2):
                        last = pe.matmul(banks[5][64 * dh:64 * dh + 64, :], actT[:, 2 * q + b, 64 * half:64 * half + 64],
                                         w2[:, f, 512 * dh:512 * dh + 512], start=False, stop=(f == FF // P - 1))
                    if f % 2:
                        if f == FF // P - 1:
                            last.then_inc(eo_done, 1)
                            pe.wait_ge(eo_done, i + 1)
                            if w2 is w2s:
                                pe.sem_inc(w2_used, 1)
                        elif w2 is w2s:
                            last.then_inc(w2_used, 1)

            def scatter(i, tt):
                if tt == 0:
                    pe.wait_ge(eo_ready, i + 1)
                    pe.wait_ge(selgT_ready, i + 1)
                if not (isinstance(i, int) and i == 0 and tt == 0):
                    pe.wait_ge(y_added, i * 4 + 2 * tt)
                spread(tt, 6).then_inc(y_done, 1)

            def spread(tt, bank):
                for dh in range(2):
                    r = slice(64 * dh, 64 * dh + 64)
                    last = pe.matmul(banks[bank + dh][:, :], selgT[r, tt, :], eo[r, :], start=True, stop=True)
                return last

            pe.wait_ge(bias_in, 2 * 16)
            pe.wait_ge(h2_ready, 2)
            keep_clock(2)
            for b in range(8):
                pe.wait_ge(drained[b], fills[b])
            gather(0)
            keep_clock(1)
            expert(0)
            expert(1)
            with pe.Fori(2, E) as i:
                expert(i)
            pe.wait_ge(route_ready, 1)
            most = pe.value_load(over[0:1, 0:1], min_val=0, max_val=T)
            with pe.If(most > SLOTS):
                with pe.Fori(E, PASSES * E) as i:
                    expert(i)
                pe.wait_ge(eo_ready, PASSES * E)
                pe.wait_ge(selgT_ready, PASSES * E)
                pe.wait_ge(y_added, 4 * (PASSES * E - 1))
            pe.wait_ge(eo_ready, E)
            pe.wait_ge(selgT_ready, E)
            pe.wait_ge(y_added, 4 * (E - 1))
            pe.wait_ge(lin_ready, 2 * E)
            for tt in range(NT):
                spread(tt, LAST_BANKS[tt]).then_inc(last_scattered, 1)


_INS = ['x', 'norm_mix_g', 'w_in', 'gla_gate_up', 'gla_gate_bias', 'gla_norm_g', 'rwkv_mu', 'rwkv_w0', 'rwkv_w2', 'rwkv_a0',
        'rwkv_a2', 'rwkv_g2', 'rwkv_k_k', 'rwkv_k_a', 'rwkv_r_k', 'rwkv_ln_w', 'rwkv_ln_b', 'w_branch_a', 'w_branch_b',
        'w_out', 'norm_ffn_g', 'router_w', 'router_b', 'expert_w1', 'expert_b1', 'expert_w2', 'expert_b2', 'norm_final_g']
_OUTS = [((1, 256, 1024), 'float32')]


def kernel(**inputs):
    import numpy as _np
    import concourse.bacc as _bacc
    from concourse import mybir as _mybir
    from concourse.bass_utils import run_bass_kernel_spmd as _run

    nc = _bacc.Bacc("TRN2", target_bir_lowering=False, num_devices=1)
    arrays, args = {}, []
    for name in _INS:
        a = _np.ascontiguousarray(inputs[name])
        arrays[f"in_{name}_dram"] = a
        args.append(nc.dram_tensor(f"in_{name}_dram", a.shape, _mybir.dt.from_np(a.dtype), kind="ExternalInput").ap())
    for i, (shape, dtype) in enumerate(_OUTS):
        dt = _mybir.dt.from_np(_np.dtype(dtype))
        args.append(nc.dram_tensor(f"out_{i}_dram", shape, dt, kind="ExternalOutput").ap())
    bass_hybrid_gla_rwkv7_moe_block(nc, *args)
    r = _run(nc, [arrays], core_ids=[0])
    got = tuple(r.results[0][f"out_{i}_dram"] for i in range(len(_OUTS)))
    return got[0]
```
